# Optimizing a Trainium2 kernel written in Bass

```python
import math
import jax, jax.numpy as jnp
from jax import lax
import numpy as np

D_MODEL = 1024
BATCH = 1
SEQ = 256
DEPTH = 2

GRID_W = 64
CTX_LEN = 256
HEAD_DIM = 64
MIX_WIDTH = D_MODEL
FOURIER_GROUPS = 4
FOURIER_WIDTH = MIX_WIDTH // 4
FOURIER_GROUP_DIM = FOURIER_WIDTH // FOURIER_GROUPS
GQA_HEADS = (MIX_WIDTH // 2) // HEAD_DIM
GQA_KV_HEADS = GQA_HEADS // 4
NA_HEADS = (MIX_WIDTH // 4) // HEAD_DIM
NA_WIN_H = 8
NA_WIN_W = 16
Q_BLOCK = 128
ROPE_THETA = 10000.0
ROPE_PAIRS_PER_AXIS = HEAD_DIM // 4
D_FF = 256 * math.ceil(8 * D_MODEL / 3 / 256)
N_BRANCHES = 3
N_MOD = 9
EPS = 1e-6
GQA_Q_WIDTH = GQA_HEADS * HEAD_DIM
GQA_KV_WIDTH = GQA_KV_HEADS * HEAD_DIM
NA_WIDTH = NA_HEADS * HEAD_DIM
PROJ_SPLITS = tuple(int(v) for v in np.cumsum([FOURIER_WIDTH, GQA_Q_WIDTH, GQA_KV_WIDTH, GQA_KV_WIDTH, NA_WIDTH, NA_WIDTH, NA_WIDTH]))
IN_PROJ_WIDTH = PROJ_SPLITS[-1] + N_BRANCHES * D_MODEL

kernel_name = "hybrid_gated_mixer_dit_block"

def rms_norm(x, gain):
    xf = x.astype(jnp.float32)
    y = xf * lax.rsqrt(jnp.mean(xf * xf, axis=-1, keepdims=True) + EPS)
    return (y * gain.astype(jnp.float32)).astype(x.dtype)

def modulate(u, shift, scale):
    return u * (1 + scale) + shift

def swiglu(u, w_in, w_out):
    a, g = jnp.split(u @ w_in, 2, axis=-1)
    return (jax.nn.silu(g) * a) @ w_out

def heads(t, n):
    return t.reshape(t.shape[0], t.shape[1], n, HEAD_DIM)

def axial_rope_tables(seq_len):
    t = jnp.arange(seq_len)
    row = (t // GRID_W).astype(jnp.float32)
    col = (t % GRID_W).astype(jnp.float32)
    freqs = ROPE_THETA ** (-jnp.arange(ROPE_PAIRS_PER_AXIS, dtype=jnp.float32) / ROPE_PAIRS_PER_AXIS)
    ang = jnp.concatenate([row[:, None] * freqs, col[:, None] * freqs], axis=-1)
    return jnp.cos(ang), jnp.sin(ang)

def apply_rope(x, cos, sin):
    xf = x.astype(jnp.float32).reshape(*x.shape[:-1], HEAD_DIM // 2, 2)
    x0, x1 = xf[..., 0], xf[..., 1]
    c, s = cos[None, :, None, :], sin[None, :, None, :]
    out = jnp.stack([x0 * c - x1 * s, x0 * s + x1 * c], axis=-1)
    return out.reshape(x.shape).astype(x.dtype)

def fourier_mix(u):
    b, t, _ = u.shape
    ug = u.astype(jnp.float32).reshape(b, t, FOURIER_GROUPS, FOURIER_GROUP_DIM)
    y = jnp.fft.fft2(ug, axes=(1, 3), norm="ortho").real
    return y.reshape(b, t, FOURIER_WIDTH).astype(u.dtype)

def gqa_attend(q, k, v):
    b, t, h, hd = q.shape
    kvh = k.shape[2]
    qg = q.reshape(b, t, kvh, h // kvh, hd)
    s = jnp.einsum("btkgd,blkd->bkgtl", qg, k).astype(jnp.float32) * (hd ** -0.5)
    p = jax.nn.softmax(s, axis=-1).astype(v.dtype)
    o = jnp.einsum("bkgtl,blkd->btkgd", p, v)
    return o.reshape(b, t, h * hd)

def gqa_latent(q, k_all, v_all):
    b, s, h, hd = q.shape
    qb = jnp.moveaxis(q.reshape(b, s // Q_BLOCK, Q_BLOCK, h, hd), 1, 0)
    out = lax.map(lambda blk: gqa_attend(blk, k_all, v_all), qb)
    return jnp.moveaxis(out, 0, 1).reshape(b, s, h * hd)

def neighbourhood_attention(q, k, v, k_ctx, v_ctx, rpb):
    b, s, nh, hd = q.shape
    rows = s // GRID_W
    kh = min(NA_WIN_H, rows)
    qg = jnp.moveaxis(q.reshape(b, rows, GRID_W, nh, hd), 1, 0)
    kg = k.reshape(b, rows, GRID_W, nh, hd)
    vg = v.reshape(b, rows, GRID_W, nh, hd)
    col = jnp.arange(GRID_W)
    cs = jnp.clip(col - NA_WIN_W // 2, 0, GRID_W - NA_WIN_W)
    band = (col[None, :] >= cs[:, None]) & (col[None, :] < cs[:, None] + NA_WIN_W)
    dc = jnp.clip(col[None, :] - col[:, None], -(NA_WIN_W - 1), NA_WIN_W - 1) + NA_WIN_W - 1
    scale = hd ** -0.5

    def row_block(args):
        q_row, r = args
        rs = jnp.clip(r - kh // 2, 0, rows - kh)
        k_blk = lax.dynamic_slice_in_dim(kg, rs, kh, axis=1)
        v_blk = lax.dynamic_slice_in_dim(vg, rs, kh, axis=1)
        dr = rs + jnp.arange(kh) - r + NA_WIN_H - 1
        bias = rpb[:, dr[:, None, None], dc[None, :, :]]
        bias = jnp.transpose(bias, (0, 2, 1, 3)).astype(jnp.float32)
        s_loc = jnp.einsum("bqhd,bikhd->bhqik", q_row, k_blk).astype(jnp.float32) * scale + bias[None]
        s_loc = jnp.where(band[:, None, :], s_loc, -jnp.inf).reshape(b, nh, GRID_W, kh * GRID_W)
        s_ctx = jnp.einsum("bqhd,bjhd->bhqj", q_row, k_ctx).astype(jnp.float32) * scale
        p = jax.nn.softmax(jnp.concatenate([s_loc, s_ctx], axis=-1), axis=-1).astype(v.dtype)
        p_loc = p[..., : kh * GRID_W].reshape(b, nh, GRID_W, kh, GRID_W)
        p_ctx = p[..., kh * GRID_W:]
        return (jnp.einsum("bhqik,bikhd->bqhd", p_loc, v_blk)
                + jnp.einsum("bhqj,bjhd->bqhd", p_ctx, v_ctx))

    out = lax.map(row_block, (qg, jnp.arange(rows)))
    return jnp.moveaxis(out, 0, 1).reshape(b, s, nh * hd)

def gated_merge(gate_logits, y_f, y_g, y_n):
    g_f, g_g, g_n = jnp.split(jax.nn.sigmoid(gate_logits), N_BRANCHES, axis=-1)
    return g_f * y_f + g_g * y_g + g_n * y_n

def token_mixer(ux, uh, w_in, q_norm, k_norm, na_rpb, w_fourier, w_gqa_out, w_na_out, w_o, cos, sin, ctx_out):
    fx, gqx, gkx, gvx, nqx, nkx, nvx, gatex = jnp.split(ux @ w_in, PROJ_SPLITS, axis=-1)
    fh, gqh, gkh, gvh, nqh, nkh, nvh, gateh = jnp.split(uh @ w_in, PROJ_SPLITS, axis=-1)
    gk_h = rms_norm(heads(gkh, GQA_KV_HEADS), k_norm)
    gv_h = heads(gvh, GQA_KV_HEADS)
    nk_h = heads(nkh, NA_HEADS)
    nv_h = heads(nvh, NA_HEADS)
    y_f = fourier_mix(fx) @ w_fourier
    q = apply_rope(rms_norm(heads(gqx, GQA_HEADS), q_norm), cos, sin)
    k = apply_rope(rms_norm(heads(gkx, GQA_KV_HEADS), k_norm), cos, sin)
    v = heads(gvx, GQA_KV_HEADS)
    y_g = gqa_latent(q, jnp.concatenate([gk_h, k], axis=1), jnp.concatenate([gv_h, v], axis=1)) @ w_gqa_out
    y_n = neighbourhood_attention(heads(nqx, NA_HEADS), heads(nkx, NA_HEADS), heads(nvx, NA_HEADS), nk_h, nv_h, na_rpb) @ w_na_out
    yx = gated_merge(gatex, y_f, y_g, y_n) @ w_o
    if not ctx_out:
        return yx, None
    y_fh = fourier_mix(fh) @ w_fourier
    y_gh = gqa_attend(rms_norm(heads(gqh, GQA_HEADS), q_norm), gk_h, gv_h) @ w_gqa_out
    y_nh = gqa_attend(heads(nqh, NA_HEADS), nk_h, nv_h) @ w_na_out
    yh = gated_merge(gateh, y_fh, y_gh, y_nh) @ w_o
    return yx, yh

def setup_inputs(seed: int = 0) -> dict:
    key = jax.random.key(seed)
    ks = jax.random.split(key, 24)
    f32 = jnp.float32
    L, D = DEPTH, D_MODEL

    def w(k, shape, fan_in, gain=1.0):
        return (gain * fan_in ** -0.5) * jax.random.normal(k, shape, f32)

    def g(k, shape):
        return 1.0 + 0.02 * jax.random.normal(k, shape, f32)

    return {
        "x": jax.random.normal(ks[0], (BATCH, SEQ, D), f32),
        "c": jax.random.normal(ks[1], (BATCH, D), f32),
        "ctx": jax.random.normal(ks[2], (BATCH, CTX_LEN, D), f32),
        "c_ctx": jax.random.normal(ks[3], (D,), f32),
        "mod_w": w(ks[4], (L, D, N_MOD * D), D, 0.5),
        "mod_b": 0.01 * jax.random.normal(ks[5], (L, N_MOD * D), f32),
        "norm_ffn1": g(ks[6], (L, D)),
        "ffn1_w_in": w(ks[7], (L, D, 2 * D_FF), D),
        "ffn1_w_out": w(ks[8], (L, D_FF, D), D_FF),
        "norm_mix": g(ks[9], (L, D)),
        "w_in": w(ks[10], (L, D, IN_PROJ_WIDTH), D),
        "q_norm": g(ks[11], (L, HEAD_DIM)),
        "k_norm": g(ks[12], (L, HEAD_DIM)),
        "na_rpb": 0.1 * jax.random.normal(ks[13], (L, NA_HEADS, 2 * NA_WIN_H - 1, 2 * NA_WIN_W - 1), f32),
        "w_fourier": w(ks[14], (L, FOURIER_WIDTH, D), FOURIER_WIDTH),
        "w_gqa_out": w(ks[15], (L, GQA_Q_WIDTH, D), GQA_Q_WIDTH),
        "w_na_out": w(ks[16], (L, NA_WIDTH, D), NA_WIDTH),
        "w_o": w(ks[17], (L, D, D), D),
        "norm_ffn2": g(ks[18], (L, D)),
        "ffn2_w_in": w(ks[19], (L, D, 2 * D_FF), D),
        "ffn2_w_out": w(ks[20], (L, D_FF, D), D_FF),
        "final_norm": g(ks[21], (D,)),
    }

def reference(x, c, ctx, c_ctx, mod_w, mod_b, norm_ffn1, ffn1_w_in, ffn1_w_out, norm_mix, w_in, q_norm, k_norm, na_rpb, w_fourier, w_gqa_out, w_na_out, w_o, norm_ffn2, ffn2_w_in, ffn2_w_out, final_norm):
    cos, sin = axial_rope_tables(x.shape[1])
    h = ctx
    for l in range(DEPTH):
        last = l == DEPTH - 1
        mx = jnp.split((jax.nn.silu(c) @ mod_w[l] + mod_b[l])[:, None, :], N_MOD, axis=-1)
        mh = jnp.split((jax.nn.silu(c_ctx) @ mod_w[l] + mod_b[l])[None, None, :], N_MOD, axis=-1)
        x = x + 0.5 * mx[2] * swiglu(modulate(rms_norm(x, norm_ffn1[l]), mx[0], mx[1]), ffn1_w_in[l], ffn1_w_out[l])
        h = h + 0.5 * mh[2] * swiglu(modulate(rms_norm(h, norm_ffn1[l]), mh[0], mh[1]), ffn1_w_in[l], ffn1_w_out[l])
        ux = modulate(rms_norm(x, norm_mix[l]), mx[3], mx[4])
        uh = modulate(rms_norm(h, norm_mix[l]), mh[3], mh[4])
        yx, yh = token_mixer(ux, uh, w_in[l], q_norm[l], k_norm[l], na_rpb[l], w_fourier[l], w_gqa_out[l], w_na_out[l], w_o[l], cos, sin, not last)
        x = x + mx[5] * yx
        x = x + 0.5 * mx[8] * swiglu(modulate(rms_norm(x, norm_ffn2[l]), mx[6], mx[7]), ffn2_w_in[l], ffn2_w_out[l])
        if not last:
            h = h + mh[5] * yh
            h = h + 0.5 * mh[8] * swiglu(modulate(rms_norm(h, norm_ffn2[l]), mh[6], mh[7]), ffn2_w_in[l], ffn2_w_out[l])
    return rms_norm(x, final_norm)


_drawn_inputs = setup_inputs


def setup_inputs(seed=0):
    import zlib

    import numpy as np

    out = dict(_drawn_inputs(seed))
    spreads = {}
    factors = {'mod_b': 5.071,
     'norm_ffn1': 8.0,
     'norm_mix': 8.0,
     'q_norm': 8.0,
     'k_norm': 8.0,
     'na_rpb': 8.0,
     'norm_ffn2': 8.0,
     'final_norm': 2.756}
    for name, (base, spread) in spreads.items():
        noise = np.random.default_rng([zlib.crc32(name.encode()), seed]).standard_normal(out[name].shape)
        drawn = base * np.exp(spread * noise) if base else spread * noise
        out[name] = __import__('jax').numpy.asarray(drawn.astype(out[name].dtype))
    for name, factor in factors.items():
        out[name] = (out[name] * factor).astype(out[name].dtype)
    return out
```

```python
from contextlib import ExitStack

import numpy as np
import concourse.bass as bass
from concourse import mybir

F32 = mybir.dt.float32
F32R = mybir.dt.float32r
ALU = mybir.AluOpType
ACT = mybir.ActivationFunctionType
AX_X = mybir.AxisListType.X

P = 128
D = 1024
DC = D // P
SEQ = 256
CTX = 256
TOK = SEQ + CTX
TT = SEQ // P
DEPTH = 2
GRID_W = 64
ROWS = SEQ // GRID_W
HD = 64
KV_HEADS = 2
GQA_CHUNKS = 4
NA_HEADS = 4
WIN_H, WIN_W = 8, 16
D_FF = 2816
FH = D_FF // P // 2
FW = 256
FG = 64
N_MOD = 9
MODC = N_MOD * DC
EPS = 1e-6
COL_F, COL_Q, COL_K, COL_V = 0, 256, 768, 896
COL_NQ, COL_NK, COL_NV, COL_GATE = 1024, 1280, 1536, 1792
MG = 512
MK = 4
MGC = MG // P
N_START = 4
RING = 4
V_MODB, V_N1, V_NM, V_N2, V_FIN, V_C, V_CC, V_QN, V_KN, V_ROWS = 0, 72, 80, 88, 96, 104, 112, 120, 121, 122


class Phase:

    def __init__(self, plan, steps, kd, w=None):
        self.nu, self.steps, self.kd = len(kd), steps, kd
        self.w = w or [1] * len(kd)
        self.g0 = plan["g"]
        self.base = list(plan["loaded"])
        for q in range(steps * self.nu):
            plan["loaded"][(self.g0 + q) % RING] += 16 * self.w[q % self.nu]
        plan["g"] += steps * self.nu

    def at(self, j, c, i=0, per=0):
        q = self.nu * c + j
        slot = (self.g0 + q) % RING
        if self.steps == 1:
            same = [self.w[jj] for jj in range(j + 1) if (j - jj) % RING == 0]
            return slot, self.g0 + q, self.base[slot] + 16 * sum(same)
        turns = self.nu * per // RING
        return slot, self.g0 + q + self.nu * per * i, self.base[slot] + 16 * self.w[j] * (q // RING + 1 + turns * i)


def build(nc, t, out):
    ctx = ExitStack()
    sem = {}

    def S(name):
        if name not in sem:
            sem[name] = ctx.enter_context(nc.semaphore(name))
        return sem[name]

    def place(st, name, shape, dt=F32):
        return st.enter_context(nc.sbuf_tensor(name, shape, dt))

    def sb(name, shape, dt=F32):
        return place(ctx, name, shape, dt)

    plan = {"g": 0, "loaded": [0] * RING}
    FFN_IN, FFN_OUT = [8, 8], [6, 5]
    phases = {}
    for l in range(DEPTH):
        for f in (1, 2):
            if f == 2:
                phases[l, "head"] = Phase(plan, 1, [8] * 14, [1, 2, 2, 2, 2] + [1] * 9)
                phases[l, "gate"] = Phase(plan, DC, [8, 8, 8, 8], [1, 1, 1, 4])
                phases[l, "wo"] = Phase(plan, DC // 2, [8, 8])
            for half in (0, 1):
                phases[l, f, "in", half] = Phase(plan, FH, FFN_IN)
                phases[l, f, "out", half] = Phase(plan, DC, FFN_OUT)
    UNITS = plan["g"]
    order = list(phases)
    HEAD = ([("k", COL_K)] + [("q", c) for c in range(GQA_CHUNKS)] + [("v", COL_V)]
            + [("nk", COL_NK + P * c) for c in range(2)] + [("nq", COL_NQ + P * c) for c in range(2)]
            + [("nv", COL_NV + P * c) for c in range(2)] + [("f", COL_F + P * c) for c in range(2)])

    def head_tokens(l, kind):
        return SEQ if l == DEPTH - 1 and kind in ("q", "nq", "f") else TOK

    def late_tokens(l):
        return SEQ if l == DEPTH - 1 else TOK

    def norm_tokens(k):
        return TOK if k < 5 else SEQ

    BG = {(0, 1): (0, N_START, 14), (0, 2): (1, 0, 18)}
    BG_BASE = {(0, 1): 0, (0, 2): 14}

    def jobs(l):
        streams = (0,) if l == DEPTH - 1 else (0, 1)
        return ([("g", c, up, s) for c in range(GQA_CHUNKS) for s in streams for up in (0, 1)]
                + [("n", c, up, s) for c in range(2) for s in streams for up in (0, 1)])

    job0, z0 = [0], [0]
    for l in range(DEPTH):
        job0.append(job0[-1] + len(jobs(l)))
        z0.append(z0[-1] + (TT if l == DEPTH - 1 else 2 * TT))

    x = sb("x", [P, DC, TOK])
    u_hi = sb("u_hi", [P, DC, TOK], F32R)
    u_lo = sb("u_lo", [P, DC, TOK], F32R)
    w_raw = sb("w_raw", [P, RING, 8, P])
    w_hi = sb("w_hi", [P, RING, 8, P], F32R)
    w_lo = sb("w_lo", [P, RING, 8, P], F32R)
    ident = sb("ident", [P, P])
    ones_mean = sb("ones_mean", [P, P])
    ones_f = sb("ones_f", [P, P])
    ones_r = sb("ones_r", [P, P], F32R)
    head_mean = sb("head_mean", [P, P])
    rope_swap = sb("rope_swap", [P, P])
    flip = sb("flip", [P, P])
    band = sb("band", [P, GRID_W])
    vec_rows = sb("vec_rows", [V_ROWS, DEPTH, P])
    vec = sb("vec", [P, DEPTH, V_ROWS])
    sil = sb("sil", [P, 2, DC])
    modcol = sb("modcol", [P, DEPTH, 2, MODC])
    colA = sb("colA", [P, 6, 2, DC])
    colB = sb("colB", [P, 6, 2, DC])
    colG = sb("colG", [P, 6, 2, DC])
    eps_col = sb("eps_col", [P, 1])
    gq = sb("gq", [P, DEPTH])
    sq = sb("sq", [P, 2, TOK])
    ssq = sb("ssq", [P, TOK])
    root = sb("root", [P, TOK])
    rstd = sb("rstd", [P, TOK])
    tmp = sb("tmp", [P, 4, TOK])
    smax = sb("smax", [P, 2, 2])
    rsum = sb("rsum", [P, 2, 2])
    rrec = sb("rrec", [P, 2, 2])
    with ExitStack() as st:
        h_hi = place(st, "h_hi", [P, FH, TOK], F32R)
        h_lo = place(st, "h_lo", [P, FH, TOK], F32R)
        sg = place(st, "sg", [P, 2, TOK])
        hf = place(st, "hf", [P, 2, TOK])
        mod_w = place(st, "mod_w", [P, 2, MK, MG])
        acc = place(st, "acc", [P, 2, MG])
        acc_hi = place(st, "acc_hi", [P, 2, MG], F32R)
        acc_lo = place(st, "acc_lo", [P, 2, MG], F32R)
        mtmp = place(st, "mtmp", [P, MGC, P])
    with ExitStack() as st:
        tok_rows = place(st, "tok_rows", [P, 2 * TT, D])
        mod_first = place(st, "mod_first", [P, N_START, DC, MG])
    with ExitStack() as st:
        mod_rows = place(st, "mod_rows", [2, N_START, MG])
        y_rows = place(st, "y_rows", [P, TT, D])
    with ExitStack() as st:
        cat_hi = place(st, "cat_hi", [P, DC, TOK], F32R)
        cat_lo = place(st, "cat_lo", [P, DC, TOK], F32R)
        with ExitStack() as st2:
            qk = place(st2, "qk", [P, 1 + GQA_CHUNKS, TOK])
            nqk = place(st2, "nqk", [P, 4, TOK])
            Vn = place(st2, "Vn", [P, 4, 3 * P])
            bias = place(st2, "bias", [P, TT, NA_HEADS, SEQ])
            with ExitStack() as st3:
                probs = place(st3, "probs", [P, 2, 2, TOK])
                pT = place(st3, "pT", [P, 2, 4, SEQ])
            with ExitStack() as st3:
                fT = place(st3, "fT", [P, 2, TOK])
                Zs = place(st3, "Zs", [P, 2, 4, 2 * P])
                dft_chan = place(st3, "dft_chan", [P, 2 * P])
                dft_tok = place(st3, "dft_tok", [P, 2, TT, SEQ])
        with ExitStack() as st2:
            mg_hi = place(st2, "mg_hi", [P, DC, TOK], F32R)
            mg_lo = place(st2, "mg_lo", [P, DC, TOK], F32R)
            sig = place(st2, "sig", [P, 3, TOK])
    rope_cs = tmp[:, 3, :].rearrange("p (a t) -> p a t", a=2)
    vT = tmp[:, 0:3, :]

    bank = ctx.enter_context(nc.psum_tensor("bank", [P, 8, 512], F32))

    w_loaded = [S(f"w_loaded{i}") for i in range(RING)]
    mod_loaded = [S(f"mod_loaded{i}") for i in range(2)]
    first_loaded = [S(f"first_loaded{i}") for i in range(N_START)]
    rows_loaded = [S(f"rows_loaded{i}") for i in range(2)]
    vec_loaded = S("vec_loaded")
    ident_loaded = S("ident_loaded")
    const_loaded = S("const_loaded")

    def wait(eng, s, value):
        if not (isinstance(value, int) and value <= 0):
            eng.wait_ge(s, value)

    def turns(eng, n, body, peel=False, stop=None):
        lo = 0
        if peel:
            body(0)
            lo = 1
        if n - lo > 1:
            with eng.Fori(lo, n) as i:
                body(i)
        elif n - lo == 1:
            body(lo)

    def finished(ph, j, c, i=0, per=0):
        return ph.at(j, c, i, per)[1] + 1

    def ffn_step(l, f, half):
        return ((2 * l + f - 1) * 2 + half) * FH

    def out_step(l, f, half=0):
        return DC + l * 5 * DC + {1: half * DC, 0: 2 * DC, 2: (3 + half) * DC}[f]

    def norm_of(l, f):
        return 3 * l + {1: 0, 0: 1, 2: 2}[f]

    def bodies_of_mods(l, f, part, half):
        if (l, f) not in BG:
            return None
        count = BG[l, f][2]
        at = 0
        for h2 in (0, 1):
            for p2, loop, tail in (("in", 5, 0), ("out", 3, 1)):
                if (p2, h2) == (part, half):
                    return (BG_BASE[l, f] + at, loop, tail) if at < count else None
                at += loop + tail

    def mods_done(l, f):
        return sum(BG[k][2] for k in BG if k <= (l, f))

    block = ctx.enter_context(nc.Block())

    @block.sync
    def _(sp):
        sp.dma_start(ident[:], t["c_ident"]).then_inc(ident_loaded, 16)
        sp.dma_start(vec_rows[:], t["vec_rows"]).then_inc(vec_loaded, 16)
        for s in range(2):
            rows = (t["x"], t["ctx"])[s]
            sp.dma_start(tok_rows[:, TT * s:TT * s + TT, :], rows.rearrange("(a p) d -> p a d", p=P)).then_inc(rows_loaded[s], 16)
        for g in range(N_START):
            sp.dma_start(mod_first[:, g], t["mod_w"][0].rearrange("(k p) c -> p k c", p=P)[:, :, MG * g:MG * g + MG]).then_inc(first_loaded[g], 16)

        def load(ph, srcs, j, c, i=0, per=0):
            slot, g, _ = ph.at(j, c, i, per)
            wait(sp, S("w_lo_ready"), g - RING + 1)
            for p0, p1, k0, k1, src in srcs:
                sp.dma_start(w_raw[p0:p1, slot, k0:k1, :], src).then_inc(w_loaded[slot], 16)

        for key in order:
            ph = phases[key]
            l = key[0]
            if len(key) == 4:
                _, f, part, half = key
                w = t[f"ffn{f}_w_in"][l] if part == "in" else t[f"ffn{f}_w_out"][l]
                w = w.rearrange("(k p) c -> p k c", p=P)
                if part == "in":
                    def body(i, steps=2):
                        for c in range(steps):
                            for j in range(2):
                                col = j * D_FF + (half * FH + c) * P + i * (2 * P)
                                load(ph, [(0, P, 0, DC, w[:, :, bass.ds(col, P)])], j, c, i, 2)
                    turns(sp, FH // 2, body, peel=ph.g0 == 0)
                    body(FH // 2, 1)
                else:
                    def body(i):
                        for c in range(2):
                            for j in range(2):
                                k0, n = half * FH + j * FFN_OUT[0], FFN_OUT[j]
                                load(ph, [(0, P, 0, n, w[:, k0:k0 + n, bass.ds(c * P + i * (2 * P), P)])], j, c, i, 2)
                    turns(sp, DC // 2, body)
            elif key[1] == "head":
                w = t["w_in"][l].rearrange("(k p) c -> p k c", p=P)
                for idx, (kind, col) in enumerate(HEAD):
                    if kind == "q":
                        srcs = [(0, P, 0, DC, w[:, :, COL_Q + HD * h:COL_Q + HD * h + HD]) for h in (col, col + GQA_CHUNKS)]
                        slot, g, _ = ph.at(idx, 0)
                        wait(sp, S("w_lo_ready"), g - RING + 1)
                        for up in (0, 1):
                            sp.dma_start(w_raw[:, slot, :, HD * up:HD * up + HD], srcs[up][4]).then_inc(w_loaded[slot], 16)
                    else:
                        load(ph, [(0, P, 0, DC, w[:, :, col:col + P])], idx, 0)
            elif key[1] == "gate":
                w = t["w_in"][l].rearrange("(k p) c -> p k c", p=P)
                wf = t["w_fourier"][l].rearrange("(k p) c -> p k c", p=P)
                wg = t["w_gqa_out"][l].rearrange("(u c p) n -> u p c n", u=2, p=HD)
                wn = t["w_na_out"][l].rearrange("(k p) c -> p k c", p=P)

                def body(i):
                    for j in range(3):
                        load(ph, [(0, P, 0, DC, w[:, :, bass.ds(COL_GATE + j * D + i * P, P)])], j, 0, i, 1)
                    cols = bass.ds(i * P, P)
                    load(ph, [(HD, P, 2, 6, wg[1][:, :, cols]), (0, HD, 2, 6, wg[0][:, :, cols]),
                              (0, P, 0, 2, wf[:, :, cols]), (0, P, 6, 8, wn[:, :, cols])], 3, 0, i, 1)
                turns(sp, DC, body)
            else:
                w = t["w_o"][l].rearrange("(k p) c -> p k c", p=P)

                def body(i):
                    for c in range(2):
                        for j in range(2):
                            load(ph, [(0, P, 0, DC, w[:, :, bass.ds((2 * c + j) * P + i * (4 * P), P)])], j, c, i, 2)
                turns(sp, 2, body)
        for a in range(TT):
            sp.wait_ge(S("y_rows_ready"), 4 * TT)
            sp.dma_start(out[a * P:a * P + P, :], y_rows[:, a, :]).then_inc(S("stored"), 16)
        sp.wait_ge(S("stored"), 16 * TT)

    @block.gpsimd
    def _(pool):
        for dst, name in ((head_mean, "c_head_mean"), (rope_swap, "c_rope_swap"), (flip, "c_flip"), (band, "c_band")):
            pool.dma_start(dst[:], t[name]).then_inc(const_loaded, 16)
        pool.memset(ones_mean[:], 1.0 / D).then_inc(S("ones_set"), 1)
        pool.memset(ones_f[:], 1.0).then_inc(S("ones_set"), 1)
        pool.memset(eps_col[:], EPS).then_inc(S("ones_set"), 1)

        def lo(ph, j, c, i=0, per=0):
            slot, g, _ = ph.at(j, c, i, per)
            n = ph.kd[j]
            pool.wait_ge(S("w_hi_ready"), g + 1)
            pool.tensor_tensor(w_lo[:, slot, 0:n, :], w_raw[:, slot, 0:n, :], w_hi[:, slot, 0:n, :].bitcast(F32),
                               ALU.subtract).then_inc(S("w_lo_ready"), 1)

        for key in order:
            ph = phases[key]
            l = key[0]
            if len(key) == 4:
                def body(i, steps=2):
                    for c in range(steps):
                        for j in range(2):
                            lo(ph, j, c, i, 2)
                if key[2] == "in":
                    turns(pool, FH // 2, body)
                    body(FH // 2, 1)
                else:
                    turns(pool, DC // 2, body)
            elif key[1] == "head":
                for idx in range(len(HEAD)):
                    lo(ph, idx, 0)
            elif key[1] == "gate":
                turns(pool, DC, lambda i: [lo(ph, j, 0, i, 1) for j in range(4)])
            else:
                turns(pool, 2, lambda i: [lo(ph, j, c, i, 2) for c in range(2) for j in range(2)])

    @block.scalar
    def _(act):
        def hi(ph, j, c, i=0, per=0):
            slot, g, loaded = ph.at(j, c, i, per)
            n = ph.kd[j]
            act.wait_ge(w_loaded[slot], loaded)
            wait(act, S("w_used"), g - RING + 1)
            act.activation(w_hi[:, slot, 0:n, :], w_raw[:, slot, 0:n, :], ACT.Copy).then_inc(S("w_hi_ready"), 1)

        def first_hi(key):
            ph = phases[key]
            for q in range(2):
                hi(ph, q % ph.nu, q // ph.nu)

        def following(key):
            at = order.index(key) + 1
            return order[at] if at < len(order) else None

        def square_at(M, Q, par, m, n):
            act.wait_ge(S("x_done"), M + 1)
            wait(act, S("ssq_added"), Q - 1)
            act.activation(sq[:, par, 0:n], x[:, bass.ds(m, 1), 0:n].rearrange("p a n -> p (a n)"), ACT.Square).then_inc(S("sq_ready"), 1)

        def norm(k):
            n = norm_tokens(k)
            act.wait_ge(S("ms_ready"), k + 1)
            act.activation(root[:, 0:n], bank[:, 6, 0:n], ACT.Sqrt, bias=eps_col[:, 0:1]).then_inc(S("root_ready"), 1)
            if k == 6:
                return
            for d in range(DC):
                q = DC * k + d
                act.wait_ge(S("t_ready"), q + 1)
                wait(act, S("u_ready"), q - 1)
                for v in range(n // SEQ):
                    cols = slice(SEQ * v, SEQ * v + SEQ)
                    last = act.activation(tmp[:, 2 + d % 2, cols], tmp[:, d % 2, cols], ACT.Identity,
                                          bias=colB[:, k, v, d:d + 1], scale=colA[:, k, v, d:d + 1])
                last.then_inc(S("uf_ready"), 1)

        def load_mod(G, l, group):
            wait(act, S("mod_mac"), 2 * DC * G)
            w = t["mod_w"][l].rearrange("(k p) c -> p k c", p=P)
            for kh in range(2):
                act.dma_start(mod_w[:, kh], w[:, MK * kh:MK * kh + MK, bass.ds(group * MG, MG)]).then_inc(mod_loaded[kh], 16)

        def mod_plan(l, f, G):
            layer, first, _ = BG[l, f]
            return layer, first + G - BG_BASE[l, f]

        def ffn(l, f):
            k = norm_of(l, f)
            n = norm_tokens(k)
            nxt = norm_of(l, f) + 1
            if (l, f) in BG:
                G = BG_BASE[l, f]
                act.wait_ge(S("u_ready"), DC * k + 1)
                load_mod(G, *mod_plan(l, f, G))
            for half in (0, 1):
                key = (l, f, "in", half)
                ph = phases[key]
                mods = bodies_of_mods(l, f, "in", half)
                s0 = ffn_step(l, f, half)

                def silu(s, c, i=0):
                    act.wait_ge(S("w_used"), finished(phases[l, f, "in", half], 1, c, i, 2))
                    b = (s0 + c) % 2
                    wait(act, S("h_prod"), s0 + s - 1)
                    act.activation(sg[:, b, 0:n], bank[:, 2 * b + 1, 0:n], ACT.Silu).then_inc(S("silu_ready"), 1)

                def body(i, more=True):
                    for c in range(2):
                        for j in range(2):
                            hi(ph, j, c + 1, i, 2)
                        if c == 1 and mods and more:
                            G = mods[0] + i + 1
                            load_mod(G, *mod_plan(l, f, G))
                        silu(c + i * 2, c, i)
                last_group = mods and mods[0] + mods[1] == BG_BASE[l, f] + BG[l, f][2]
                if last_group:
                    turns(act, FH // 2 - 1, body, peel=s0 == 0)
                    body(FH // 2 - 1, more=False)
                else:
                    turns(act, FH // 2, body, peel=s0 == 0)
                first_hi(following(key))
                silu(FH - 1, FH - 1)
                key = (l, f, "out", half)
                ph = phases[key]
                mods = bodies_of_mods(l, f, "out", half)
                m0 = out_step(l, f, half)

                def body(i, tail=False):
                    for c in range(2):
                        if not (tail and c == 1):
                            for j in range(2):
                                hi(ph, j, c + 1, i, 2)
                        elif following(key):
                            first_hi(following(key))
                        if c == 1 and mods:
                            G = mods[0] + i + 1
                            if not tail or G < BG_BASE[l, f] + BG[l, f][2]:
                                load_mod(G, *mod_plan(l, f, G))
                        if half == 1:
                            square_at(m0 + c + i * 2, DC * nxt + c + i * 2, c, c + i * 2, norm_tokens(nxt))
                turns(act, DC // 2 - 1, body)
                body(DC // 2 - 1, tail=True)

        act.wait_ge(S("vec_ready"), 1)
        act.activation(sil[:].rearrange("p v k -> p (v k)"), vec[:, 0, V_C:V_C + 2 * DC], ACT.Silu).then_inc(S("sil_ready"), 1)
        for d in range(DC):
            square_at(d, d, d % 2, d, TOK)
        for g in range(N_START):
            act.wait_ge(S("rows_mm"), g + 1)
            act.activation(mod_rows[:, g, :], bank[0:2, g, :], ACT.Copy).then_inc(S("mod_rows_ready"), 1)
        first_hi(order[0])
        norm(0)
        for l in range(DEPTH):
            ffn(l, 1)
            norm(norm_of(l, 0))
            nh = len(HEAD)
            key = (l, "head")
            ph = phases[key]
            act.wait_ge(S("u_ready"), DC * (norm_of(l, 0) + 1))
            act.dma_start(rope_cs, t["c_rope"]).then_inc(S("tables_loaded"), 16)
            act.dma_start(dft_chan[:], t["c_dft_chan"]).then_inc(S("tables_loaded"), 16)
            act.dma_start(dft_tok[:], t["c_dft_tok"]).then_inc(S("tables_loaded"), 16)
            width = 2 * WIN_W - 1
            for r in range(ROWS):
                for h in range(NA_HEADS):
                    first = ((l * NA_HEADS + h) * (2 * WIN_H - 1) + WIN_H - 1 - r) * width + WIN_W - GRID_W
                    src = bass.AP(tensor=t["na_rpb"].tensor, offset=first, ap=[[1, GRID_W], [width, ROWS], [1, GRID_W]])
                    p0 = (r % 2) * GRID_W
                    dst = bias[p0:p0 + GRID_W, r // 2, h, :].rearrange("p (i k) -> p i k", k=GRID_W)
                    act.dma_start(dst, src).then_inc(S("bias_loaded"), 16)
            for idx, (kind, arg) in enumerate(HEAD):
                if idx + 2 < nh:
                    hi(ph, idx + 2, 0)
                elif idx + 2 == nh:
                    first_hi((l, "gate"))
                n = head_tokens(l, kind)
                if idx < 5:
                    act.wait_ge(S("qk_raw"), 5 * l + idx + 1)
                    act.activation(sq[:, idx % 2, 0:n], qk[:, idx, 0:n], ACT.Square).then_inc(S("qk_sq"), 1)
                if 1 <= idx < 6:
                    c = idx - 1
                    nc_ = head_tokens(l, HEAD[c][0])
                    act.wait_ge(S("qk_ms"), 5 * l + c + 1)
                    wait(act, S("qk_normed"), 5 * l + c)
                    act.activation(root[:, 0:nc_], bank[:, 4, 0:nc_], ACT.Sqrt, bias=eps_col[:, 0:1]).then_inc(S("qk_root"), 1)
                if idx >= 5:
                    act.wait_ge(S("w_used"), finished(ph, idx, 0))
                    tile, first = {"v": (vT, 5), "nk": (nqk, 6), "nq": (nqk, 6), "nv": (vT, 9), "f": (fT, 12)}[kind]
                    dst = tile[:, idx - first, 0:n]
                    act.activation(dst, bank[:, idx % 4, 0:n], ACT.Copy,
                                   scale=HD ** -0.5 if kind == "nq" else 1.0).then_inc(S("head_copied"), 1)
            for c in range(3):
                act.wait_ge(S("vt_ready"), 3 * l + c + 1)
                act.activation(Vn[:, :, P * c:P * c + P], bank[:, 4 + c % 2, :].rearrange("p (k d) -> p k d", k=4), ACT.Copy)\
                   .then_inc(S("vn_ready"), 1)
            js = jobs(l)

            def copy_pt(q):
                J = job0[l] + q
                kind, c, up, s = js[q]
                act.wait_ge(S("pt_ready"), J + 1)
                src = bank[:, 5, :].rearrange("p (k t) -> p k t", k=2)
                dst = pT[:, J % 2, 2:4, :] if s == 0 else pT[:, J % 2, 1:2, :]
                act.activation(dst, src if s == 0 else src[:, 0:1, :], ACT.Copy).then_inc(S("pt_act"), 1)

            for q, (kind, c, up, s) in enumerate(js):
                J = job0[l] + q
                keys = TOK if s == 0 else CTX
                act.wait_ge(S("max_ready"), J + 1)
                wait(act, S("pt_ready"), J - 1)
                for b in range(TT):
                    last = act.activation(probs[:, J % 2, b, 0:keys], bank[:, 2 * (J % 2) + b, 0:keys], ACT.Exp,
                                          bias=smax[:, J % 2, b:b + 1], accum_out=rsum[:, J % 2, b:b + 1])
                last.then_inc(S("exp_done"), 1)
                if q:
                    copy_pt(q - 1)
            copy_pt(len(js) - 1)
            key = (l, "gate")
            ph = phases[key]
            n = late_tokens(l)

            def gate(i, j):
                act.wait_ge(S("w_used"), finished(ph, j, 0, i, 1))
                wait(act, S("prod_done"), DC * l + i)
                act.activation(sig[:, j, 0:n], bank[:, j, 0:n], ACT.Sigmoid).then_inc(S("sig_ready"), 1)

            def body(i, last=False):
                hi(ph, 2, 0, i, 1)
                gate(i, 0)
                hi(ph, 3, 0, i, 1)
                gate(i, 1)
                if not last:
                    hi(ph, 0, 1, i, 1)
                    gate(i, 2)
                    hi(ph, 1, 1, i, 1)
                else:
                    first_hi((l, "wo"))
                    gate(i, 2)
            turns(act, DC - 1, body, peel=True)
            body(DC - 1, last=True)
            key = (l, "wo")
            ph = phases[key]
            k = norm_of(l, 2)
            for m in range(DC):
                if m + 2 < DC:
                    hi(ph, m % 2, (m + 2) // 2)
                elif m + 2 == DC:
                    first_hi(following(key))
                square_at(out_step(l, 0) + m, DC * k + m, m % 2, m, norm_tokens(k))
            norm(k)
            ffn(l, 2)
            norm(norm_of(l, 2) + 1)
        for q in range(2 * TT):
            act.wait_ge(S("yt_ready"), q + 1)
            act.activation(y_rows[:, q // 2, 512 * (q % 2):512 * (q % 2) + 512], bank[:, q, :], ACT.Copy).then_inc(S("y_rows_ready"), 2)

    @block.vector
    def _(dve):
        chain = [0]

        def link(ins):
            chain[0] += 1
            ins.then_inc(S("dve_chain"), 1)
            dve.wait_ge(S("dve_chain"), chain[0])

        def columns_norm(k):
            l, w = k // 3, k % 3
            gain = vec[:, l, V_N1 + DC * w:V_N1 + DC * w + DC]
            for v in range(2):
                o = 3 * DC * w
                link(dve.tensor_tensor(colB[:, k, v, :], modcol[:, l, v, o:o + DC], vec[:, l, o:o + DC], ALU.add))
                link(dve.tensor_tensor(colA[:, k, v, :], modcol[:, l, v, o + DC:o + 2 * DC], vec[:, l, o + DC:o + 2 * DC], ALU.add))
                link(dve.scalar_tensor_tensor(out=colA[:, k, v, :], in0=colA[:, k, v, :], scalar=1.0, in1=gain,
                                              op0=ALU.add, op1=ALU.mult))

        def columns_gate(k):
            l, w = k // 3, k % 3
            for v in range(2):
                o = 3 * DC * w + 2 * DC
                link(dve.tensor_tensor(colG[:, k, v, :], modcol[:, l, v, o:o + DC], vec[:, l, o:o + DC], ALU.add))
                if w != 1:
                    link(dve.tensor_scalar(colG[:, k, v, :], colG[:, k, v, :], 0.5, None, ALU.mult))

        def add_squares(Q, par, n):
            dve.wait_ge(S("sq_ready"), Q + 1)
            wait(dve, S("ssq_added"), Q)
            dve.tensor_tensor(ssq[:, 0:n], ssq[:, 0:n], sq[:, par, 0:n], ALU.add).then_inc(S("ssq_added"), 1)

        def norm(k):
            n = norm_tokens(k)
            dve.wait_ge(S("root_ready"), k + 1)
            link(dve.reciprocal(rstd[:, 0:n], root[:, 0:n]))
            if k == 6:
                return

            def scale(d):
                dve.tensor_tensor(tmp[:, d % 2, 0:n], x[:, d, 0:n], rstd[:, 0:n], ALU.mult).then_inc(S("t_ready"), 1)

            scale(0)
            for d in range(DC):
                q = DC * k + d
                if d + 1 < DC:
                    scale(d + 1)
                dve.wait_ge(S("uf_ready"), q + 1)
                dve.tensor_copy(u_hi[:, d, 0:n], tmp[:, 2 + d % 2, 0:n]).then_inc(S("u_hi_done"), 1)
                dve.wait_ge(S("u_hi_done"), q + 1)
                dve.tensor_tensor(u_lo[:, d, 0:n], tmp[:, 2 + d % 2, 0:n], u_hi[:, d, 0:n].bitcast(F32), ALU.subtract)\
                   .then_inc(S("u_ready"), 1)

        def mod_products(G):
            for k in range(DC):
                if k % MK == 0:
                    dve.wait_ge(mod_loaded[k // MK], G * 16 + 16)
                w = mod_w[:, k // MK, k % MK, :]
                for v in range(2):
                    if k == 0:
                        ins = dve.tensor_scalar(acc[:, v, :], w, sil[:, v, k:k + 1], None, ALU.mult)
                    else:
                        dve.wait_ge(S("mod_mac"), G * (2 * DC) + 2 * k + v - 1)
                        ins = dve.scalar_tensor_tensor(out=acc[:, v, :], in0=w, scalar=sil[:, v, k:k + 1], in1=acc[:, v, :],
                                                       op0=ALU.mult, op1=ALU.add)
                    ins.then_inc(S("mod_mac"), 1)

        def mod_split(G):
            dve.wait_ge(S("mod_mac"), G * (2 * DC) + 2 * DC)
            dve.tensor_copy(acc_hi[:], acc[:]).then_inc(S("acc_hi_done"), 1)
            dve.wait_ge(S("acc_hi_done"), G + 1)
            dve.tensor_tensor(acc_lo[:], acc[:], acc_hi[:].bitcast(F32), ALU.subtract).then_inc(S("acc_ready"), 1)

        def mod_extract(G, layer, group):
            dve.wait_ge(S("red_ready"), G + 1)
            for v in range(2):
                if v:
                    dve.wait_ge(S("mod_kept"), G * 2 + 1)
                dve.tensor_tensor(mtmp[:], bank[:, 6 + v, :].rearrange("p (a b) -> p a b", a=MGC),
                                  ident[:].unsqueeze(1).to_broadcast([P, MGC, P]), ALU.mult).then_inc(S("mod_masked"), 1)
                dve.wait_ge(S("mod_masked"), G * 2 + v + 1)
                dve.tensor_reduce(modcol[:, layer, v, bass.ds(group * MGC, MGC)], mtmp[:], AX_X, ALU.add).then_inc(S("mod_kept"), 1)

        def mod_plan(l, f, G):
            layer, first, _ = BG[l, f]
            return layer, first + G - BG_BASE[l, f]

        def update(done, par, m, k, n):
            dve.wait_ge(S("w_used"), done)
            for v in range(n // SEQ):
                cols = slice(SEQ * v, SEQ * v + SEQ)
                xs = x[:, bass.ds(m, 1), cols].rearrange("p a n -> p (a n)")
                last = dve.scalar_tensor_tensor(out=xs, in0=bank[:, 4 + par, cols], scalar=colG[:, k, v, bass.ds(m, 1)],
                                                in1=xs, op0=ALU.mult, op1=ALU.add)
            last.then_inc(S("x_done"), 1)

        def ffn(l, f):
            k = norm_of(l, f)
            n = norm_tokens(k)
            nxt = k + 1
            for half in (0, 1):
                s0 = ffn_step(l, f, half)
                mods = bodies_of_mods(l, f, "in", half)

                def hidden(s, c):
                    b = (s0 + c) % 2
                    dve.wait_ge(S("silu_ready"), s0 + s + 1)
                    dve.tensor_tensor(hf[:, b, 0:n], bank[:, 2 * b, 0:n], sg[:, b, 0:n], ALU.mult).then_inc(S("h_prod"), 1)
                    dve.wait_ge(S("h_prod"), s0 + s + 1)
                    hs = h_hi[:, bass.ds(s, 1), 0:n].rearrange("p a n -> p (a n)")
                    dve.tensor_copy(hs, hf[:, b, 0:n]).then_inc(S("h_hi_done"), 1)
                    dve.wait_ge(S("h_hi_done"), s0 + s + 1)
                    dve.tensor_tensor(h_lo[:, bass.ds(s, 1), 0:n].rearrange("p a n -> p (a n)"), hf[:, b, 0:n],
                                      hs.bitcast(F32), ALU.subtract).then_inc(S("h_ready"), 1)

                def body(i):
                    G = mods[0] + i if mods else None
                    if mods:
                        mod_products(G)
                    hidden(0 + i * 2, 0)
                    if mods:
                        mod_split(G)
                    hidden(1 + i * 2, 1)
                    if mods:
                        mod_extract(G, *mod_plan(l, f, G))
                turns(dve, FH // 2, body, peel=s0 == 0)
                hidden(FH - 1, FH - 1)
                if half == 0:
                    dve.wait_ge(S("mod_kept"), 2 * (BG_BASE[l, f] + 5 if (l, f) in BG else mods_done(l, f)))
                    columns_gate(k)
                else:
                    if k < 5:
                        dve.wait_ge(S("mod_kept"), 2 * min(mods_done(l, f), BG_BASE.get((l, f), 99) + 14))
                        columns_norm(nxt)
                    link(dve.memset(ssq[:], 0.0))
                m0 = out_step(l, f, half)
                mods = bodies_of_mods(l, f, "out", half)

                def body(i):
                    G = mods[0] + i if mods else None
                    if mods:
                        mod_products(G)
                        mod_split(G)
                    for c in range(2):
                        update(finished(phases[l, f, "out", half], 1, c, i, 2), c, c + i * 2, k, n)
                        if half == 1:
                            add_squares(DC * nxt + c + i * 2, c, norm_tokens(nxt))
                    if mods:
                        mod_extract(G, *mod_plan(l, f, G))
                turns(dve, DC // 2 - 1, body)
                body(DC // 2 - 1)

        dve.wait_ge(S("ones_set"), 3)
        dve.tensor_copy(ones_r[:], ones_f[:]).then_inc(S("ones_r_set"), 1)
        link(dve.memset(ssq[:], 0.0))
        dve.wait_ge(S("vec_t"), 1)
        dve.tensor_copy(vec[:], bank[:, 6, 0:DEPTH * V_ROWS].rearrange("p (l r) -> p l r", l=DEPTH)).then_inc(S("vec_ready"), 1)
        dve.wait_ge(S("vec_ready"), 1)
        link(dve.tensor_scalar(gq[:], vec[:, :, V_QN], HD ** -0.5, None, ALU.mult))
        for d in range(DC):
            dve.wait_ge(S("x_turned"), d + 1)
            dve.tensor_copy(x[:, d, :], bank[:, 4 + d % 2, :]).then_inc(S("x_done"), 1)
            add_squares(d, d % 2, TOK)
        dve.wait_ge(S("modt_ready"), 1)
        for g in range(N_START):
            ins = dve.tensor_copy(modcol[:, 0, :, MGC * g:MGC * g + MGC],
                                  bank[:, 7, 2 * MGC * g:2 * MGC * (g + 1)].rearrange("p (a v) -> p v a", v=2))
        link(ins)
        columns_norm(0)
        norm(0)
        for l in range(DEPTH):
            ffn(l, 1)
            k = norm_of(l, 0)
            norm(k)
            nh = len(HEAD)
            for idx in range(7):
                if idx < 5:
                    n = head_tokens(l, HEAD[idx][0])
                    dve.wait_ge(S("w_used"), finished(phases[l, "head"], idx, 0))
                    dve.tensor_copy(qk[:, idx, 0:n], bank[:, idx % 4, 0:n]).then_inc(S("qk_raw"), 1)
                if 1 <= idx < 6:
                    c = idx - 1
                    n = head_tokens(l, HEAD[c][0])
                    gain = vec[:, l, V_KN:V_KN + 1] if c == 0 else gq[:, l:l + 1]
                    dve.wait_ge(S("qk_root"), 5 * l + c + 1)
                    link(dve.reciprocal(rstd[:, 0:n], root[:, 0:n]))
                    dve.scalar_tensor_tensor(out=qk[:, c, 0:n], in0=qk[:, c, 0:n], scalar=gain, in1=rstd[:, 0:n],
                                             op0=ALU.mult, op1=ALU.mult).then_inc(S("qk_normed"), 1)
                if idx >= 2:
                    c = idx - 2
                    dve.wait_ge(S("tables_loaded"), 48 * (l + 1))
                    dve.wait_ge(S("qk_swapped"), 5 * l + c + 1)
                    link(dve.tensor_tensor(ssq[:, 0:SEQ], bank[:, 5, 0:SEQ], rope_cs[:, 1, :], ALU.mult))
                    link(dve.tensor_tensor(ssq[:, SEQ:TOK], qk[:, c, 0:SEQ], rope_cs[:, 0, :], ALU.mult))
                    dve.tensor_tensor(qk[:, c, 0:SEQ], ssq[:, SEQ:TOK], ssq[:, 0:SEQ], ALU.add).then_inc(S("qk_ready"), 1)
            for j in range(4):
                dve.wait_ge(S("flipped"), 4 * l + j + 1)
                dve.tensor_tensor(bias[:, j // 2, 2 * (j % 2):2 * (j % 2) + 2, :].rearrange("p h (i k) -> p (h i) k", k=GRID_W),
                                  bank[:, 6 + j % 2, :].rearrange("p (i k) -> p i k", k=GRID_W),
                                  band[:].unsqueeze(1).to_broadcast([P, 2 * ROWS, GRID_W]), ALU.add).then_inc(S("bias_ready"), 1)
            tiles = TT if l == DEPTH - 1 else 2 * TT
            for c in range(2):
                for b in range(tiles // 2):
                    dve.wait_ge(S("z_ready"), z0[l] + c * (tiles // 2) + b + 1)
                    dve.tensor_copy(Zs[:, c, 2 * b:2 * b + 2, :], bank[:, 6 + b, :].rearrange("p (a z) -> p a z", a=2))\
                       .then_inc(S("z_copied"), 1)
            n = late_tokens(l)

            def to_cat(src, c, signal):
                link(dve.tensor_copy(cat_hi[:, c, 0:n], src))
                dve.tensor_tensor(cat_lo[:, c, 0:n], src, cat_hi[:, c, 0:n].bitcast(F32), ALU.subtract).then_inc(S("cat_ready"), 1)

            for c in range(2):
                dve.wait_ge(S("four_ready"), 2 * l + c + 1)
                to_cat(bank[:, 6 + c, 0:n], c, 1)
            js = jobs(l)
            per = 2 if l == DEPTH - 1 else 4

            def maximum(q):
                kind, c, up, s = js[q]
                J = job0[l] + q
                keys = TOK if s == 0 else CTX
                dve.wait_ge(S("s_ready"), J + 1)
                sc = bank[:, 2 * (J % 2):2 * (J % 2) + 2, 0:keys]
                if kind == "n" and s == 0:
                    link(dve.tensor_tensor(sc[:, :, 0:SEQ], sc[:, :, 0:SEQ], bias[:, :, 2 * c + up, :], ALU.add))
                link(dve.tensor_reduce(smax[:, J % 2, :], sc, AX_X, ALU.max))
                dve.tensor_scalar(smax[:, J % 2, :], smax[:, J % 2, :], -1.0, None, ALU.mult).then_inc(S("max_ready"), 1)

            def normalise(q):
                kind, c, up, s = js[q]
                J = job0[l] + q
                keys = TOK if s == 0 else CTX
                dve.wait_ge(S("exp_done"), J + 1)
                link(dve.reciprocal(rrec[:, J % 2, :], rsum[:, J % 2, :]))
                for b in range(TT):
                    last = dve.tensor_scalar(probs[:, J % 2, b, 0:keys], probs[:, J % 2, b, 0:keys], rrec[:, J % 2, b:b + 1],
                                             None, ALU.mult)
                last.then_inc(S("p_ready"), 1)

            def copy_pt(q):
                kind, c, up, s = js[q]
                J = job0[l] + q
                dve.wait_ge(S("pt_ready"), J + 1)
                src = bank[:, 4, :].rearrange("p (k t) -> p k t", k=2)
                dst = pT[:, J % 2, 0:2, :] if s == 0 else pT[:, J % 2, 0:1, :]
                dve.tensor_copy(dst, src if s == 0 else src[:, 0:1, :]).then_inc(S("pt_dve"), 1)

            def finish(q):
                if (q + 1) % per == 0:
                    chunk = q // per
                    dve.wait_ge(S("o_ready"), job0[l] + q + 1)
                    to_cat(bank[:, 6 + chunk % 2, 0:n], 2 + chunk, 1)

            N = len(js)
            for q in range(N + 4):
                if q < N:
                    maximum(q)
                if 1 <= q <= N:
                    normalise(q - 1)
                if 2 <= q <= N + 1:
                    copy_pt(q - 2)
                if q >= 4:
                    finish(q - 4)
            key = (l, "gate")
            MG0 = DC * l

            def body(i):
                dve.wait_ge(S("sig_ready"), 3 * MG0 + 3 + i * 3)
                dve.wait_ge(S("w_used"), finished(phases[key], 3, 0, i, 1))
                for j in range(3):
                    last = dve.tensor_tensor(tmp[:, j, 0:n], bank[:, 3 + j, 0:n], sig[:, j, 0:n], ALU.mult)
                last.then_inc(S("prod_done"), 1)
                dve.wait_ge(S("prod_done"), MG0 + 1 + i)
                dve.tensor_tensor(tmp[:, 3, 0:n], tmp[:, 0, 0:n], tmp[:, 1, 0:n], ALU.add).then_inc(S("sum_step"), 1)
                dve.wait_ge(S("sum_step"), 2 * MG0 + 1 + i * 2)
                dve.tensor_tensor(tmp[:, 3, 0:n], tmp[:, 3, 0:n], tmp[:, 2, 0:n], ALU.add).then_inc(S("sum_step"), 1)
                dve.wait_ge(S("sum_step"), 2 * MG0 + 2 + i * 2)
                ms = mg_hi[:, bass.ds(i, 1), 0:n].rearrange("p a n -> p (a n)")
                dve.tensor_copy(ms, tmp[:, 3, 0:n]).then_inc(S("mg_hi_done"), 1)
                dve.wait_ge(S("mg_hi_done"), MG0 + 1 + i)
                dve.tensor_tensor(mg_lo[:, bass.ds(i, 1), 0:n].rearrange("p a n -> p (a n)"), tmp[:, 3, 0:n],
                                  ms.bitcast(F32), ALU.subtract).then_inc(S("mg_ready"), 1)
            turns(dve, DC, body)
            if l == 0:
                dve.wait_ge(S("mod_kept"), 2 * mods_done(0, 1))
            columns_gate(k)
            columns_norm(k + 1)
            link(dve.memset(ssq[:], 0.0))
            for m in range(DC):
                update(finished(phases[l, "wo"], m % 2, m // 2), m % 2, m, k, late_tokens(l))
                add_squares(DC * (k + 1) + m, m % 2, norm_tokens(k + 1))
            norm(k + 1)
            ffn(l, 2)
            norm(k + 2)
        for d in range(DC):
            ins = dve.scalar_tensor_tensor(out=x[:, d, 0:SEQ], in0=x[:, d, 0:SEQ], scalar=vec[:, 0, V_FIN + d:V_FIN + d + 1],
                                           in1=rstd[:, 0:SEQ], op0=ALU.mult, op1=ALU.mult)
            ins.then_inc(S("y_ready_t"), 1)

    @block.tensor
    def _(pe):
        def products(ph, j, c, i, per, dst, hi_, lo_, k0, n, start, stop, k_wait=None):
            slot, g, _ = ph.at(j, c, i, per)
            pe.wait_ge(S("w_lo_ready"), g + 1)
            nk = ph.kd[j]
            for kk in range(nk):
                if k_wait:
                    k_wait(k0 + kk)
                last = three(dst, slot, kk, hi_, lo_, k0 + kk, n, start and kk == 0, stop and kk == nk - 1)
            last.then_inc(S("w_used"), 1)

        def three(dst, slot, kk, hi_, lo_, ka, n, start, stop):
            pe.matmul(dst, w_hi[:, slot, kk, :], hi_[:, ka, 0:n], start=start, stop=False)
            pe.matmul(dst, w_hi[:, slot, kk, :], lo_[:, ka, 0:n], start=False, stop=False)
            return pe.matmul(dst, w_lo[:, slot, kk, :], hi_[:, ka, 0:n], start=False, stop=stop)

        def pair(ph, units, dsts, n, k):
            slots = []
            for (j, c) in units:
                slot, g, _ = ph.at(j, c)
                pe.wait_ge(S("w_lo_ready"), g + 1)
                slots.append(slot)
            for kk in range(DC):
                pe.wait_ge(S("u_ready"), DC * k + kk + 1)
                for s, d, nn in zip(slots, dsts, n):
                    last = three(d, s, kk, u_hi, u_lo, kk, nn, kk == 0, kk == DC - 1)
                    if kk == DC - 1:
                        last.then_inc(S("w_used"), 1)

        def mean_square(k):
            n = norm_tokens(k)
            pe.wait_ge(S("ssq_added"), DC * (k + 1))
            pe.matmul(bank[:, 6, 0:n], ones_mean[:], ssq[:, 0:n], start=True, stop=True).then_inc(S("ms_ready"), 1)

        def mod_reduce(G):
            pe.wait_ge(S("acc_ready"), G + 1)
            wait(pe, S("mod_kept"), 2 * G)
            for v in range(2):
                pe.matmul(bank[:, 6 + v, :], ones_r[:], acc_hi[:, v, :], start=True, stop=False)
                last = pe.matmul(bank[:, 6 + v, :], ones_r[:], acc_lo[:, v, :], start=False, stop=True)
            last.then_inc(S("red_ready"), 1)

        def ffn(l, f):
            k = norm_of(l, f)
            n = norm_tokens(k)
            for half in (0, 1):
                ph = phases[l, f, "in", half]
                s0 = ffn_step(l, f, half)
                mods = bodies_of_mods(l, f, "in", half)

                def hidden(s, c, i):
                    b = (s0 + c) % 2
                    wait(pe, S("h_ready"), s0 + s - 1)
                    if isinstance(s, int) and s == 0 and half == 0:
                        pair(ph, [(0, 0), (1, 0)], [bank[:, 2 * b, 0:n], bank[:, 2 * b + 1, 0:n]], [n, n], k)
                        return
                    for j in range(2):
                        products(ph, j, c, i, 2, bank[:, 2 * b + j, 0:n], u_hi, u_lo, 0, n, True, True)

                def body(i):
                    for c in range(2):
                        hidden(c + i * 2, c, i)
                    if mods:
                        mod_reduce(mods[0] + i)
                turns(pe, FH // 2, body, peel=half == 0)
                hidden(FH - 1, FH - 1, 0)
                ph = phases[l, f, "out", half]
                m0 = out_step(l, f, half)
                mods = bodies_of_mods(l, f, "out", half)

                def body(i):
                    for c in range(2):
                        pe.wait_ge(S("x_done"), m0 - 1 + c + i * 2)
                        for j in range(2):
                            def hidden_wait(kc):
                                if kc >= FH - 2:
                                    pe.wait_ge(S("h_ready"), s0 + kc + 1)
                            products(ph, j, c, i, 2, bank[:, 4 + c, 0:n], h_hi, h_lo, j * FFN_OUT[0], n, j == 0, j == 1,
                                     hidden_wait if c == 0 else None)
                    if mods:
                        mod_reduce(mods[0] + i)
                turns(pe, DC // 2 - 1, body)
                body(DC // 2 - 1)

        pe.wait_ge(ident_loaded, 16)
        pe.wait_ge(vec_loaded, 16)
        for l in range(DEPTH):
            last = pe.transpose(bank[:, 6, V_ROWS * l:V_ROWS * (l + 1)], vec_rows[:, l, :], ident[0:V_ROWS, 0:V_ROWS])
        last.then_inc(S("vec_t"), 1)
        for s in range(2):
            pe.wait_ge(rows_loaded[s], 16)
        for d in range(DC):
            wait(pe, S("x_done"), d - 1)
            for a in range(2 * TT):
                last = pe.transpose(bank[:, 4 + d % 2, P * a:P * a + P], tok_rows[:, a, P * d:P * d + P], ident[:])
            last.then_inc(S("x_turned"), 1)
        pe.wait_ge(S("sil_ready"), 1)
        for g in range(N_START):
            pe.wait_ge(first_loaded[g], 16)
            for kk in range(DC):
                last = pe.matmul(bank[0:2, g, :], sil[:, :, kk], mod_first[:, g, kk, :], start=kk == 0, stop=kk == DC - 1)
            last.then_inc(S("rows_mm"), 1)
        for g in range(N_START):
            pe.wait_ge(S("mod_rows_ready"), g + 1)
            for a in range(MGC):
                o = 2 * (MGC * g + a)
                last = pe.transpose(bank[:, 7, o:o + 2], mod_rows[:, g, P * a:P * a + P], ident[0:2, 0:2])
        last.then_inc(S("modt_ready"), 1)
        pe.wait_ge(S("vec_ready"), 1)
        pe.wait_ge(S("ones_set"), 3)
        mean_square(0)
        pe.wait_ge(S("ones_r_set"), 1)
        for l in range(DEPTH):
            ffn(l, 1)
            k = norm_of(l, 0)
            pe.wait_ge(S("mod_kept"), 2 * mods_done(l, 1))
            mean_square(k)
            ph = phases[l, "head"]
            nh = len(HEAD)

            pe.wait_ge(const_loaded, 16 * 4)

            def statistics(c):
                n = head_tokens(l, HEAD[c][0])
                pe.wait_ge(S("qk_sq"), 5 * l + c + 1)
                wait(pe, S("qk_root"), 5 * l + c)
                pe.matmul(bank[:, 4, 0:n], head_mean[:], sq[:, c % 2, 0:n], start=True, stop=True).then_inc(S("qk_ms"), 1)

            def swap(c):
                pe.wait_ge(S("qk_normed"), 5 * l + c + 1)
                wait(pe, S("qk_ready"), 5 * l + c)
                pe.matmul(bank[:, 5, 0:SEQ], rope_swap[:], qk[:, c, 0:SEQ], start=True, stop=True).then_inc(S("qk_swapped"), 1)

            for idx in range(nh):
                n = head_tokens(l, HEAD[idx][0])
                if idx == 0:
                    n1 = head_tokens(l, HEAD[1][0])
                    pair(ph, [(0, 0), (1, 0)], [bank[:, 0, 0:n], bank[:, 1, 0:n1]], [n, n1], k)
                    continue
                if idx > 1:
                    if idx >= 4:
                        if idx - 4 < 5:
                            pe.wait_ge(S("qk_raw"), 5 * l + idx - 3)
                        else:
                            pe.wait_ge(S("head_copied"), 9 * l + idx - 8)
                    products(ph, idx, 0, 0, 0, bank[:, idx % 4, 0:n], u_hi, u_lo, 0, n, True, True)
                if 1 <= idx <= 5:
                    statistics(idx - 1)
                if 2 <= idx <= 6:
                    swap(idx - 2)
            for c in range(3):
                if c < 2:
                    pe.wait_ge(S("qk_ready"), 5 * l + 5)
                    pe.wait_ge(S("head_copied"), 9 * l + (1, 6, 7)[c])
                else:
                    pe.wait_ge(S("head_copied"), 9 * l + 7)
                    pe.wait_ge(S("vn_ready"), 3 * l + 1)
                for a in range(4):
                    last = pe.transpose(bank[:, 4 + c % 2, P * a:P * a + P], vT[:, c, P * a:P * a + P], ident[:])
                last.then_inc(S("vt_ready"), 1)
            pe.wait_ge(S("bias_loaded"), 16 * ROWS * NA_HEADS * (l + 1))
            for j in range(4):
                if j >= 2:
                    pe.wait_ge(S("bias_ready"), 4 * l + j - 1)
                pe.matmul(bank[:, 6 + j % 2, :], flip[:], bias[:, j // 2, 2 * (j % 2):2 * (j % 2) + 2, :],
                          start=True, stop=True).then_inc(S("flipped"), 1)
            pe.wait_ge(S("bias_ready"), 4 * l + 4)
            pe.wait_ge(S("tables_loaded"), 48 * (l + 1))
            pe.wait_ge(S("head_copied"), 9 * l + 9)
            tiles = TT if l == DEPTH - 1 else 2 * TT
            for c in range(2):
                for b in range(tiles // 2):
                    if c == 1:
                        pe.wait_ge(S("z_copied"), z0[l] + b + 1)
                    for a in range(2):
                        o = (2 * b + a) * P
                        last = pe.matmul(bank[:, 6 + b, 2 * P * a:2 * P * a + 2 * P], fT[:, c, o:o + P], dft_chan[:],
                                         start=True, stop=True)
                    last.then_inc(S("z_ready"), 1)
            pe.wait_ge(S("z_copied"), z0[l] + tiles)
            for c in range(2):
                for s in range(tiles // TT):
                    for a in range(TT):
                        for part in range(2):
                            last = pe.matmul(bank[:, 6 + c, SEQ * s:SEQ * s + SEQ], Zs[:, c, TT * s + a, P * part:P * part + P],
                                             dft_tok[:, part, a, :], start=a == 0 and part == 0, stop=a == TT - 1 and part == 1)
                last.then_inc(S("four_ready"), 1)
            js = jobs(l)
            per = 2 if l == DEPTH - 1 else 4

            def scores(q):
                kind, c, up, s = js[q]
                J = job0[l] + q
                rows = slice(HD * up, HD * up + HD)
                keys = slice(0, TOK) if s == 0 else slice(SEQ, TOK)
                nk = TOK if s == 0 else CTX
                if kind == "g":
                    qs, ks = qk[rows, 1 + c, :], qk[rows, 0, keys]
                else:
                    qs, ks = nqk[rows, 2 + c, :], nqk[rows, c, keys]
                wait(pe, S("exp_done"), J - 1)
                for b in range(TT):
                    o = SEQ * s + P * b
                    last = pe.matmul(bank[:, 2 * (J % 2) + b, 0:nk], qs[:, o:o + P], ks, start=True, stop=True)
                last.then_inc(S("s_ready"), 1)

            def transposes(q):
                kind, c, up, s = js[q]
                J = job0[l] + q
                pe.wait_ge(S("p_ready"), J + 1)
                wait(pe, S("pt_act"), J)
                wait(pe, S("pt_dve"), J)
                for kt in range(4 if s == 0 else 2):
                    for b in range(TT):
                        dst = bank[:, 4 + kt // 2, SEQ * (kt % 2) + P * b:SEQ * (kt % 2) + P * b + P] if s == 0 \
                            else bank[:, 4 + kt, P * b:P * b + P]
                        last = pe.transpose(dst, probs[:, J % 2, b, P * kt:P * kt + P], ident[:])
                last.then_inc(S("pt_ready"), 1)

            def values(q):
                kind, c, up, s = js[q]
                J = job0[l] + q
                chunk = q // per
                if q % per == 0 and chunk >= 2:
                    pe.wait_ge(S("cat_ready"), DC * l + 2 + chunk - 1)
                pe.wait_ge(S("pt_act"), J + 1)
                pe.wait_ge(S("pt_dve"), J + 1)
                v0 = HD * up if kind == "g" else P + P * c + HD * up
                dst = bank[HD * up:HD * up + HD, 6 + chunk % 2, SEQ * s:SEQ * s + SEQ]
                tiles_ = 4 if s == 0 else 2
                for kt in range(tiles_):
                    key_tile = kt if s == 0 else 2 + kt
                    last = pe.matmul(dst, Vn[:, key_tile, v0:v0 + HD], pT[:, J % 2, kt, :], start=kt == 0, stop=kt == tiles_ - 1)
                last.then_inc(S("o_ready"), 1)

            pe.wait_ge(S("head_copied"), 9 * l + 9)
            pe.wait_ge(S("vn_ready"), 3 * l + 3)
            pe.wait_ge(S("cat_ready"), DC * l + 2)
            N = len(js)
            for q in range(N + 3):
                if q < N:
                    scores(q)
                if 2 <= q <= N + 1:
                    transposes(q - 2)
                if q >= 3:
                    values(q - 3)
            ph = phases[l, "gate"]
            n = late_tokens(l)
            pe.wait_ge(S("exp_done"), job0[l] + N)
            pe.wait_ge(S("pt_dve"), job0[l] + N)
            pe.wait_ge(S("pt_act"), job0[l] + N)
            MG0 = DC * l

            def body(i):
                for j in range(3):
                    wait(pe, S("sig_ready"), 3 * MG0 + j - 2 + i * 3)
                    products(ph, j, 0, i, 1, bank[:, j, 0:n], u_hi, u_lo, 0, n, True, True)
                wait(pe, S("prod_done"), MG0 + i)
                if isinstance(i, int):
                    pe.wait_ge(S("cat_ready"), DC * (l + 1))
                slot, g, _ = ph.at(3, 0, i, 1)
                pe.wait_ge(S("w_lo_ready"), g + 1)
                for b, (k0, k1) in enumerate(((0, 2), (2, 6), (6, 8))):
                    for kk in range(k0, k1):
                        last = three(bank[:, 3 + b, 0:n], slot, kk, cat_hi, cat_lo, kk, n, kk == k0, kk == k1 - 1)
                last.then_inc(S("w_used"), 1)
            turns(pe, DC, body, peel=True)
            ph = phases[l, "wo"]
            m0 = out_step(l, 0)
            pe.wait_ge(S("prod_done"), MG0 + DC)

            def body(i):
                for c in range(2):
                    for j in range(2):
                        pe.wait_ge(S("x_done"), m0 - 1 + 2 * c + j + i * 4)

                        def merged(kc):
                            if c == 0 and j == 0:
                                pe.wait_ge(S("mg_ready"), MG0 + kc + 1)
                        products(ph, j, c, i, 2, bank[:, 4 + j, 0:n], mg_hi, mg_lo, 0, n, True, True, merged)
            turns(pe, 2, body)
            mean_square(norm_of(l, 2))
            ffn(l, 2)
            if l == 0:
                pe.wait_ge(S("mod_kept"), 2 * mods_done(l, 2))
            mean_square(norm_of(l, 2) + 1)
        for a in range(TT):
            for d in range(DC):
                pe.wait_ge(S("y_ready_t"), d + 1)
                q = 2 * a + d // 4
                last = pe.transpose(bank[:, q, P * (d % 4):P * (d % 4) + P], x[:, d, P * a:P * a + P], ident[:])
                if d % 4 == 3:
                    last.then_inc(S("yt_ready"), 1)
    ctx.close()


IN_NAMES = ["x", "c", "ctx", "c_ctx", "mod_w", "mod_b", "norm_ffn1", "ffn1_w_in", "ffn1_w_out", "norm_mix", "w_in", "q_norm",
            "k_norm", "na_rpb", "w_fourier", "w_gqa_out", "w_na_out", "w_o", "norm_ffn2", "ffn2_w_in", "ffn2_w_out", "final_norm"]


def constants():
    f32 = np.float32
    c = {"c_ident": np.eye(P, dtype=f32)}
    c["c_head_mean"] = np.kron(np.eye(2), np.full((HD, HD), 1.0 / HD)).astype(f32)
    swap = np.zeros((P, P), f32)
    for i in range(0, P, 2):
        swap[i + 1, i] = -1.0
        swap[i, i + 1] = 1.0
    c["c_rope_swap"] = swap
    c["c_flip"] = np.kron(np.eye(2), np.eye(GRID_W)[::-1]).astype(f32)
    tok = np.arange(SEQ)
    freqs = f32(10000.0) ** (-np.arange(HD // 4, dtype=f32) / f32(HD // 4))
    ang = np.concatenate([(tok // GRID_W).astype(f32)[:, None] * freqs, (tok % GRID_W).astype(f32)[:, None] * freqs], axis=1)
    pair = (np.arange(P) % HD) // 2
    c["c_rope"] = np.stack([np.cos(ang.astype(np.float64)).T[pair], np.sin(ang.astype(np.float64)).T[pair]], axis=1).astype(f32)
    ch = np.arange(FG)
    a = 2 * np.pi * (np.outer(ch, ch) % FG) / FG
    c["c_dft_chan"] = np.concatenate([np.kron(np.eye(2), np.cos(a)), np.kron(np.eye(2), np.sin(a))], axis=1).astype(f32)
    b = 2 * np.pi * (np.outer(tok, tok) % SEQ) / SEQ
    norm = 1.0 / np.sqrt(SEQ * FG)
    both = np.stack([np.cos(b) * norm, -np.sin(b) * norm])
    c["c_dft_tok"] = np.ascontiguousarray(both.reshape(2, TT, P, SEQ).transpose(2, 0, 1, 3)).astype(f32)
    col = np.arange(GRID_W)
    cs = np.clip(col - WIN_W // 2, 0, GRID_W - WIN_W)
    inside = (col[None, :] >= cs[:, None]) & (col[None, :] < cs[:, None] + WIN_W)
    c["c_band"] = np.where(np.tile(inside, (2, 1)), 0.0, -1e30).astype(f32)
    return c


def kernel(**inputs):
    import concourse.bacc as _bacc
    from concourse.bass_utils import run_bass_kernel_spmd as _run

    nc = _bacc.Bacc("TRN2", target_bir_lowering=False, num_devices=1)
    a = {n: np.ascontiguousarray(inputs[n]) for n in IN_NAMES}
    feed = {n: a[n] for n in ("mod_w", "ffn1_w_in", "ffn1_w_out", "w_in", "na_rpb", "w_fourier", "w_gqa_out", "w_na_out", "w_o",
                              "ffn2_w_in", "ffn2_w_out")}
    feed["x"], feed["ctx"] = a["x"][0], a["ctx"][0]
    packs = []
    for l in range(DEPTH):
        rows = [a["mod_b"][l], a["norm_ffn1"][l], a["norm_mix"][l], a["norm_ffn2"][l], a["final_norm"], a["c"][0], a["c_ctx"],
                a["q_norm"][l], a["q_norm"][l], a["k_norm"][l], a["k_norm"][l]]
        packs.append(np.concatenate([r.reshape(-1) for r in rows]).reshape(V_ROWS, P))
    feed["vec_rows"] = np.ascontiguousarray(np.stack(packs, axis=1))
    feed.update(constants())
    arrays, t = {}, {}
    for name, v in feed.items():
        arrays[f"in_{name}"] = v
        t[name] = nc.dram_tensor(f"in_{name}", v.shape, mybir.dt.from_np(v.dtype), kind="ExternalInput").ap()
    out = nc.dram_tensor("out_y", (SEQ, D), F32, kind="ExternalOutput").ap()
    build(nc, t, out)
    r = _run(nc, [arrays], core_ids=[0])
    return r.results[0]["out_y"].reshape(1, SEQ, D)
```

```python
from contextlib import ExitStack

import numpy as np
import concourse.bass as bass
from concourse import mybir

F32 = mybir.dt.float32
F32R = mybir.dt.float32r
ALU = mybir.AluOpType
ACT = mybir.ActivationFunctionType
AX_X = mybir.AxisListType.X

P = 128
D = 1024
DC = D // P
SEQ = 256
CTX = 256
TOK = SEQ + CTX
TT = SEQ // P
DEPTH = 2
GRID_W = 64
ROWS = SEQ // GRID_W
HD = 64
KV_HEADS = 2
GQA_CHUNKS = 4
NA_HEADS = 4
WIN_H, WIN_W = 8, 16
D_FF = 2816
FH = D_FF // P // 2
FW = 256
FG = 64
N_MOD = 9
MODC = N_MOD * DC
EPS = 1e-6
COL_F, COL_Q, COL_K, COL_V = 0, 256, 768, 896
COL_NQ, COL_NK, COL_NV, COL_GATE = 1024, 1280, 1536, 1792
MG = 512
MK = 4
MGC = MG // P
N_START = 4
RING = 4
V_MODB, V_N1, V_NM, V_N2, V_FIN, V_C, V_CC, V_QN, V_KN, V_ROWS = 0, 72, 80, 88, 96, 104, 112, 120, 121, 122


class Phase:

    def __init__(self, plan, steps, kd, w=None):
        self.nu, self.steps, self.kd = len(kd), steps, kd
        self.w = w or [1] * len(kd)
        self.g0 = plan["g"]
        self.base = list(plan["loaded"])
        for q in range(steps * self.nu):
            plan["loaded"][(self.g0 + q) % RING] += 16 * self.w[q % self.nu]
        plan["g"] += steps * self.nu

    def at(self, j, c, i=0, per=0):
        q = self.nu * c + j
        slot = (self.g0 + q) % RING
        if self.steps == 1:
            same = [self.w[jj] for jj in range(j + 1) if (j - jj) % RING == 0]
            return slot, self.g0 + q, self.base[slot] + 16 * sum(same)
        turns = self.nu * per // RING
        return slot, self.g0 + q + self.nu * per * i, self.base[slot] + 16 * self.w[j] * (q // RING + 1 + turns * i)


def build(nc, t, out):
    ctx = ExitStack()
    sem = {}

    def S(name):
        if name not in sem:
            sem[name] = ctx.enter_context(nc.semaphore(name))
        return sem[name]

    def place(st, name, shape, dt=F32):
        return st.enter_context(nc.sbuf_tensor(name, shape, dt))

    def sb(name, shape, dt=F32):
        return place(ctx, name, shape, dt)

    plan = {"g": 0, "loaded": [0] * RING}
    FFN_IN, FFN_OUT = [8, 8], [6, 5]
    phases = {}
    for l in range(DEPTH):
        for f in (1, 2):
            if f == 2:
                phases[l, "head"] = Phase(plan, 1, [8] * 14, [1, 2, 2, 2, 2] + [1] * 9)
                phases[l, "gate"] = Phase(plan, DC, [8, 8, 8, 8], [1, 1, 1, 4])
                phases[l, "wo"] = Phase(plan, DC // 2, [8, 8])
            for half in (0, 1):
                phases[l, f, "in", half] = Phase(plan, FH, FFN_IN)
                phases[l, f, "out", half] = Phase(plan, DC, FFN_OUT)
    UNITS = plan["g"]
    order = list(phases)
    HEAD = ([("k", COL_K)] + [("q", c) for c in range(GQA_CHUNKS)] + [("v", COL_V)]
            + [("nk", COL_NK + P * c) for c in range(2)] + [("nq", COL_NQ + P * c) for c in range(2)]
            + [("nv", COL_NV + P * c) for c in range(2)] + [("f", COL_F + P * c) for c in range(2)])

    def head_tokens(l, kind):
        return SEQ if l == DEPTH - 1 and kind in ("q", "nq", "f") else TOK

    def late_tokens(l):
        return SEQ if l == DEPTH - 1 else TOK

    def norm_tokens(k):
        return TOK if k < 5 else SEQ

    BG = {(0, 1): (0, N_START), (0, 2): (1, 0), (1, 1): (1, 13)}
    BG_PARTS = {(0, 1): {("in", 0): 5, ("out", 0): 4, ("in", 1): 5}, (0, 2): {("in", 0): 4, ("out", 0): 4, ("in", 1): 5},
                (1, 1): {("in", 1): 5}}
    BG_COUNT = {k: sum(v.values()) for k, v in BG_PARTS.items()}
    BG_BASE = {k: sum(BG_COUNT[o] for o in BG if o < k) for k in BG}

    def jobs(l):
        streams = (0,) if l == DEPTH - 1 else (0, 1)
        return ([("g", c, up, s) for c in range(GQA_CHUNKS) for s in streams for up in (0, 1)]
                + [("n", c, up, s) for c in range(2) for s in streams for up in (0, 1)])

    job0, z0 = [0], [0]
    for l in range(DEPTH):
        job0.append(job0[-1] + len(jobs(l)))
        z0.append(z0[-1] + (TT if l == DEPTH - 1 else 2 * TT))

    x = sb("x", [P, DC, TOK])
    u_hi = sb("u_hi", [P, DC, TOK], F32R)
    u_lo = sb("u_lo", [P, DC, TOK], F32R)
    w_raw = sb("w_raw", [P, RING, 8, P])
    w_hi = sb("w_hi", [P, RING, 8, P], F32R)
    w_lo = sb("w_lo", [P, RING, 8, P], F32R)
    ident = sb("ident", [P, P])
    ones_mean = sb("ones_mean", [P, P])
    ones_f = sb("ones_f", [P, P])
    ones_r = sb("ones_r", [P, P], F32R)
    head_mean = sb("head_mean", [P, P])
    rope_swap = sb("rope_swap", [P, P])
    flip = sb("flip", [P, P])
    band = sb("band", [P, GRID_W])
    vec_rows = sb("vec_rows", [V_ROWS, DEPTH, P])
    vec = sb("vec", [P, DEPTH, V_ROWS])
    sil = sb("sil", [P, 2, DC])
    modcol = sb("modcol", [P, DEPTH, 2, MODC])
    colA = sb("colA", [P, 6, 2, DC])
    colB = sb("colB", [P, 6, 2, DC])
    colG = sb("colG", [P, 6, 2, DC])
    eps_col = sb("eps_col", [P, 1])
    shift_split = sb("shift_split", [P, DC, 4], F32R)
    shift_sum = sb("shift_sum", [P, 2, 2])
    gq = sb("gq", [P, DEPTH])
    sq = sb("sq", [P, 2, TOK])
    ssq = sb("ssq", [P, TOK])
    root = sb("root", [P, TOK])
    rstd = sb("rstd", [P, TOK])
    tmp = sb("tmp", [P, 4, TOK])
    smax = sb("smax", [P, 2, 2])
    rsum = sb("rsum", [P, 2, 2])
    rrec = sb("rrec", [P, 2, 2])
    with ExitStack() as st:
        h_hi = place(st, "h_hi", [P, FH, TOK], F32R)
        h_lo = place(st, "h_lo", [P, FH, TOK], F32R)
        sg = place(st, "sg", [P, 2, TOK])
        hf = place(st, "hf", [P, 2, TOK])
        mod_w = place(st, "mod_w", [P, 2, MK, MG])
        acc = place(st, "acc", [P, 2, MG])
        acc_hi = place(st, "acc_hi", [P, 2, MG], F32R)
        acc_lo = place(st, "acc_lo", [P, 2, MG], F32R)
        mtmp = place(st, "mtmp", [P, 2 * MGC, P])
    with ExitStack() as st:
        tok_rows = place(st, "tok_rows", [P, 2 * TT, D])
        mod_first = place(st, "mod_first", [P, N_START, DC, MG])
    with ExitStack() as st:
        mod_rows = place(st, "mod_rows", [2, N_START, MG])
        y_rows = place(st, "y_rows", [P, TT, D])
    with ExitStack() as st:
        cat_hi = place(st, "cat_hi", [P, DC, TOK], F32R)
        cat_lo = place(st, "cat_lo", [P, DC, TOK], F32R)
        with ExitStack() as st2:
            qk = place(st2, "qk", [P, 1 + GQA_CHUNKS, TOK])
            nqk = place(st2, "nqk", [P, 4, TOK])
            Vn = place(st2, "Vn", [P, 4, 3 * P])
            bias = place(st2, "bias", [P, TT, NA_HEADS, SEQ])
            with ExitStack() as st3:
                probs = place(st3, "probs", [P, 2, 2, TOK])
                pT = place(st3, "pT", [P, 2, 4, SEQ])
            with ExitStack() as st3:
                fT = place(st3, "fT", [P, 2, TOK])
                Zs = place(st3, "Zs", [P, 2, 4, 2 * P])
                dft_chan = place(st3, "dft_chan", [P, 2 * P])
                dft_tok = place(st3, "dft_tok", [P, 2, TT, SEQ])
        with ExitStack() as st2:
            mg_hi = place(st2, "mg_hi", [P, DC, TOK], F32R)
            mg_lo = place(st2, "mg_lo", [P, DC, TOK], F32R)
            sig = place(st2, "sig", [P, 3, TOK])
    rope_cs = tmp[:, 3, :].rearrange("p (a t) -> p a t", a=2)
    vT = tmp[:, 0:3, :]

    bank = ctx.enter_context(nc.psum_tensor("bank", [P, 8, 512], F32))

    w_loaded = [S(f"w_loaded{i}") for i in range(RING)]
    mod_loaded = [S(f"mod_loaded{i}") for i in range(2)]
    first_loaded = [S(f"first_loaded{i}") for i in range(N_START)]
    rows_loaded = [S(f"rows_loaded{i}") for i in range(2)]
    vec_loaded = S("vec_loaded")
    ident_loaded = S("ident_loaded")
    const_loaded = S("const_loaded")

    def wait(eng, s, value):
        if not (isinstance(value, int) and value <= 0):
            eng.wait_ge(s, value)

    def turns(eng, n, body, peel=False, stop=None):
        lo = 0
        if peel:
            body(0)
            lo = 1
        if n - lo > 1:
            with eng.Fori(lo, n) as i:
                body(i)
        elif n - lo == 1:
            body(lo)

    def finished(ph, j, c, i=0, per=0):
        return ph.at(j, c, i, per)[1] + 1

    def ffn_step(l, f, half):
        return ((2 * l + f - 1) * 2 + half) * FH

    def out_step(l, f, half=0):
        return DC + l * 5 * DC + {1: half * DC, 0: 2 * DC, 2: (3 + half) * DC}[f]

    def x_count(k):
        l, w = divmod(k - 1, 3)
        return out_step(l, (1, 0, 2)[w], 0 if w == 1 else 1)

    def norm_of(l, f):
        return 3 * l + {1: 0, 0: 1, 2: 2}[f]

    def bodies_of_mods(l, f, part, half):
        parts = BG_PARTS.get((l, f), {})
        if (part, half) not in parts:
            return None
        names = list(parts)
        return BG_BASE[l, f] + sum(parts[o] for o in names[:names.index((part, half))]), parts[part, half]

    def mods_done(l, f):
        return sum(BG_COUNT[k] for k in BG if k <= (l, f))

    block = ctx.enter_context(nc.Block())

    @block.sync
    def _(sp):
        sp.dma_start(ident[:], t["c_ident"]).then_inc(ident_loaded, 16)
        sp.dma_start(vec_rows[:], t["vec_rows"]).then_inc(vec_loaded, 16)
        for s in range(2):
            rows = (t["x"], t["ctx"])[s]
            sp.dma_start(tok_rows[:, TT * s:TT * s + TT, :], rows.rearrange("(a p) d -> p a d", p=P)).then_inc(rows_loaded[s], 16)
        for g in range(N_START):
            sp.dma_start(mod_first[:, g], t["mod_w"][0].rearrange("(k p) c -> p k c", p=P)[:, :, MG * g:MG * g + MG]).then_inc(first_loaded[g], 16)

        def load(ph, srcs, j, c, i=0, per=0):
            slot, g, _ = ph.at(j, c, i, per)
            wait(sp, S("w_lo_ready"), g - RING + 1)
            for p0, p1, k0, k1, src in srcs:
                sp.dma_start(w_raw[p0:p1, slot, k0:k1, :], src).then_inc(w_loaded[slot], 16)

        for key in order:
            ph = phases[key]
            l = key[0]
            if len(key) == 4:
                _, f, part, half = key
                w = t[f"ffn{f}_w_in"][l] if part == "in" else t[f"ffn{f}_w_out"][l]
                w = w.rearrange("(k p) c -> p k c", p=P)
                if part == "in":
                    def body(i, steps=2):
                        for c in range(steps):
                            for j in range(2):
                                col = j * D_FF + (half * FH + c) * P + i * (2 * P)
                                load(ph, [(0, P, 0, DC, w[:, :, bass.ds(col, P)])], j, c, i, 2)
                    turns(sp, FH // 2, body, peel=ph.g0 == 0)
                    body(FH // 2, 1)
                else:
                    def body(i):
                        for c in range(2):
                            for j in range(2):
                                k0, n = half * FH + j * FFN_OUT[0], FFN_OUT[j]
                                load(ph, [(0, P, 0, n, w[:, k0:k0 + n, bass.ds(c * P + i * (2 * P), P)])], j, c, i, 2)
                    turns(sp, DC // 2, body)
            elif key[1] == "head":
                w = t["w_in"][l].rearrange("(k p) c -> p k c", p=P)
                for idx, (kind, col) in enumerate(HEAD):
                    if kind == "q":
                        srcs = [(0, P, 0, DC, w[:, :, COL_Q + HD * h:COL_Q + HD * h + HD]) for h in (col, col + GQA_CHUNKS)]
                        slot, g, _ = ph.at(idx, 0)
                        wait(sp, S("w_lo_ready"), g - RING + 1)
                        for up in (0, 1):
                            sp.dma_start(w_raw[:, slot, :, HD * up:HD * up + HD], srcs[up][4]).then_inc(w_loaded[slot], 16)
                    else:
                        load(ph, [(0, P, 0, DC, w[:, :, col:col + P])], idx, 0)
            elif key[1] == "gate":
                w = t["w_in"][l].rearrange("(k p) c -> p k c", p=P)
                wf = t["w_fourier"][l].rearrange("(k p) c -> p k c", p=P)
                wg = t["w_gqa_out"][l].rearrange("(u c p) n -> u p c n", u=2, p=HD)
                wn = t["w_na_out"][l].rearrange("(k p) c -> p k c", p=P)

                def body(i):
                    for j in range(3):
                        load(ph, [(0, P, 0, DC, w[:, :, bass.ds(COL_GATE + j * D + i * P, P)])], j, 0, i, 1)
                    cols = bass.ds(i * P, P)
                    load(ph, [(HD, P, 2, 6, wg[1][:, :, cols]), (0, HD, 2, 6, wg[0][:, :, cols]),
                              (0, P, 0, 2, wf[:, :, cols]), (0, P, 6, 8, wn[:, :, cols])], 3, 0, i, 1)
                turns(sp, DC, body)
            else:
                w = t["w_o"][l].rearrange("(k p) c -> p k c", p=P)

                def body(i):
                    for c in range(2):
                        for j in range(2):
                            load(ph, [(0, P, 0, DC, w[:, :, bass.ds((2 * c + j) * P + i * (4 * P), P)])], j, c, i, 2)
                turns(sp, 2, body)
        for a in range(TT):
            sp.wait_ge(S("y_rows_ready"), 4 * TT)
            sp.dma_start(out[a * P:a * P + P, :], y_rows[:, a, :]).then_inc(S("stored"), 16)
        sp.wait_ge(S("stored"), 16 * TT)

    @block.gpsimd
    def _(pool):
        for dst, name in ((head_mean, "c_head_mean"), (rope_swap, "c_rope_swap"), (flip, "c_flip"), (band, "c_band")):
            pool.dma_start(dst[:], t[name]).then_inc(const_loaded, 16)
        pool.memset(ones_mean[:], 1.0 / D).then_inc(S("ones_set"), 1)
        pool.memset(ones_f[:], 1.0).then_inc(S("ones_set"), 1)
        pool.memset(eps_col[:], EPS).then_inc(S("ones_set"), 1)

        def lo(ph, j, c, i=0, per=0):
            slot, g, _ = ph.at(j, c, i, per)
            n = ph.kd[j]
            pool.wait_ge(S("w_hi_ready"), g + 1)
            pool.tensor_tensor(w_lo[:, slot, 0:n, :], w_raw[:, slot, 0:n, :], w_hi[:, slot, 0:n, :].bitcast(F32),
                               ALU.subtract).then_inc(S("w_lo_ready"), 1)

        for key in order:
            ph = phases[key]
            l = key[0]
            if len(key) == 4:
                def body(i, steps=2):
                    for c in range(steps):
                        for j in range(2):
                            lo(ph, j, c, i, 2)
                if key[2] == "in":
                    turns(pool, FH // 2, body)
                    body(FH // 2, 1)
                else:
                    turns(pool, DC // 2, body)
            elif key[1] == "head":
                for idx in range(len(HEAD)):
                    lo(ph, idx, 0)
            elif key[1] == "gate":
                turns(pool, DC, lambda i: [lo(ph, j, 0, i, 1) for j in range(4)])
            else:
                turns(pool, 2, lambda i: [lo(ph, j, c, i, 2) for c in range(2) for j in range(2)])

    @block.scalar
    def _(act):
        def hi(ph, j, c, i=0, per=0):
            slot, g, loaded = ph.at(j, c, i, per)
            n = ph.kd[j]
            act.wait_ge(w_loaded[slot], loaded)
            wait(act, S("w_used"), g - RING + 1)
            act.activation(w_hi[:, slot, 0:n, :], w_raw[:, slot, 0:n, :], ACT.Copy).then_inc(S("w_hi_ready"), 1)

        def first_hi(key):
            ph = phases[key]
            for q in range(2):
                hi(ph, q % ph.nu, q // ph.nu)

        def following(key):
            at = order.index(key) + 1
            return order[at] if at < len(order) else None

        def square_at(M, Q, par, m, n):
            act.wait_ge(S("x_done"), M + 1)
            wait(act, S("ssq_added"), Q - 1)
            act.activation(sq[:, par, 0:n], x[:, bass.ds(m, 1), 0:n].rearrange("p a n -> p (a n)"), ACT.Square).then_inc(S("sq_ready"), 1)

        def first_scaled(k, m, par, i=0):
            q = DC * (k - 1) + m
            act.wait_ge(S("x_done"), x_count(k) + m + 1 + i * 2)
            wait(act, S("first_u_ready"), q - 1 + i * 2)
            for v in range(norm_tokens(k) // SEQ):
                cols = slice(SEQ * v, SEQ * v + SEQ)
                last = act.activation(tmp[:, 2 + par, cols], x[:, bass.ds(m + i * 2, 1), cols].rearrange("p a n -> p (a n)"),
                                      ACT.Copy, scale=colA[:, k, v, bass.ds(m + i * 2, 1)])
            last.then_inc(S("first_scaled"), 1)

        def root_of(k):
            n = norm_tokens(k)
            act.wait_ge(S("ms_ready"), k + 1)
            act.activation(root[:, 0:n], bank[:, 6, 0:n], ACT.Sqrt, bias=eps_col[:, 0:1]).then_inc(S("root_ready"), 1)

        def norm(k, key=None):
            n = norm_tokens(k)
            if k:
                if key:
                    ph = phases[key]
                    for q in (2, 3):
                        hi(ph, q % ph.nu, q // ph.nu)
                root_of(k)
            if k == 6:
                return
            if k:
                act.wait_ge(S("first_u_ready"), DC * k)
            for d in range(DC):
                if k == 0 and d == DC // 2:
                    copy_mod_rows(N_START - 1)
                q = DC * k + d
                act.wait_ge(S("t_ready"), q + 1)
                wait(act, S("u_ready"), q - 1)
                for v in range(n // SEQ):
                    cols = slice(SEQ * v, SEQ * v + SEQ)
                    last = act.activation(tmp[:, 2 + d % 2, cols], tmp[:, d % 2, cols], ACT.Identity,
                                          bias=colB[:, k, v, d:d + 1], scale=colA[:, k, v, d:d + 1])
                last.then_inc(S("uf_ready"), 1)

        def load_mod(G, l, group):
            wait(act, S("mod_mac"), 2 * DC * G)
            w = t["mod_w"][l].rearrange("(k p) c -> p k c", p=P)
            for kh in range(2):
                act.dma_start(mod_w[:, kh], w[:, MK * kh:MK * kh + MK, bass.ds(group * MG, MG)]).then_inc(mod_loaded[kh], 16)

        def mod_plan(l, f, G):
            layer, first = BG[l, f]
            return layer, first + G - BG_BASE[l, f]

        def ffn(l, f):
            k = norm_of(l, f)
            n = norm_tokens(k)
            nxt = norm_of(l, f) + 1
            if (l, f) in BG:
                G = BG_BASE[l, f]
                act.wait_ge(S("u_ready"), DC * k + 1)
                load_mod(G, *mod_plan(l, f, G))
            for half in (0, 1):
                key = (l, f, "in", half)
                ph = phases[key]
                mods = bodies_of_mods(l, f, "in", half)
                s0 = ffn_step(l, f, half)

                def silu(s, c, i=0):
                    act.wait_ge(S("w_used"), finished(phases[l, f, "in", half], 1, c, i, 2))
                    b = (s0 + c) % 2
                    wait(act, S("h_prod"), s0 + s - 1)
                    act.activation(sg[:, b, 0:n], bank[:, 2 * b + 1, 0:n], ACT.Silu).then_inc(S("silu_ready"), 1)

                def first_silu():
                    act.wait_ge(S("gate_scaled"), 2 * l + f - 1)
                    for v in range(n // SEQ):
                        cols = slice(SEQ * v, SEQ * v + SEQ)
                        last = act.activation(sg[:, s0 % 2, cols], sg[:, s0 % 2, cols], ACT.Silu, bias=shift_sum[:, 1, v:v + 1])
                    last.then_inc(S("silu_ready"), 1)

                def body(i, more=True):
                    start = half == 0 and isinstance(i, int) and i == 0
                    for c in range(2):
                        if not (start and c == 0):
                            for j in range(2):
                                hi(ph, j, c + 1, i, 2)
                        if c == 1 and mods and more and not (start and k):
                            G = mods[0] + i + 1 - (1 if half == 0 and k else 0)
                            load_mod(G, *mod_plan(l, f, G))
                        if start and c == 0 and k:
                            first_silu()
                        else:
                            silu(c + i * 2, c, i)
                if mods and mods[0] + mods[1] == BG_BASE[l, f] + BG_COUNT[l, f]:
                    turns(act, FH // 2 - 1, body, peel=half == 0)
                    body(FH // 2 - 1, more=False)
                else:
                    turns(act, FH // 2, body, peel=half == 0)
                first_hi(following(key))
                silu(FH - 1, FH - 1)
                key = (l, f, "out", half)
                ph = phases[key]
                mods = bodies_of_mods(l, f, "out", half)
                m0 = out_step(l, f, half)

                def body(i, tail=False):
                    for c in range(2):
                        if not (tail and c == 1):
                            for j in range(2):
                                hi(ph, j, c + 1, i, 2)
                        elif following(key):
                            first_hi(following(key))
                        if c == 1 and mods:
                            G = mods[0] + i + 1
                            load_mod(G, *mod_plan(l, f, G))
                        if half == 1:
                            square_at(m0 + c + i * 2, DC * nxt + c + i * 2, c, c + i * 2, norm_tokens(nxt))
                            if nxt < 6:
                                first_scaled(nxt, c, c, i)
                turns(act, DC // 2 - 1, body, peel=half == 1 and nxt == 1)
                body(DC // 2 - 1, tail=True)

        act.wait_ge(S("vec_ready"), 1)
        act.activation(sil[:].rearrange("p v k -> p (v k)"), vec[:, 0, V_C:V_C + 2 * DC], ACT.Silu).then_inc(S("sil_ready"), 1)
        for d in range(DC):
            square_at(d, d, d % 2, d, TOK)
        def copy_mod_rows(g):
            act.wait_ge(S("rows_mm"), g + 1)
            act.activation(mod_rows[:, g, :], bank[0:2, g, :], ACT.Copy).then_inc(S("mod_rows_ready"), 1)
        copy_mod_rows(0)
        copy_mod_rows(1)
        root_of(0)
        first_hi(order[0])
        copy_mod_rows(2)
        for j in range(2):
            hi(phases[order[0]], j, 1)
        norm(0)
        for l in range(DEPTH):
            ffn(l, 1)
            norm(norm_of(l, 0), (l, "head"))
            nh = len(HEAD)
            key = (l, "head")
            ph = phases[key]
            act.wait_ge(S("u_ready"), DC * (norm_of(l, 0) + 1))
            act.dma_start(rope_cs, t["c_rope"]).then_inc(S("rope_loaded"), 16)

            def load_bias(r, h):
                width = 2 * WIN_W - 1
                first = ((l * NA_HEADS + h) * (2 * WIN_H - 1) + WIN_H - 1 - r) * width + WIN_W - GRID_W
                src = bass.AP(tensor=t["na_rpb"].tensor, offset=first, ap=[[1, GRID_W], [width, ROWS], [1, GRID_W]])
                p0 = (r % 2) * GRID_W
                dst = bias[p0:p0 + GRID_W, r // 2, h, :].rearrange("p (i k) -> p i k", k=GRID_W)
                act.dma_start(dst, src).then_inc(S("bias_loaded"), 16)

            for idx, (kind, arg) in enumerate(HEAD):
                if 4 <= idx + 2 < nh:
                    hi(ph, idx + 2, 0)
                elif idx + 2 == nh:
                    first_hi((l, "gate"))
                if idx == 5:
                    act.dma_start(dft_chan[:], t["c_dft_chan"]).then_inc(S("dft_loaded"), 16)
                    act.dma_start(dft_tok[:], t["c_dft_tok"]).then_inc(S("dft_loaded"), 16)
                if 6 <= idx:
                    for b in range(2 * (idx - 6), 2 * (idx - 5)):
                        load_bias(b // NA_HEADS, b % NA_HEADS)
                n = head_tokens(l, kind)
                if 2 <= idx < 7:
                    c = idx - 2
                    nc_ = head_tokens(l, HEAD[c][0])
                    act.wait_ge(S("qk_ms"), 5 * l + c + 1)
                    wait(act, S("qk_normed"), 5 * l + c)
                    act.activation(root[:, 0:nc_], bank[:, 4, 0:nc_], ACT.Sqrt, bias=eps_col[:, 0:1]).then_inc(S("qk_root"), 1)
                if idx < 5:
                    act.wait_ge(S("qk_raw"), 5 * l + idx + 1)
                    act.activation(sq[:, idx % 2, 0:n], qk[:, idx, 0:n], ACT.Square).then_inc(S("qk_sq"), 1)
                if idx >= 5:
                    act.wait_ge(S("w_used"), finished(ph, idx, 0))
                    tile, first = {"v": (vT, 5), "nk": (nqk, 6), "nq": (nqk, 6), "nv": (vT, 9), "f": (fT, 12)}[kind]
                    dst = tile[:, idx - first, 0:n]
                    act.activation(dst, bank[:, idx % 4, 0:n], ACT.Copy,
                                   scale=HD ** -0.5 if kind == "nq" else 1.0).then_inc(S("head_copied"), 1)
            for c in range(3):
                act.wait_ge(S("vt_ready"), 3 * l + c + 1)
                act.activation(Vn[:, :, P * c:P * c + P], bank[:, 4 + c % 2, :].rearrange("p (k d) -> p k d", k=4), ACT.Copy)\
                   .then_inc(S("vn_ready"), 1)
            js = jobs(l)

            def copy_pt(q):
                J = job0[l] + q
                kind, c, up, s = js[q]
                act.wait_ge(S("pt_ready"), J + 1)
                src = bank[:, 5, :].rearrange("p (k t) -> p k t", k=2)
                dst = pT[:, J % 2, 2:4, :] if s == 0 else pT[:, J % 2, 1:2, :]
                act.activation(dst, src if s == 0 else src[:, 0:1, :], ACT.Copy).then_inc(S("pt_act"), 1)

            for q, (kind, c, up, s) in enumerate(js):
                J = job0[l] + q
                keys = TOK if s == 0 else CTX
                act.wait_ge(S("max_ready"), J + 1)
                wait(act, S("pt_ready"), J - 1)
                for b in range(TT):
                    last = act.activation(probs[:, J % 2, b, 0:keys], bank[:, 2 * (J % 2) + b, 0:keys], ACT.Exp,
                                          bias=smax[:, J % 2, b:b + 1], accum_out=rsum[:, J % 2, b:b + 1])
                last.then_inc(S("exp_done"), 1)
                if q:
                    copy_pt(q - 1)
            copy_pt(len(js) - 1)
            key = (l, "gate")
            ph = phases[key]
            n = late_tokens(l)

            def gate(i, j):
                act.wait_ge(S("w_used"), finished(ph, j, 0, i, 1))
                wait(act, S("prod_done"), DC * l + i)
                act.activation(sig[:, j, 0:n], bank[:, j, 0:n], ACT.Sigmoid).then_inc(S("sig_ready"), 1)

            def body(i, last=False):
                hi(ph, 2, 0, i, 1)
                gate(i, 0)
                hi(ph, 3, 0, i, 1)
                gate(i, 1)
                if not last:
                    hi(ph, 0, 1, i, 1)
                    gate(i, 2)
                    hi(ph, 1, 1, i, 1)
                else:
                    first_hi((l, "wo"))
                    gate(i, 2)
            turns(act, DC - 1, body, peel=True)
            body(DC - 1, last=True)
            key = (l, "wo")
            ph = phases[key]
            k = norm_of(l, 2)
            for m in range(DC):
                if m + 2 < DC:
                    hi(ph, m % 2, (m + 2) // 2)
                elif m + 2 == DC:
                    first_hi(following(key))
                square_at(out_step(l, 0) + m, DC * k + m, m % 2, m, norm_tokens(k))
                first_scaled(k, m, m % 2)
            norm(k, following(key))
            ffn(l, 2)
            norm(k + 1, (l + 1, 1, "in", 0) if l + 1 < DEPTH else None)
        for q in range(2 * TT):
            act.wait_ge(S("yt_ready"), q + 1)
            act.activation(y_rows[:, q // 2, 512 * (q % 2):512 * (q % 2) + 512], bank[:, q, :], ACT.Copy).then_inc(S("y_rows_ready"), 2)

    @block.vector
    def _(dve):
        chain = [0]

        def link(ins):
            chain[0] += 1
            ins.then_inc(S("dve_chain"), 1)
            dve.wait_ge(S("dve_chain"), chain[0])

        def columns_norm(k, d0=0, d1=DC):
            l, w = k // 3, k % 3
            gain = vec[:, l, V_N1 + DC * w + d0:V_N1 + DC * w + d1]
            for v in range(2):
                b0, b1 = 3 * DC * w + d0, 3 * DC * w + d1
                a0, a1 = b0 + DC, b1 + DC
                link(dve.tensor_tensor(colB[:, k, v, d0:d1], modcol[:, l, v, b0:b1], vec[:, l, b0:b1], ALU.add))
                link(dve.tensor_tensor(colA[:, k, v, d0:d1], modcol[:, l, v, a0:a1], vec[:, l, a0:a1], ALU.add))
                link(dve.scalar_tensor_tensor(out=colA[:, k, v, d0:d1], in0=colA[:, k, v, d0:d1], scalar=1.0, in1=gain,
                                              op0=ALU.add, op1=ALU.mult))
            if k:
                shift = colB[:, k].rearrange("p v d -> p d v")
                link(dve.tensor_copy(shift_split[:, :, 0:2], shift))
                dve.tensor_tensor(shift_split[:, :, 2:4], shift, shift_split[:, :, 0:2].bitcast(F32), ALU.subtract)\
                   .then_inc(S("shift_ready"), 1)

        def columns_gate(k):
            l, w = k // 3, k % 3
            for v in range(2):
                o = 3 * DC * w + 2 * DC
                link(dve.tensor_tensor(colG[:, k, v, :], modcol[:, l, v, o:o + DC], vec[:, l, o:o + DC], ALU.add))
                if w != 1:
                    link(dve.tensor_scalar(colG[:, k, v, :], colG[:, k, v, :], 0.5, None, ALU.mult))

        def add_squares(Q, par, n):
            dve.wait_ge(S("sq_ready"), Q + 1)
            wait(dve, S("ssq_added"), Q)
            dve.tensor_tensor(ssq[:, 0:n], ssq[:, 0:n], sq[:, par, 0:n], ALU.add).then_inc(S("ssq_added"), 1)

        def first_split(k, m, par, i=0):
            n = norm_tokens(k)
            q = DC * (k - 1) + m
            dve.wait_ge(S("first_scaled"), q + 1 + i * 2)
            us = u_hi[:, bass.ds(m + i * 2, 1), 0:n].rearrange("p a n -> p (a n)")
            dve.tensor_copy(us, tmp[:, 2 + par, 0:n]).then_inc(S("first_hi_done"), 1)
            dve.wait_ge(S("first_hi_done"), q + 1 + i * 2)
            dve.tensor_tensor(u_lo[:, bass.ds(m + i * 2, 1), 0:n].rearrange("p a n -> p (a n)"), tmp[:, 2 + par, 0:n],
                              us.bitcast(F32), ALU.subtract).then_inc(S("first_u_ready"), 1)

        def rstd_of(k):
            n = norm_tokens(k)
            dve.wait_ge(S("root_ready"), k + 1)
            link(dve.reciprocal(rstd[:, 0:n], root[:, 0:n]))

        def norm(k, first=None):
            n = norm_tokens(k)
            if k:
                rstd_of(k)
            if k == 6:
                return
            if k:
                dve.wait_ge(S("shift_summed"), k)
                sums = bank[:, 7, 0:8].rearrange("p (u a v) -> p u a v", u=2, a=2)
                link(dve.tensor_copy(shift_sum[:], sums[:, :, 0, :]))
                link(dve.tensor_tensor(shift_sum[:], shift_sum[:], sums[:, :, 1, :], ALU.add))

            def scale(d):
                dve.tensor_tensor(tmp[:, d % 2, 0:n], x[:, d, 0:n], rstd[:, 0:n], ALU.mult).then_inc(S("t_ready"), 1)

            scale(0)
            for d in range(DC):
                q = DC * k + d
                if k == 0 and d == DC // 2 - 1:
                    start_columns(N_START - 1, N_START)
                    columns_norm(0, DC // 2, DC)
                if d + 1 < DC:
                    scale(d + 1)
                dve.wait_ge(S("uf_ready"), q + 1)
                if k and d < DC - 1:
                    dve.wait_ge(S("first_used"), (DC - 1) * (k - 1) + d + 1)
                elif k:
                    dve.wait_ge(S("w_used"), finished(*first))
                dve.tensor_copy(u_hi[:, d, 0:n], tmp[:, 2 + d % 2, 0:n]).then_inc(S("u_hi_done"), 1)
                dve.wait_ge(S("u_hi_done"), q + 1)
                dve.tensor_tensor(u_lo[:, d, 0:n], tmp[:, 2 + d % 2, 0:n], u_hi[:, d, 0:n].bitcast(F32), ALU.subtract)\
                   .then_inc(S("u_ready"), 1)

        def mod_products(G):
            for k in range(DC):
                if k % MK == 0:
                    dve.wait_ge(mod_loaded[k // MK], G * 16 + 16)
                w = mod_w[:, k // MK, k % MK, :]
                for v in range(2):
                    if k == 0:
                        ins = dve.tensor_scalar(acc[:, v, :], w, sil[:, v, k:k + 1], None, ALU.mult)
                    else:
                        dve.wait_ge(S("mod_mac"), G * (2 * DC) + 2 * k + v - 1)
                        ins = dve.scalar_tensor_tensor(out=acc[:, v, :], in0=w, scalar=sil[:, v, k:k + 1], in1=acc[:, v, :],
                                                       op0=ALU.mult, op1=ALU.add)
                    ins.then_inc(S("mod_mac"), 1)

        def mod_split(G):
            dve.wait_ge(S("mod_mac"), G * (2 * DC) + 2 * DC)
            dve.tensor_copy(acc_hi[:], acc[:]).then_inc(S("acc_hi_done"), 1)
            dve.wait_ge(S("acc_hi_done"), G + 1)
            dve.tensor_tensor(acc_lo[:], acc[:], acc_hi[:].bitcast(F32), ALU.subtract).then_inc(S("acc_ready"), 1)

        def mod_extract(G, layer, group):
            dve.wait_ge(S("red_ready"), G + 1)
            dve.tensor_tensor(mtmp[:], bank[:, 6:8, :].rearrange("p v (a b) -> p (v a) b", a=MGC),
                              ident[:].unsqueeze(1).to_broadcast([P, 2 * MGC, P]), ALU.mult).then_inc(S("mod_masked"), 1)
            dve.wait_ge(S("mod_masked"), G + 1)
            dve.tensor_reduce(modcol[:, layer, :, bass.ds(group * MGC, MGC)], mtmp[:].rearrange("p (v a) b -> p v a b", v=2),
                              AX_X, ALU.add).then_inc(S("mod_kept"), 1)

        def mod_plan(l, f, G):
            layer, first = BG[l, f]
            return layer, first + G - BG_BASE[l, f]

        def update(done, par, m, k, n):
            dve.wait_ge(S("w_used"), done)
            for v in range(n // SEQ):
                cols = slice(SEQ * v, SEQ * v + SEQ)
                xs = x[:, bass.ds(m, 1), cols].rearrange("p a n -> p (a n)")
                last = dve.scalar_tensor_tensor(out=xs, in0=bank[:, 4 + par, cols], scalar=colG[:, k, v, bass.ds(m, 1)],
                                                in1=xs, op0=ALU.mult, op1=ALU.add)
            last.then_inc(S("x_done"), 1)

        def ffn(l, f):
            k = norm_of(l, f)
            n = norm_tokens(k)
            nxt = k + 1
            for half in (0, 1):
                s0 = ffn_step(l, f, half)
                mods = bodies_of_mods(l, f, "in", half)

                def hidden(s, c):
                    b = (s0 + c) % 2
                    dve.wait_ge(S("silu_ready"), s0 + s + 1)
                    dve.tensor_tensor(hf[:, b, 0:n], bank[:, 2 * b, 0:n], sg[:, b, 0:n], ALU.mult).then_inc(S("h_prod"), 1)
                    split_hidden(s, b)

                def split_hidden(s, b):
                    dve.wait_ge(S("h_prod"), s0 + s + 1)
                    hs = h_hi[:, bass.ds(s, 1), 0:n].rearrange("p a n -> p (a n)")
                    dve.tensor_copy(hs, hf[:, b, 0:n]).then_inc(S("h_hi_done"), 1)
                    dve.wait_ge(S("h_hi_done"), s0 + s + 1)
                    dve.tensor_tensor(h_lo[:, bass.ds(s, 1), 0:n].rearrange("p a n -> p (a n)"), hf[:, b, 0:n],
                                      hs.bitcast(F32), ALU.subtract).then_inc(S("h_ready"), 1)

                def first_hidden():
                    b = s0 % 2
                    dve.wait_ge(S("w_used"), finished(phases[l, f, "in", 0], 1, 0))
                    dve.tensor_tensor(sg[:, b, 0:n], bank[:, 2 * b + 1, 0:n], rstd[:, 0:n], ALU.mult).then_inc(S("gate_scaled"), 1)
                    link(dve.tensor_tensor(hf[:, b, 0:n], bank[:, 2 * b, 0:n], rstd[:, 0:n], ALU.mult))
                    dve.wait_ge(S("silu_ready"), s0 + 1)
                    for v in range(n // SEQ):
                        cols = slice(SEQ * v, SEQ * v + SEQ)
                        last = dve.scalar_tensor_tensor(out=hf[:, b, cols], in0=hf[:, b, cols], scalar=shift_sum[:, 0, v:v + 1],
                                                        in1=sg[:, b, cols], op0=ALU.add, op1=ALU.mult)
                    last.then_inc(S("h_prod"), 1)
                    split_hidden(0, b)

                def body(i):
                    start = half == 0 and isinstance(i, int) and i == 0
                    with_mods = mods and not (start and k)
                    G = mods[0] + i - (1 if half == 0 and k else 0) if with_mods else None
                    if with_mods:
                        mod_products(G)
                    if start and k:
                        first_hidden()
                    else:
                        hidden(0 + i * 2, 0)
                    if with_mods:
                        mod_split(G)
                    hidden(1 + i * 2, 1)
                    if with_mods:
                        mod_extract(G, *mod_plan(l, f, G))
                turns(dve, FH // 2, body, peel=half == 0)
                hidden(FH - 1, FH - 1)
                if half == 0:
                    dve.wait_ge(S("mod_kept"), BG_BASE[l, f] + BG_PARTS[l, f].get(("in", 0), 0) if (l, f) in BG else mods_done(l, f))
                    columns_gate(k)
                else:
                    if k < 5:
                        dve.wait_ge(S("mod_kept"), mods_done(l, f))
                        columns_norm(nxt)
                    link(dve.memset(ssq[:], 0.0))
                m0 = out_step(l, f, half)
                mods = bodies_of_mods(l, f, "out", half)

                def body(i):
                    G = mods[0] + i if mods else None
                    if mods:
                        mod_products(G)
                        mod_split(G)
                    for c in range(2):
                        update(finished(phases[l, f, "out", half], 1, c, i, 2), c, c + i * 2, k, n)
                        if half == 1:
                            add_squares(DC * nxt + c + i * 2, c, norm_tokens(nxt))
                            if nxt < 6:
                                first_split(nxt, c, c, i)
                    if mods:
                        mod_extract(G, *mod_plan(l, f, G))
                turns(dve, DC // 2 - 1, body)
                body(DC // 2 - 1)

        dve.wait_ge(S("ones_set"), 3)
        dve.tensor_copy(ones_r[:], ones_f[:]).then_inc(S("ones_r_set"), 1)
        link(dve.memset(ssq[:], 0.0))
        dve.wait_ge(S("vec_t"), 1)
        dve.tensor_copy(vec[:], bank[:, 6, 0:DEPTH * V_ROWS].rearrange("p (l r) -> p l r", l=DEPTH)).then_inc(S("vec_ready"), 1)
        dve.wait_ge(S("vec_ready"), 1)
        link(dve.tensor_scalar(gq[:], vec[:, :, V_QN], HD ** -0.5, None, ALU.mult))
        for d in range(DC):
            dve.wait_ge(S("x_turned"), d + 1)
            dve.tensor_copy(x[:, d, :], bank[:, 4 + d % 3, :]).then_inc(S("x_done"), 1)
            add_squares(d, d % 2, TOK)

        def start_columns(g0, g1):
            dve.wait_ge(S("modt_ready"), 1 if g1 < N_START else 2)
            link(dve.tensor_copy(modcol[:, 0, :, MGC * g0:MGC * g1],
                                 bank[:, 7, 2 * MGC * g0:2 * MGC * g1].rearrange("p (a v) -> p v a", v=2)))
        rstd_of(0)
        start_columns(0, N_START - 1)
        columns_norm(0, 0, DC // 2)
        norm(0)
        for l in range(DEPTH):
            ffn(l, 1)
            k = norm_of(l, 0)
            norm(k, (phases[l, "head"], 1, 0))
            nh = len(HEAD)
            for idx in range(8):
                if idx < 5:
                    n = head_tokens(l, HEAD[idx][0])
                    dve.wait_ge(S("w_used"), finished(phases[l, "head"], idx, 0))
                if idx < 2:
                    link(dve.tensor_tensor(qk[:, idx, 0:n], bank[:, idx, 0:n], rstd[:, 0:n], ALU.mult))
                    for v in range(n // SEQ):
                        cols = slice(SEQ * v, SEQ * v + SEQ)
                        last = dve.tensor_scalar(qk[:, idx, cols], qk[:, idx, cols], shift_sum[:, idx, v:v + 1], None, ALU.add)
                    last.then_inc(S("qk_raw"), 1)
                elif idx < 5:
                    dve.tensor_copy(qk[:, idx, 0:n], bank[:, idx % 4, 0:n]).then_inc(S("qk_raw"), 1)
                if 2 <= idx < 7:
                    c = idx - 2
                    n = head_tokens(l, HEAD[c][0])
                    gain = vec[:, l, V_KN:V_KN + 1] if c == 0 else gq[:, l:l + 1]
                    dve.wait_ge(S("qk_root"), 5 * l + c + 1)
                    link(dve.reciprocal(rstd[:, 0:n], root[:, 0:n]))
                    dve.scalar_tensor_tensor(out=qk[:, c, 0:n], in0=qk[:, c, 0:n], scalar=gain, in1=rstd[:, 0:n],
                                             op0=ALU.mult, op1=ALU.mult).then_inc(S("qk_normed"), 1)
                if idx >= 3:
                    c = idx - 3
                    dve.wait_ge(S("rope_loaded"), 16 * (l + 1))
                    dve.wait_ge(S("qk_swapped"), 5 * l + c + 1)
                    link(dve.tensor_tensor(ssq[:, 0:SEQ], bank[:, 5, 0:SEQ], rope_cs[:, 1, :], ALU.mult))
                    link(dve.tensor_tensor(ssq[:, SEQ:TOK], qk[:, c, 0:SEQ], rope_cs[:, 0, :], ALU.mult))
                    dve.tensor_tensor(qk[:, c, 0:SEQ], ssq[:, SEQ:TOK], ssq[:, 0:SEQ], ALU.add).then_inc(S("qk_ready"), 1)
            for j in range(4):
                dve.wait_ge(S("flipped"), 4 * l + j + 1)
                dve.tensor_tensor(bias[:, j // 2, 2 * (j % 2):2 * (j % 2) + 2, :].rearrange("p h (i k) -> p (h i) k", k=GRID_W),
                                  bank[:, 6 + j % 2, :].rearrange("p (i k) -> p i k", k=GRID_W),
                                  band[:].unsqueeze(1).to_broadcast([P, 2 * ROWS, GRID_W]), ALU.add).then_inc(S("bias_ready"), 1)
            tiles = TT if l == DEPTH - 1 else 2 * TT
            for c in range(2):
                for b in range(tiles // 2):
                    dve.wait_ge(S("z_ready"), z0[l] + c * (tiles // 2) + b + 1)
                    dve.tensor_copy(Zs[:, c, 2 * b:2 * b + 2, :], bank[:, 6 + b, :].rearrange("p (a z) -> p a z", a=2))\
                       .then_inc(S("z_copied"), 1)
            n = late_tokens(l)

            def to_cat(src, c, signal):
                link(dve.tensor_copy(cat_hi[:, c, 0:n], src))
                dve.tensor_tensor(cat_lo[:, c, 0:n], src, cat_hi[:, c, 0:n].bitcast(F32), ALU.subtract).then_inc(S("cat_ready"), 1)

            for c in range(2):
                dve.wait_ge(S("four_ready"), 2 * l + c + 1)
                to_cat(bank[:, 6 + c, 0:n], c, 1)
            js = jobs(l)
            per = 2 if l == DEPTH - 1 else 4

            def maximum(q):
                kind, c, up, s = js[q]
                J = job0[l] + q
                keys = TOK if s == 0 else CTX
                dve.wait_ge(S("s_ready"), J + 1)
                sc = bank[:, 2 * (J % 2):2 * (J % 2) + 2, 0:keys]
                if kind == "n" and s == 0:
                    link(dve.tensor_tensor(sc[:, :, 0:SEQ], sc[:, :, 0:SEQ], bias[:, :, 2 * c + up, :], ALU.add))
                link(dve.tensor_reduce(smax[:, J % 2, :], sc, AX_X, ALU.max))
                dve.tensor_scalar(smax[:, J % 2, :], smax[:, J % 2, :], -1.0, None, ALU.mult).then_inc(S("max_ready"), 1)

            def normalise(q):
                kind, c, up, s = js[q]
                J = job0[l] + q
                keys = TOK if s == 0 else CTX
                dve.wait_ge(S("exp_done"), J + 1)
                link(dve.reciprocal(rrec[:, J % 2, :], rsum[:, J % 2, :]))
                for b in range(TT):
                    last = dve.tensor_scalar(probs[:, J % 2, b, 0:keys], probs[:, J % 2, b, 0:keys], rrec[:, J % 2, b:b + 1],
                                             None, ALU.mult)
                last.then_inc(S("p_ready"), 1)

            def copy_pt(q):
                kind, c, up, s = js[q]
                J = job0[l] + q
                dve.wait_ge(S("pt_ready"), J + 1)
                src = bank[:, 4, :].rearrange("p (k t) -> p k t", k=2)
                dst = pT[:, J % 2, 0:2, :] if s == 0 else pT[:, J % 2, 0:1, :]
                dve.tensor_copy(dst, src if s == 0 else src[:, 0:1, :]).then_inc(S("pt_dve"), 1)

            def finish(q):
                if (q + 1) % per == 0:
                    chunk = q // per
                    dve.wait_ge(S("o_ready"), job0[l] + q + 1)
                    to_cat(bank[:, 6 + chunk % 2, 0:n], 2 + chunk, 1)

            N = len(js)
            for q in range(N + 4):
                if q < N:
                    maximum(q)
                if 1 <= q <= N:
                    normalise(q - 1)
                if 2 <= q <= N + 1:
                    copy_pt(q - 2)
                if q >= 4:
                    finish(q - 4)
            key = (l, "gate")
            MG0 = DC * l

            def body(i):
                dve.wait_ge(S("sig_ready"), 3 * MG0 + 3 + i * 3)
                dve.wait_ge(S("w_used"), finished(phases[key], 3, 0, i, 1))
                for j in range(3):
                    last = dve.tensor_tensor(tmp[:, j, 0:n], bank[:, 3 + j, 0:n], sig[:, j, 0:n], ALU.mult)
                last.then_inc(S("prod_done"), 1)
                dve.wait_ge(S("prod_done"), MG0 + 1 + i)
                dve.tensor_tensor(tmp[:, 3, 0:n], tmp[:, 0, 0:n], tmp[:, 1, 0:n], ALU.add).then_inc(S("sum_step"), 1)
                dve.wait_ge(S("sum_step"), 2 * MG0 + 1 + i * 2)
                dve.tensor_tensor(tmp[:, 3, 0:n], tmp[:, 3, 0:n], tmp[:, 2, 0:n], ALU.add).then_inc(S("sum_step"), 1)
                dve.wait_ge(S("sum_step"), 2 * MG0 + 2 + i * 2)
                ms = mg_hi[:, bass.ds(i, 1), 0:n].rearrange("p a n -> p (a n)")
                dve.tensor_copy(ms, tmp[:, 3, 0:n]).then_inc(S("mg_hi_done"), 1)
                dve.wait_ge(S("mg_hi_done"), MG0 + 1 + i)
                dve.tensor_tensor(mg_lo[:, bass.ds(i, 1), 0:n].rearrange("p a n -> p (a n)"), tmp[:, 3, 0:n],
                                  ms.bitcast(F32), ALU.subtract).then_inc(S("mg_ready"), 1)
            turns(dve, DC, body)
            dve.wait_ge(S("mod_kept"), mods_done(l, 1))
            columns_gate(k)
            columns_norm(k + 1)
            link(dve.memset(ssq[:], 0.0))
            for m in range(DC):
                update(finished(phases[l, "wo"], m % 2, m // 2), m % 2, m, k, late_tokens(l))
                add_squares(DC * (k + 1) + m, m % 2, norm_tokens(k + 1))
                first_split(k + 1, m, m % 2)
            norm(k + 1, (phases[l, 2, "in", 0], 1, 0))
            ffn(l, 2)
            norm(k + 2, (phases[l + 1, 1, "in", 0], 1, 0) if l + 1 < DEPTH else None)
        for d in range(DC):
            ins = dve.scalar_tensor_tensor(out=x[:, d, 0:SEQ], in0=x[:, d, 0:SEQ], scalar=vec[:, 0, V_FIN + d:V_FIN + d + 1],
                                           in1=rstd[:, 0:SEQ], op0=ALU.mult, op1=ALU.mult)
            ins.then_inc(S("y_ready_t"), 1)

    @block.tensor
    def _(pe):
        def chunk_of(k):
            return lambda kk: pe.wait_ge(S("u_ready"), DC * k + kk + 1)

        def products(ph, j, c, i, per, dst, hi_, lo_, k0, n, start, stop, k_wait=None):
            slot, g, _ = ph.at(j, c, i, per)
            pe.wait_ge(S("w_lo_ready"), g + 1)
            nk = ph.kd[j]
            for kk in range(nk):
                if k_wait:
                    k_wait(k0 + kk)
                last = three(dst, slot, kk, hi_, lo_, k0 + kk, n, start and kk == 0, stop and kk == nk - 1)
            last.then_inc(S("w_used"), 1)

        def three(dst, slot, kk, hi_, lo_, ka, n, start, stop):
            pe.matmul(dst, w_hi[:, slot, kk, :], hi_[:, ka, 0:n], start=start, stop=False)
            pe.matmul(dst, w_hi[:, slot, kk, :], lo_[:, ka, 0:n], start=False, stop=False)
            return pe.matmul(dst, w_lo[:, slot, kk, :], hi_[:, ka, 0:n], start=False, stop=stop)

        def pair(ph, units, dsts, n, k):
            slots = []
            for (j, c) in units:
                slot, g, _ = ph.at(j, c)
                pe.wait_ge(S("w_lo_ready"), g + 1)
                slots.append(slot)
            if k:
                pe.wait_ge(S("shift_ready"), k)
                for u, s in enumerate(slots):
                    for kk in range(DC):
                        pe.matmul(bank[:, 7, 4 * u:4 * u + 4], w_hi[:, s, kk, :], shift_split[:, kk, :], start=kk == 0, stop=False)
                        last = pe.matmul(bank[:, 7, 4 * u:4 * u + 4], w_lo[:, s, kk, :], shift_split[:, kk, :],
                                         start=False, stop=kk == DC - 1)
                last.then_inc(S("shift_summed"), 1)
                mean_square(k)
            for kk in range(DC):
                if k:
                    pe.wait_ge(S("first_u_ready"), DC * (k - 1) + kk + 1)
                else:
                    pe.wait_ge(S("u_ready"), kk + 1)
                for s, d, nn in zip(slots, dsts, n):
                    last = three(d, s, kk, u_hi, u_lo, kk, nn, kk == 0, kk == DC - 1)
                    if kk == DC - 1:
                        last.then_inc(S("w_used"), 1)
                if k and kk < DC - 1:
                    last.then_inc(S("first_used"), 1)

        def mean_square(k):
            n = norm_tokens(k)
            pe.wait_ge(S("ssq_added"), DC * (k + 1))
            pe.matmul(bank[:, 6, 0:n], ones_mean[:], ssq[:, 0:n], start=True, stop=True).then_inc(S("ms_ready"), 1)

        def mod_reduce(G):
            pe.wait_ge(S("acc_ready"), G + 1)
            wait(pe, S("mod_kept"), G)
            for v in range(2):
                pe.matmul(bank[:, 6 + v, :], ones_r[:], acc_hi[:, v, :], start=True, stop=False)
                last = pe.matmul(bank[:, 6 + v, :], ones_r[:], acc_lo[:, v, :], start=False, stop=True)
            last.then_inc(S("red_ready"), 1)

        def ffn(l, f):
            k = norm_of(l, f)
            n = norm_tokens(k)
            for half in (0, 1):
                ph = phases[l, f, "in", half]
                s0 = ffn_step(l, f, half)
                mods = bodies_of_mods(l, f, "in", half)

                def hidden(s, c, i):
                    b = (s0 + c) % 2
                    wait(pe, S("h_ready"), s0 + s - 1)
                    if isinstance(s, int) and s == 0 and half == 0:
                        pair(ph, [(0, 0), (1, 0)], [bank[:, 2 * b, 0:n], bank[:, 2 * b + 1, 0:n]], [n, n], k)
                        return
                    second = isinstance(s, int) and s == 1 and half == 0
                    for j in range(2):
                        products(ph, j, c, i, 2, bank[:, 2 * b + j, 0:n], u_hi, u_lo, 0, n, True, True,
                                 chunk_of(k) if second and j == 0 else None)

                def body(i):
                    for c in range(2):
                        hidden(c + i * 2, c, i)
                    if mods and not (half == 0 and k and isinstance(i, int)):
                        mod_reduce(mods[0] + i - (1 if half == 0 and k else 0))
                turns(pe, FH // 2, body, peel=half == 0)
                hidden(FH - 1, FH - 1, 0)
                ph = phases[l, f, "out", half]
                m0 = out_step(l, f, half)
                mods = bodies_of_mods(l, f, "out", half)

                def body(i):
                    for c in range(2):
                        pe.wait_ge(S("x_done"), m0 - 1 + c + i * 2)
                        for j in range(2):
                            def hidden_wait(kc):
                                if kc >= FH - 2:
                                    pe.wait_ge(S("h_ready"), s0 + kc + 1)
                            products(ph, j, c, i, 2, bank[:, 4 + c, 0:n], h_hi, h_lo, j * FFN_OUT[0], n, j == 0, j == 1,
                                     hidden_wait if c == 0 else None)
                    if mods:
                        mod_reduce(mods[0] + i)
                turns(pe, DC // 2 - 1, body)
                body(DC // 2 - 1)

        pe.wait_ge(ident_loaded, 16)
        pe.wait_ge(vec_loaded, 16)
        for l in range(DEPTH):
            last = pe.transpose(bank[:, 6, V_ROWS * l:V_ROWS * (l + 1)], vec_rows[:, l, :], ident[0:V_ROWS, 0:V_ROWS])
        last.then_inc(S("vec_t"), 1)
        for s in range(2):
            pe.wait_ge(rows_loaded[s], 16)

        def turn_x(d):
            wait(pe, S("x_done"), d - 2)
            for a in range(2 * TT):
                last = pe.transpose(bank[:, 4 + d % 3, P * a:P * a + P], tok_rows[:, a, P * d:P * d + P], ident[:])
            last.then_inc(S("x_turned"), 1)

        def mod_group(g, k0=0, k1=DC):
            pe.wait_ge(first_loaded[g], 16)
            for kk in range(k0, k1):
                last = pe.matmul(bank[0:2, g, :], sil[:, :, kk], mod_first[:, g, kk, :], start=kk == 0, stop=kk == DC - 1)
            if k1 == DC:
                last.then_inc(S("rows_mm"), 1)

        def turn_mod(g0, g1):
            pe.wait_ge(S("mod_rows_ready"), g1)
            for g in range(g0, g1):
                for a in range(MGC):
                    o = 2 * (MGC * g + a)
                    last = pe.transpose(bank[:, 7, o:o + 2], mod_rows[:, g, P * a:P * a + P], ident[0:2, 0:2])
            last.then_inc(S("modt_ready"), 1)

        pe.wait_ge(S("vec_ready"), 1)
        pe.wait_ge(S("ones_set"), 3)
        pe.wait_ge(S("ones_r_set"), 1)
        for d in range(5):
            turn_x(d)
        pe.wait_ge(S("sil_ready"), 1)
        mod_group(0)
        for d in range(5, DC):
            turn_x(d)
        mod_group(1)
        mean_square(0)
        mod_group(2)
        mod_group(3, 0, 2)
        turn_mod(0, 3)
        mod_group(3, 2, DC)
        turn_mod(3, 4)
        for l in range(DEPTH):
            ffn(l, 1)
            k = norm_of(l, 0)
            pe.wait_ge(S("mod_kept"), mods_done(l, 1))
            ph = phases[l, "head"]
            nh = len(HEAD)

            pe.wait_ge(const_loaded, 16 * 4)

            def statistics(c):
                n = head_tokens(l, HEAD[c][0])
                pe.wait_ge(S("qk_sq"), 5 * l + c + 1)
                wait(pe, S("qk_root"), 5 * l + c)
                pe.matmul(bank[:, 4, 0:n], head_mean[:], sq[:, c % 2, 0:n], start=True, stop=True).then_inc(S("qk_ms"), 1)

            def swap(c):
                pe.wait_ge(S("qk_normed"), 5 * l + c + 1)
                wait(pe, S("qk_ready"), 5 * l + c)
                pe.matmul(bank[:, 5, 0:SEQ], rope_swap[:], qk[:, c, 0:SEQ], start=True, stop=True).then_inc(S("qk_swapped"), 1)

            for idx in range(nh):
                n = head_tokens(l, HEAD[idx][0])
                if idx == 0:
                    n1 = head_tokens(l, HEAD[1][0])
                    pair(ph, [(0, 0), (1, 0)], [bank[:, 0, 0:n], bank[:, 1, 0:n1]], [n, n1], k)
                    continue
                if idx > 1:
                    if idx >= 4:
                        if idx - 4 < 5:
                            pe.wait_ge(S("qk_raw"), 5 * l + idx - 3)
                        else:
                            pe.wait_ge(S("head_copied"), 9 * l + idx - 8)
                    products(ph, idx, 0, 0, 0, bank[:, idx % 4, 0:n], u_hi, u_lo, 0, n, True, True,
                             chunk_of(k) if idx == 2 else None)
                if 2 <= idx <= 6:
                    statistics(idx - 2)
                if 3 <= idx <= 7:
                    swap(idx - 3)
            for c in range(3):
                if c < 2:
                    pe.wait_ge(S("qk_ready"), 5 * l + 5)
                    pe.wait_ge(S("head_copied"), 9 * l + (1, 6, 7)[c])
                else:
                    pe.wait_ge(S("head_copied"), 9 * l + 7)
                    pe.wait_ge(S("vn_ready"), 3 * l + 1)
                for a in range(4):
                    last = pe.transpose(bank[:, 4 + c % 2, P * a:P * a + P], vT[:, c, P * a:P * a + P], ident[:])
                last.then_inc(S("vt_ready"), 1)
            pe.wait_ge(S("bias_loaded"), 16 * ROWS * NA_HEADS * (l + 1))
            for j in range(4):
                if j >= 2:
                    pe.wait_ge(S("bias_ready"), 4 * l + j - 1)
                pe.matmul(bank[:, 6 + j % 2, :], flip[:], bias[:, j // 2, 2 * (j % 2):2 * (j % 2) + 2, :],
                          start=True, stop=True).then_inc(S("flipped"), 1)
            pe.wait_ge(S("bias_ready"), 4 * l + 4)
            pe.wait_ge(S("dft_loaded"), 32 * (l + 1))
            pe.wait_ge(S("head_copied"), 9 * l + 9)
            tiles = TT if l == DEPTH - 1 else 2 * TT
            for c in range(2):
                for b in range(tiles // 2):
                    if c == 1:
                        pe.wait_ge(S("z_copied"), z0[l] + b + 1)
                    for a in range(2):
                        o = (2 * b + a) * P
                        last = pe.matmul(bank[:, 6 + b, 2 * P * a:2 * P * a + 2 * P], fT[:, c, o:o + P], dft_chan[:],
                                         start=True, stop=True)
                    last.then_inc(S("z_ready"), 1)
            pe.wait_ge(S("z_copied"), z0[l] + tiles)
            for c in range(2):
                for s in range(tiles // TT):
                    for a in range(TT):
                        for part in range(2):
                            last = pe.matmul(bank[:, 6 + c, SEQ * s:SEQ * s + SEQ], Zs[:, c, TT * s + a, P * part:P * part + P],
                                             dft_tok[:, part, a, :], start=a == 0 and part == 0, stop=a == TT - 1 and part == 1)
                last.then_inc(S("four_ready"), 1)
            js = jobs(l)
            per = 2 if l == DEPTH - 1 else 4

            def scores(q):
                kind, c, up, s = js[q]
                J = job0[l] + q
                rows = slice(HD * up, HD * up + HD)
                keys = slice(0, TOK) if s == 0 else slice(SEQ, TOK)
                nk = TOK if s == 0 else CTX
                if kind == "g":
                    qs, ks = qk[rows, 1 + c, :], qk[rows, 0, keys]
                else:
                    qs, ks = nqk[rows, 2 + c, :], nqk[rows, c, keys]
                wait(pe, S("exp_done"), J - 1)
                for b in range(TT):
                    o = SEQ * s + P * b
                    last = pe.matmul(bank[:, 2 * (J % 2) + b, 0:nk], qs[:, o:o + P], ks, start=True, stop=True)
                last.then_inc(S("s_ready"), 1)

            def transposes(q):
                kind, c, up, s = js[q]
                J = job0[l] + q
                pe.wait_ge(S("p_ready"), J + 1)
                wait(pe, S("pt_act"), J)
                wait(pe, S("pt_dve"), J)
                for kt in range(4 if s == 0 else 2):
                    for b in range(TT):
                        dst = bank[:, 4 + kt // 2, SEQ * (kt % 2) + P * b:SEQ * (kt % 2) + P * b + P] if s == 0 \
                            else bank[:, 4 + kt, P * b:P * b + P]
                        last = pe.transpose(dst, probs[:, J % 2, b, P * kt:P * kt + P], ident[:])
                last.then_inc(S("pt_ready"), 1)

            def values(q):
                kind, c, up, s = js[q]
                J = job0[l] + q
                chunk = q // per
                if q % per == 0 and chunk >= 2:
                    pe.wait_ge(S("cat_ready"), DC * l + 2 + chunk - 1)
                pe.wait_ge(S("pt_act"), J + 1)
                pe.wait_ge(S("pt_dve"), J + 1)
                v0 = HD * up if kind == "g" else P + P * c + HD * up
                dst = bank[HD * up:HD * up + HD, 6 + chunk % 2, SEQ * s:SEQ * s + SEQ]
                tiles_ = 4 if s == 0 else 2
                for kt in range(tiles_):
                    key_tile = kt if s == 0 else 2 + kt
                    last = pe.matmul(dst, Vn[:, key_tile, v0:v0 + HD], pT[:, J % 2, kt, :], start=kt == 0, stop=kt == tiles_ - 1)
                last.then_inc(S("o_ready"), 1)

            pe.wait_ge(S("head_copied"), 9 * l + 9)
            pe.wait_ge(S("vn_ready"), 3 * l + 3)
            pe.wait_ge(S("cat_ready"), DC * l + 2)
            N = len(js)
            for q in range(N + 3):
                if q < N:
                    scores(q)
                if 2 <= q <= N + 1:
                    transposes(q - 2)
                if q >= 3:
                    values(q - 3)
            ph = phases[l, "gate"]
            n = late_tokens(l)
            pe.wait_ge(S("exp_done"), job0[l] + N)
            pe.wait_ge(S("pt_dve"), job0[l] + N)
            pe.wait_ge(S("pt_act"), job0[l] + N)
            MG0 = DC * l

            def body(i):
                for j in range(3):
                    wait(pe, S("sig_ready"), 3 * MG0 + j - 2 + i * 3)
                    products(ph, j, 0, i, 1, bank[:, j, 0:n], u_hi, u_lo, 0, n, True, True)
                wait(pe, S("prod_done"), MG0 + i)
                if isinstance(i, int):
                    pe.wait_ge(S("cat_ready"), DC * (l + 1))
                slot, g, _ = ph.at(3, 0, i, 1)
                pe.wait_ge(S("w_lo_ready"), g + 1)
                for b, (k0, k1) in enumerate(((0, 2), (2, 6), (6, 8))):
                    for kk in range(k0, k1):
                        last = three(bank[:, 3 + b, 0:n], slot, kk, cat_hi, cat_lo, kk, n, kk == k0, kk == k1 - 1)
                last.then_inc(S("w_used"), 1)
            turns(pe, DC, body, peel=True)
            ph = phases[l, "wo"]
            m0 = out_step(l, 0)
            pe.wait_ge(S("prod_done"), MG0 + DC)

            def body(i):
                for c in range(2):
                    for j in range(2):
                        pe.wait_ge(S("x_done"), m0 - 1 + 2 * c + j + i * 4)

                        def merged(kc):
                            if c == 0 and j == 0:
                                pe.wait_ge(S("mg_ready"), MG0 + kc + 1)
                        products(ph, j, c, i, 2, bank[:, 4 + j, 0:n], mg_hi, mg_lo, 0, n, True, True, merged)
            turns(pe, 2, body)
            ffn(l, 2)
            pe.wait_ge(S("mod_kept"), mods_done(l, 2))
        mean_square(3 * DEPTH)
        for a in range(TT):
            for d in range(DC):
                pe.wait_ge(S("y_ready_t"), d + 1)
                q = 2 * a + d // 4
                last = pe.transpose(bank[:, q, P * (d % 4):P * (d % 4) + P], x[:, d, P * a:P * a + P], ident[:])
                if d % 4 == 3:
                    last.then_inc(S("yt_ready"), 1)
    ctx.close()


IN_NAMES = ["x", "c", "ctx", "c_ctx", "mod_w", "mod_b", "norm_ffn1", "ffn1_w_in", "ffn1_w_out", "norm_mix", "w_in", "q_norm",
            "k_norm", "na_rpb", "w_fourier", "w_gqa_out", "w_na_out", "w_o", "norm_ffn2", "ffn2_w_in", "ffn2_w_out", "final_norm"]


def constants():
    f32 = np.float32
    c = {"c_ident": np.eye(P, dtype=f32)}
    c["c_head_mean"] = np.kron(np.eye(2), np.full((HD, HD), 1.0 / HD)).astype(f32)
    swap = np.zeros((P, P), f32)
    for i in range(0, P, 2):
        swap[i + 1, i] = -1.0
        swap[i, i + 1] = 1.0
    c["c_rope_swap"] = swap
    c["c_flip"] = np.kron(np.eye(2), np.eye(GRID_W)[::-1]).astype(f32)
    tok = np.arange(SEQ)
    freqs = f32(10000.0) ** (-np.arange(HD // 4, dtype=f32) / f32(HD // 4))
    ang = np.concatenate([(tok // GRID_W).astype(f32)[:, None] * freqs, (tok % GRID_W).astype(f32)[:, None] * freqs], axis=1)
    pair = (np.arange(P) % HD) // 2
    c["c_rope"] = np.stack([np.cos(ang.astype(np.float64)).T[pair], np.sin(ang.astype(np.float64)).T[pair]], axis=1).astype(f32)
    ch = np.arange(FG)
    a = 2 * np.pi * (np.outer(ch, ch) % FG) / FG
    c["c_dft_chan"] = np.concatenate([np.kron(np.eye(2), np.cos(a)), np.kron(np.eye(2), np.sin(a))], axis=1).astype(f32)
    b = 2 * np.pi * (np.outer(tok, tok) % SEQ) / SEQ
    norm = 1.0 / np.sqrt(SEQ * FG)
    both = np.stack([np.cos(b) * norm, -np.sin(b) * norm])
    c["c_dft_tok"] = np.ascontiguousarray(both.reshape(2, TT, P, SEQ).transpose(2, 0, 1, 3)).astype(f32)
    col = np.arange(GRID_W)
    cs = np.clip(col - WIN_W // 2, 0, GRID_W - WIN_W)
    inside = (col[None, :] >= cs[:, None]) & (col[None, :] < cs[:, None] + WIN_W)
    c["c_band"] = np.where(np.tile(inside, (2, 1)), 0.0, -1e30).astype(f32)
    return c


def kernel(**inputs):
    import concourse.bacc as _bacc
    from concourse.bass_utils import run_bass_kernel_spmd as _run

    nc = _bacc.Bacc("TRN2", target_bir_lowering=False, num_devices=1)
    a = {n: np.ascontiguousarray(inputs[n]) for n in IN_NAMES}
    feed = {n: a[n] for n in ("mod_w", "ffn1_w_in", "ffn1_w_out", "w_in", "na_rpb", "w_fourier", "w_gqa_out", "w_na_out", "w_o",
                              "ffn2_w_in", "ffn2_w_out")}
    feed["x"], feed["ctx"] = a["x"][0], a["ctx"][0]
    packs = []
    for l in range(DEPTH):
        rows = [a["mod_b"][l], a["norm_ffn1"][l], a["norm_mix"][l], a["norm_ffn2"][l], a["final_norm"], a["c"][0], a["c_ctx"],
                a["q_norm"][l], a["q_norm"][l], a["k_norm"][l], a["k_norm"][l]]
        packs.append(np.concatenate([r.reshape(-1) for r in rows]).reshape(V_ROWS, P))
    feed["vec_rows"] = np.ascontiguousarray(np.stack(packs, axis=1))
    feed.update(constants())
    arrays, t = {}, {}
    for name, v in feed.items():
        arrays[f"in_{name}"] = v
        t[name] = nc.dram_tensor(f"in_{name}", v.shape, mybir.dt.from_np(v.dtype), kind="ExternalInput").ap()
    out = nc.dram_tensor("out_y", (SEQ, D), F32, kind="ExternalOutput").ap()
    build(nc, t, out)
    r = _run(nc, [arrays], core_ids=[0])
    return r.results[0]["out_y"].reshape(1, SEQ, D)
```

```python
from contextlib import ExitStack

import numpy as np
import concourse.bass as bass
from concourse import mybir

F32 = mybir.dt.float32
F32R = mybir.dt.float32r
ALU = mybir.AluOpType
ACT = mybir.ActivationFunctionType
AX_X = mybir.AxisListType.X

P = 128
D = 1024
DC = D // P
SEQ = 256
CTX = 256
TOK = SEQ + CTX
TT = SEQ // P
DEPTH = 2
GRID_W = 64
ROWS = SEQ // GRID_W
HD = 64
KV_HEADS = 2
GQA_CHUNKS = 4
NA_HEADS = 4
WIN_H, WIN_W = 8, 16
D_FF = 2816
FH = D_FF // P // 2
FW = 256
FG = 64
N_MOD = 9
MODC = N_MOD * DC
EPS = 1e-6
COL_F, COL_Q, COL_K, COL_V = 0, 256, 768, 896
COL_NQ, COL_NK, COL_NV, COL_GATE = 1024, 1280, 1536, 1792
MG = 512
MK = 4
MGC = MG // P
N_START = 4
RING = 4
V_MODB, V_N1, V_NM, V_N2, V_FIN, V_C, V_CC, V_QN, V_KN, V_ROWS = 0, 72, 80, 88, 96, 104, 112, 120, 121, 122


class Phase:

    def __init__(self, plan, steps, kd, w=None):
        self.nu, self.steps, self.kd = len(kd), steps, kd
        self.w = w or [1] * len(kd)
        self.g0 = plan["g"]
        self.base = list(plan["loaded"])
        for q in range(steps * self.nu):
            plan["loaded"][(self.g0 + q) % RING] += 16 * self.w[q % self.nu]
        plan["g"] += steps * self.nu

    def at(self, j, c, i=0, per=0):
        q = self.nu * c + j
        slot = (self.g0 + q) % RING
        if self.steps == 1:
            same = [self.w[jj] for jj in range(j + 1) if (j - jj) % RING == 0]
            return slot, self.g0 + q, self.base[slot] + 16 * sum(same)
        turns = self.nu * per // RING
        return slot, self.g0 + q + self.nu * per * i, self.base[slot] + 16 * self.w[j] * (q // RING + 1 + turns * i)


def build(nc, t, out):
    ctx = ExitStack()
    sem = {}

    def S(name):
        if name not in sem:
            sem[name] = ctx.enter_context(nc.semaphore(name))
        return sem[name]

    def place(st, name, shape, dt=F32):
        return st.enter_context(nc.sbuf_tensor(name, shape, dt))

    def sb(name, shape, dt=F32):
        return place(ctx, name, shape, dt)

    plan = {"g": 0, "loaded": [0] * RING}
    FFN_IN, FFN_OUT = [8, 8], [6, 5]
    phases = {}
    for l in range(DEPTH):
        for f in (1, 2):
            if f == 2:
                phases[l, "head"] = Phase(plan, 1, [8] * 14, [1, 2, 2, 2, 2] + [1] * 9)
                phases[l, "gate"] = Phase(plan, DC, [8, 8, 8, 8], [1, 1, 1, 4])
                phases[l, "wo"] = Phase(plan, DC // 2, [8, 8])
            for half in (0, 1):
                phases[l, f, "in", half] = Phase(plan, FH, FFN_IN)
                phases[l, f, "out", half] = Phase(plan, DC, FFN_OUT)
    order = list(phases)
    HEAD = ([("k", COL_K)] + [("q", c) for c in range(GQA_CHUNKS)] + [("v", COL_V)]
            + [("nk", COL_NK + P * c) for c in range(2)] + [("nq", COL_NQ + P * c) for c in range(2)]
            + [("nv", COL_NV + P * c) for c in range(2)] + [("f", COL_F + P * c) for c in range(2)])

    def head_tokens(l, kind):
        return SEQ if l == DEPTH - 1 and kind in ("q", "nq", "f") else TOK

    def late_tokens(l):
        return SEQ if l == DEPTH - 1 else TOK

    def norm_tokens(k):
        return TOK if k < 5 else SEQ

    BG = {(0, 1): (0, N_START), (0, 2): (1, 0), (1, 1): (1, 9)}
    BG_PARTS = {(0, 1): {("in", 0): 5, ("out", 0): 4, ("in", 1): 5}, (0, 2): {("in", 0): 4, ("in", 1): 5},
                (1, 1): {("in", 0): 4, ("in", 1): 5}}
    BG_COUNT = {k: sum(v.values()) for k, v in BG_PARTS.items()}
    BG_BASE = {k: 1 + sum(BG_COUNT[o] for o in BG if o < k) for k in BG}

    def jobs(l):
        streams = (0,) if l == DEPTH - 1 else (0, 1)
        return ([("g", c, up, s) for c in range(GQA_CHUNKS) for s in streams for up in (0, 1)]
                + [("n", c, up, s) for c in range(2) for s in streams for up in (0, 1)])

    job0, z0 = [0], [0]
    for l in range(DEPTH):
        job0.append(job0[-1] + len(jobs(l)))
        z0.append(z0[-1] + (TT if l == DEPTH - 1 else 2 * TT))

    x = sb("x", [P, DC, TOK])
    u_hi = sb("u_hi", [P, DC, TOK], F32R)
    u_lo = sb("u_lo", [P, DC, TOK], F32R)
    w_raw = sb("w_raw", [P, RING, 8, P])
    w_hi = sb("w_hi", [P, RING, 8, P], F32R)
    w_lo = sb("w_lo", [P, RING, 8, P], F32R)
    ident = sb("ident", [P, P])
    ones_mean = sb("ones_mean", [P, P])
    ones_f = sb("ones_f", [P, P])
    ones_r = sb("ones_r", [P, P], F32R)
    head_mean = sb("head_mean", [P, P])
    rope_swap = sb("rope_swap", [P, P])
    flip = sb("flip", [P, P])
    band = sb("band", [P, GRID_W])
    vec_rows = sb("vec_rows", [V_ROWS, DEPTH, P])
    vec = sb("vec", [P, DEPTH, V_ROWS])
    sil = sb("sil", [P, 2, DC])
    modcol = sb("modcol", [P, DEPTH, 2, MODC])
    colA = sb("colA", [P, 6, 2, DC])
    colB = sb("colB", [P, 6, 2, DC])
    colG = sb("colG", [P, 6, 2, DC])
    eps_col = sb("eps_col", [P, 1])
    shift_split = sb("shift_split", [P, DC, 4], F32R)
    shift_sum = sb("shift_sum", [P, 2, 2])
    gq = sb("gq", [P, DEPTH])
    sq = sb("sq", [P, 2, TOK])
    ssq = sb("ssq", [P, TOK])
    root = sb("root", [P, TOK])
    rstd = sb("rstd", [P, TOK])
    tmp = sb("tmp", [P, 4, TOK])
    smax = sb("smax", [P, 2, 2])
    rsum = sb("rsum", [P, 2, 2])
    rrec = sb("rrec", [P, 2, 2])
    with ExitStack() as st:
        h_hi = place(st, "h_hi", [P, FH, TOK], F32R)
        h_lo = place(st, "h_lo", [P, FH, TOK], F32R)
        sg = place(st, "sg", [P, 2, TOK])
        hf = place(st, "hf", [P, 2, TOK])
        mod_w = place(st, "mod_w", [P, 2, MK, MG])
        acc = place(st, "acc", [P, 2, MG])
        acc_hi = place(st, "acc_hi", [P, 2, MG], F32R)
        acc_lo = place(st, "acc_lo", [P, 2, MG], F32R)
        mtmp = place(st, "mtmp", [P, 2 * MGC, P])
    with ExitStack() as st:
        tok_rows = place(st, "tok_rows", [P, 2 * TT, D])
        mod_first = place(st, "mod_first", [P, N_START, DC, MG])
    with ExitStack() as st:
        mod_rows = place(st, "mod_rows", [2, N_START, MG])
        start_hi = place(st, "start_hi", [P, 2, MG], F32R)
        start_lo = place(st, "start_lo", [P, 2, MG], F32R)
        y_rows = place(st, "y_rows", [P, TT, D])
    with ExitStack() as st:
        cat_hi = place(st, "cat_hi", [P, DC, TOK], F32R)
        cat_lo = place(st, "cat_lo", [P, DC, TOK], F32R)
        with ExitStack() as st2:
            qk = place(st2, "qk", [P, 1 + GQA_CHUNKS, TOK])
            nqk = place(st2, "nqk", [P, 4, TOK])
            Vn = place(st2, "Vn", [P, 4, 3 * P])
            bias = place(st2, "bias", [P, TT, NA_HEADS, SEQ])
            with ExitStack() as st3:
                probs = place(st3, "probs", [P, 2, 2, TOK])
                pT = place(st3, "pT", [P, 2, 4, SEQ])
            with ExitStack() as st3:
                fT = place(st3, "fT", [P, 2, TOK])
                Zs = place(st3, "Zs", [P, 2, 4, 2 * P])
                dft_chan = place(st3, "dft_chan", [P, 2 * P])
                dft_tok = place(st3, "dft_tok", [P, 2, TT, SEQ])
        with ExitStack() as st2:
            mg_hi = place(st2, "mg_hi", [P, DC, TOK], F32R)
            mg_lo = place(st2, "mg_lo", [P, DC, TOK], F32R)
            sig = place(st2, "sig", [P, 3, TOK])
    rope_cs = tmp[:, 3, :].rearrange("p (a t) -> p a t", a=2)
    vT = tmp[:, 0:3, :]

    def y_cols(d):
        return tmp[:].rearrange("p a (b n) -> p (a b) n", n=SEQ)[:, d, :].rearrange("p a n -> p (a n)")

    def head_sq(c, n):
        return (sq[:, 0, 0:n], sq[:, 1, 0:n], tmp[:, 2, 0:n])[c % 3]

    sums_bg = (acc, acc_hi, acc_lo, mtmp)
    sums_start = (tmp[:, 0:2, :], start_hi, start_lo, tmp[:, 2:4, :].rearrange("p v (a b) -> p (v a) b", a=MGC))

    bank = ctx.enter_context(nc.psum_tensor("bank", [P, 8, 512], F32))

    w_loaded = [S(f"w_loaded{i}") for i in range(RING)]
    mod_loaded = [S(f"mod_loaded{i}") for i in range(2)]
    first_loaded = [S(f"first_loaded{i}") for i in range(N_START)]
    rows_loaded = [S(f"rows_loaded{i}") for i in range(2)]
    vec_loaded = S("vec_loaded")
    ident_loaded = S("ident_loaded")
    const_loaded = S("const_loaded")

    def wait(eng, s, value):
        if not (isinstance(value, int) and value <= 0):
            eng.wait_ge(s, value)

    def turns(eng, n, body, peel=False):
        lo = 0
        if peel:
            body(0)
            lo = 1
        if n - lo > 1:
            with eng.Fori(lo, n) as i:
                body(i)
        elif n - lo == 1:
            body(lo)

    def finished(ph, j, c, i=0, per=0):
        return ph.at(j, c, i, per)[1] + 1

    def ffn_step(l, f, half):
        return ((2 * l + f - 1) * 2 + half) * FH

    def out_step(l, f, half=0):
        return DC + l * 5 * DC + {1: half * DC, 0: 2 * DC, 2: (3 + half) * DC}[f]

    def x_count(k):
        l, w = divmod(k - 1, 3)
        return out_step(l, (1, 0, 2)[w], 0 if w == 1 else 1)

    def norm_of(l, f):
        return 3 * l + {1: 0, 0: 1, 2: 2}[f]

    def bodies_of_mods(l, f, part, half):
        parts = BG_PARTS.get((l, f), {})
        if (part, half) not in parts:
            return None
        names = list(parts)
        return BG_BASE[l, f] + sum(parts[o] for o in names[:names.index((part, half))]), parts[part, half]

    def mods_done(l, f):
        return 1 + sum(BG_COUNT[k] for k in BG if k <= (l, f))

    block = ctx.enter_context(nc.Block())

    @block.sync
    def _(sp):
        sp.dma_start(ident[:], t["c_ident"]).then_inc(ident_loaded, 16)
        sp.dma_start(vec_rows[:], t["vec_rows"]).then_inc(vec_loaded, 16)
        for s in range(2):
            rows = (t["x"], t["ctx"])[s]
            sp.dma_start(tok_rows[:, TT * s:TT * s + TT, :], rows.rearrange("(a p) d -> p a d", p=P)).then_inc(rows_loaded[s], 16)
        for g in (1, 0, *range(2, N_START)):
            sp.dma_start(mod_first[:, g], t["mod_w"][0].rearrange("(k p) c -> p k c", p=P)[:, :, MG * g:MG * g + MG]).then_inc(first_loaded[g], 16)

        def load(ph, srcs, j, c, i=0, per=0):
            slot, g, _ = ph.at(j, c, i, per)
            wait(sp, S("w_lo_ready"), g - RING + 1)
            for p0, p1, k0, k1, src in srcs:
                sp.dma_start(w_raw[p0:p1, slot, k0:k1, :], src).then_inc(w_loaded[slot], 16)

        for key in order:
            ph = phases[key]
            l = key[0]
            if len(key) == 4:
                _, f, part, half = key
                w = t[f"ffn{f}_w_in"][l] if part == "in" else t[f"ffn{f}_w_out"][l]
                w = w.rearrange("(k p) c -> p k c", p=P)
                if part == "in":
                    def body(i, steps=2):
                        for c in range(steps):
                            for j in range(2):
                                col = j * D_FF + (half * FH + c) * P + i * (2 * P)
                                load(ph, [(0, P, 0, DC, w[:, :, bass.ds(col, P)])], j, c, i, 2)
                    turns(sp, FH // 2, body, peel=ph.g0 == 0)
                    body(FH // 2, 1)
                else:
                    def body(i):
                        for c in range(2):
                            for j in range(2):
                                k0, n = half * FH + j * FFN_OUT[0], FFN_OUT[j]
                                load(ph, [(0, P, 0, n, w[:, k0:k0 + n, bass.ds(c * P + i * (2 * P), P)])], j, c, i, 2)
                    turns(sp, DC // 2, body)
            elif key[1] == "head":
                w = t["w_in"][l].rearrange("(k p) c -> p k c", p=P)
                for idx, (kind, col) in enumerate(HEAD):
                    if kind == "q":
                        srcs = [(0, P, 0, DC, w[:, :, COL_Q + HD * h:COL_Q + HD * h + HD]) for h in (col, col + GQA_CHUNKS)]
                        slot, g, _ = ph.at(idx, 0)
                        wait(sp, S("w_lo_ready"), g - RING + 1)
                        for up in (0, 1):
                            sp.dma_start(w_raw[:, slot, :, HD * up:HD * up + HD], srcs[up][4]).then_inc(w_loaded[slot], 16)
                    else:
                        load(ph, [(0, P, 0, DC, w[:, :, col:col + P])], idx, 0)
            elif key[1] == "gate":
                w = t["w_in"][l].rearrange("(k p) c -> p k c", p=P)
                wf = t["w_fourier"][l].rearrange("(k p) c -> p k c", p=P)
                wg = t["w_gqa_out"][l].rearrange("(u c p) n -> u p c n", u=2, p=HD)
                wn = t["w_na_out"][l].rearrange("(k p) c -> p k c", p=P)

                def body(i):
                    for j in range(3):
                        load(ph, [(0, P, 0, DC, w[:, :, bass.ds(COL_GATE + j * D + i * P, P)])], j, 0, i, 1)
                    cols = bass.ds(i * P, P)
                    load(ph, [(HD, P, 2, 6, wg[1][:, :, cols]), (0, HD, 2, 6, wg[0][:, :, cols]),
                              (0, P, 0, 2, wf[:, :, cols]), (0, P, 6, 8, wn[:, :, cols])], 3, 0, i, 1)
                turns(sp, DC, body)
            else:
                w = t["w_o"][l].rearrange("(k p) c -> p k c", p=P)

                def body(i):
                    for c in range(2):
                        for j in range(2):
                            load(ph, [(0, P, 0, DC, w[:, :, bass.ds((2 * c + j) * P + i * (4 * P), P)])], j, c, i, 2)
                turns(sp, 2, body)
        for a in range(TT):
            sp.wait_ge(S("y_rows_act"), a + 1)
            sp.wait_ge(S("y_rows_dve"), a + 1)
            sp.dma_start(out[a * P:a * P + P, :], y_rows[:, a, :]).then_inc(S("stored"), 16)
        sp.wait_ge(S("stored"), 16 * TT)

    @block.gpsimd
    def _(pool):
        for dst, name in ((head_mean, "c_head_mean"), (rope_swap, "c_rope_swap"), (flip, "c_flip"), (band, "c_band")):
            pool.dma_start(dst[:], t[name]).then_inc(const_loaded, 16)
        pool.memset(ones_mean[:], 1.0 / D).then_inc(S("ones_set"), 1)
        pool.memset(ones_f[:], 1.0).then_inc(S("ones_set"), 1)
        pool.memset(eps_col[:], EPS).then_inc(S("ones_set"), 1)

        def lo(ph, j, c, i=0, per=0):
            slot, g, _ = ph.at(j, c, i, per)
            n = ph.kd[j]
            pool.wait_ge(S("w_hi_ready"), g + 1)
            pool.tensor_tensor(w_lo[:, slot, 0:n, :], w_raw[:, slot, 0:n, :], w_hi[:, slot, 0:n, :].bitcast(F32),
                               ALU.subtract).then_inc(S("w_lo_ready"), 1)

        for key in order:
            ph = phases[key]
            l = key[0]
            if len(key) == 4:
                def body(i, steps=2):
                    for c in range(steps):
                        for j in range(2):
                            lo(ph, j, c, i, 2)
                if key[2] == "in":
                    turns(pool, FH // 2, body)
                    body(FH // 2, 1)
                else:
                    turns(pool, DC // 2, body)
            elif key[1] == "head":
                for idx in range(len(HEAD)):
                    lo(ph, idx, 0)
            elif key[1] == "gate":
                turns(pool, DC, lambda i: [lo(ph, j, 0, i, 1) for j in range(4)])
            else:
                turns(pool, 2, lambda i: [lo(ph, j, c, i, 2) for c in range(2) for j in range(2)])

    @block.scalar
    def _(act):
        def hi(ph, j, c, i=0, per=0):
            slot, g, loaded = ph.at(j, c, i, per)
            n = ph.kd[j]
            act.wait_ge(w_loaded[slot], loaded)
            wait(act, S("w_used"), g - RING + 1)
            act.activation(w_hi[:, slot, 0:n, :], w_raw[:, slot, 0:n, :], ACT.Copy).then_inc(S("w_hi_ready"), 1)

        def first_hi(key):
            ph = phases[key]
            for q in range(2):
                hi(ph, q % ph.nu, q // ph.nu)

        def following(key):
            at = order.index(key) + 1
            return order[at] if at < len(order) else None

        def square_at(M, Q, par, m, n):
            act.wait_ge(S("x_done"), M + 1)
            wait(act, S("ssq_added"), Q - 1)
            act.activation(sq[:, par, 0:n], x[:, bass.ds(m, 1), 0:n].rearrange("p a n -> p (a n)"), ACT.Square).then_inc(S("sq_ready"), 1)

        def first_scaled(k, m, i=0):
            act.wait_ge(S("x_done"), x_count(k) + m + 1 + i * 2)
            for v in range(norm_tokens(k) // SEQ):
                cols = slice(SEQ * v, SEQ * v + SEQ)
                last = act.activation(u_hi[:, bass.ds(m + i * 2, 1), cols].rearrange("p a n -> p (a n)"),
                                      x[:, bass.ds(m + i * 2, 1), cols].rearrange("p a n -> p (a n)"),
                                      ACT.Copy, scale=colA[:, k, v, bass.ds(m + i * 2, 1)])
            last.then_inc(S("first_hi_done"), 1)

        def root_of(k):
            n = norm_tokens(k)
            act.wait_ge(S("ms_ready"), k + 1)
            act.activation(root[:, 0:n], bank[:, 4, 0:n], ACT.Sqrt, bias=eps_col[:, 0:1]).then_inc(S("root_ready"), 1)

        def norm(k, key=None):
            n = norm_tokens(k)
            if k:
                ph = phases[key]
                for q in (2, 3):
                    hi(ph, q % ph.nu, q // ph.nu)
                root_of(k)
            for d in range(DC):
                if k == 0 and d == DC // 2:
                    copy_mod_rows(N_START - 1)
                    load_mod(BG_BASE[0, 1], *mod_plan(0, 1, BG_BASE[0, 1]))
                if k and d in (DC - 3, DC - 1):
                    q = 4 + (d == DC - 1)
                    hi(ph, q % ph.nu, q // ph.nu)
                q = DC * k + d
                if k and d < DC - 1:
                    act.wait_ge(S("first_used"), (DC - 1) * (k - 1) + d + 1)
                elif k:
                    act.wait_ge(S("w_used"), finished(phases[key], 1, 0))
                act.wait_ge(S("t_ready"), q + 1)
                for v in range(n // SEQ):
                    cols = slice(SEQ * v, SEQ * v + SEQ)
                    last = act.activation(u_hi[:, d, cols], tmp[:, d % 3, cols], ACT.Identity, bias=colB[:, k, v, d:d + 1])
                last.then_inc(S("u_hi_done"), 1)

        def load_mod(G, l, group):
            wait(act, S("mod_mac"), 2 * DC * G)
            w = t["mod_w"][l].rearrange("(k p) c -> p k c", p=P)
            for kh in range(2):
                act.dma_start(mod_w[:, kh], w[:, MK * kh:MK * kh + MK, bass.ds(group * MG, MG)]).then_inc(mod_loaded[kh], 16)

        def mod_plan(l, f, G):
            layer, first = BG[l, f]
            return layer, first + G - BG_BASE[l, f]

        def ffn(l, f):
            k = norm_of(l, f)
            n = norm_tokens(k)
            nxt = norm_of(l, f) + 1
            if (l, f) in BG and k:
                G = BG_BASE[l, f]
                act.wait_ge(S("u_ready"), DC * k + 1)
                load_mod(G, *mod_plan(l, f, G))
            for half in (0, 1):
                key = (l, f, "in", half)
                ph = phases[key]
                mods = bodies_of_mods(l, f, "in", half)
                s0 = ffn_step(l, f, half)

                def silu(s, c, i=0):
                    act.wait_ge(S("w_used"), finished(phases[l, f, "in", half], 1, c, i, 2))
                    b = (s0 + c) % 2
                    wait(act, S("h_prod"), s0 + s - 1)
                    act.activation(sg[:, b, 0:n], bank[:, 2 * b + 1, 0:n], ACT.Silu).then_inc(S("silu_ready"), 1)

                def first_silu():
                    act.wait_ge(S("gate_scaled"), 2 * l + f - 1)
                    for v in range(n // SEQ):
                        cols = slice(SEQ * v, SEQ * v + SEQ)
                        last = act.activation(sg[:, s0 % 2, cols], sg[:, s0 % 2, cols], ACT.Silu, bias=shift_sum[:, 1, v:v + 1])
                    last.then_inc(S("silu_ready"), 1)

                def body(i, more=True):
                    start = half == 0 and isinstance(i, int) and i == 0
                    for c in range(2):
                        if start and c == 0:
                            if not k:
                                for j in range(2):
                                    hi(ph, j, 2)
                        elif not start:
                            for j in range(2):
                                hi(ph, j, c + 1, i, 2)
                        if c == 1 and mods and more and not (start and k):
                            G = mods[0] + i + 1 - (1 if half == 0 and k else 0)
                            load_mod(G, *mod_plan(l, f, G))
                        if start and c == 0 and k:
                            first_silu()
                        else:
                            silu(c + i * 2, c, i)
                if mods and mods[0] + mods[1] == BG_BASE[l, f] + BG_COUNT[l, f]:
                    turns(act, FH // 2 - 1, body, peel=half == 0)
                    body(FH // 2 - 1, more=False)
                else:
                    turns(act, FH // 2, body, peel=half == 0)
                first_hi(following(key))
                silu(FH - 1, FH - 1)
                key = (l, f, "out", half)
                ph = phases[key]
                mods = bodies_of_mods(l, f, "out", half)
                m0 = out_step(l, f, half)

                def body(i, tail=False):
                    for c in range(2):
                        if not (tail and c == 1):
                            for j in range(2):
                                hi(ph, j, c + 1, i, 2)
                        if tail and c == 0 and following(key):
                            first_hi(following(key))
                        if c == 1 and mods:
                            G = mods[0] + i + 1
                            load_mod(G, *mod_plan(l, f, G))
                        if half == 1:
                            square_at(m0 + c + i * 2, DC * nxt + c + i * 2, c, c + i * 2, norm_tokens(nxt))
                            if nxt < 6:
                                first_scaled(nxt, c, i)
                turns(act, DC // 2 - 1, body)
                body(DC // 2 - 1, tail=True)

        act.wait_ge(S("vec_ready"), 1)
        act.activation(sil[:].rearrange("p v k -> p (v k)"), vec[:, 0, V_C:V_C + 2 * DC], ACT.Silu).then_inc(S("sil_ready"), 1)
        for d in range(DC):
            square_at(d, d, d % 2, d, TOK)
        def copy_mod_rows(g):
            act.wait_ge(S("rows_mm"), g)
            act.activation(mod_rows[:, g, :], bank[0:2, g, :], ACT.Copy).then_inc(S("mod_rows_ready"), 1)
        copy_mod_rows(1)
        root_of(0)
        first_hi(order[0])
        copy_mod_rows(2)
        for j in range(2):
            hi(phases[order[0]], j, 1)
        norm(0)
        for l in range(DEPTH):
            ffn(l, 1)
            norm(norm_of(l, 0), (l, "head"))
            nh = len(HEAD)
            key = (l, "head")
            ph = phases[key]
            act.wait_ge(S("u_ready"), DC * (norm_of(l, 0) + 1))
            act.dma_start(rope_cs, t["c_rope"]).then_inc(S("rope_loaded"), 16)

            def load_bias(r, h):
                width = 2 * WIN_W - 1
                first = ((l * NA_HEADS + h) * (2 * WIN_H - 1) + WIN_H - 1 - r) * width + WIN_W - GRID_W
                src = bass.AP(tensor=t["na_rpb"].tensor, offset=first, ap=[[1, GRID_W], [width, ROWS], [1, GRID_W]])
                p0 = (r % 2) * GRID_W
                dst = bias[p0:p0 + GRID_W, r // 2, h, :].rearrange("p (i k) -> p i k", k=GRID_W)
                act.dma_start(dst, src).then_inc(S("bias_loaded"), 16)

            for idx, (kind, arg) in enumerate(HEAD):
                if 6 <= idx + 2 < nh:
                    hi(ph, idx + 2, 0)
                elif idx + 2 == nh:
                    first_hi((l, "gate"))
                if idx == 5:
                    act.dma_start(dft_chan[:], t["c_dft_chan"]).then_inc(S("dft_loaded"), 16)
                    act.dma_start(dft_tok[:], t["c_dft_tok"]).then_inc(S("dft_loaded"), 16)
                if 6 <= idx:
                    for b in range(2 * (idx - 6), 2 * (idx - 5)):
                        load_bias(b // NA_HEADS, b % NA_HEADS)
                n = head_tokens(l, kind)
                if 3 <= idx < 8:
                    c = idx - 3
                    nc_ = head_tokens(l, HEAD[c][0])
                    act.wait_ge(S("qk_ms"), 5 * l + c + 1)
                    wait(act, S("qk_normed"), 5 * l + c)
                    act.activation(root[:, 0:nc_], bank[:, 4, 0:nc_], ACT.Sqrt, bias=eps_col[:, 0:1]).then_inc(S("qk_root"), 1)
                if idx < 5:
                    act.wait_ge(S("qk_raw"), 5 * l + idx + 1)
                    act.activation(head_sq(idx, n), qk[:, idx, 0:n], ACT.Square).then_inc(S("qk_sq"), 1)
                if idx >= 5:
                    act.wait_ge(S("w_used"), finished(ph, idx, 0))
                    tile, first = {"v": (vT, 5), "nk": (nqk, 6), "nq": (nqk, 6), "nv": (vT, 9), "f": (fT, 12)}[kind]
                    dst = tile[:, idx - first, 0:n]
                    act.activation(dst, bank[:, idx % 4, 0:n], ACT.Copy,
                                   scale=HD ** -0.5 if kind == "nq" else 1.0).then_inc(S("head_copied"), 1)
            for c in range(3):
                act.wait_ge(S("vt_ready"), 3 * l + c + 1)
                act.activation(Vn[:, :, P * c:P * c + P], bank[:, 4 + c % 2, :].rearrange("p (k d) -> p k d", k=4), ACT.Copy)\
                   .then_inc(S("vn_ready"), 1)
            for j in (2, 3):
                hi(phases[l, "gate"], j, 0)
            js = jobs(l)

            def copy_pt(q):
                J = job0[l] + q
                kind, c, up, s = js[q]
                act.wait_ge(S("pt_ready"), J + 1)
                src = bank[:, 5, :].rearrange("p (k t) -> p k t", k=2)
                dst = pT[:, J % 2, 2:4, :] if s == 0 else pT[:, J % 2, 1:2, :]
                act.activation(dst, src if s == 0 else src[:, 0:1, :], ACT.Copy).then_inc(S("pt_act"), 1)

            for q, (kind, c, up, s) in enumerate(js):
                J = job0[l] + q
                keys = TOK if s == 0 else CTX
                act.wait_ge(S("max_ready"), J + 1)
                wait(act, S("pt_ready"), J - 1)
                for b in range(TT):
                    last = act.activation(probs[:, J % 2, b, 0:keys], bank[:, 2 * (J % 2) + b, 0:keys], ACT.Exp,
                                          bias=smax[:, J % 2, b:b + 1], accum_out=rsum[:, J % 2, b:b + 1])
                last.then_inc(S("exp_done"), 1)
                if q:
                    copy_pt(q - 1)
            copy_pt(len(js) - 1)
            key = (l, "gate")
            ph = phases[key]
            n = late_tokens(l)

            def gate(i, j):
                act.wait_ge(S("w_used"), finished(ph, j, 0, i, 1))
                wait(act, S("prod_done"), DC * l + i)
                act.activation(sig[:, j, 0:n], bank[:, j, 0:n], ACT.Sigmoid).then_inc(S("sig_ready"), 1)

            def body(i, last=False):
                start = isinstance(i, int) and i == 0
                if not start:
                    hi(ph, 2, 0, i, 1)
                gate(i, 0)
                if not start:
                    hi(ph, 3, 0, i, 1)
                gate(i, 1)
                if not last:
                    hi(ph, 0, 1, i, 1)
                    gate(i, 2)
                    hi(ph, 1, 1, i, 1)
                else:
                    first_hi((l, "wo"))
                    gate(i, 2)
            turns(act, DC - 1, body, peel=True)
            body(DC - 1, last=True)
            key = (l, "wo")
            ph = phases[key]
            k = norm_of(l, 2)
            for m in range(DC):
                if m + 2 < DC:
                    hi(ph, m % 2, (m + 2) // 2)
                elif m + 2 == DC:
                    first_hi(following(key))
                square_at(out_step(l, 0) + m, DC * k + m, m % 2, m, norm_tokens(k))
                first_scaled(k, m)
            norm(k, following(key))
            ffn(l, 2)
            if l + 1 < DEPTH:
                norm(k + 1, (l + 1, 1, "in", 0))
        act.wait_ge(S("row_ms"), 1)
        act.activation(root[:, 0:TT], bank[:, 4, 0:TT], ACT.Sqrt, bias=eps_col[:, 0:1]).then_inc(S("root_ready"), 1)
        act.wait_ge(S("row_rstd"), 1)
        for a in range(TT):
            act.wait_ge(S("yt_first"), a + 1)
            act.activation(y_rows[:, a, 0:512], bank[:, 2 * a, :], ACT.Copy, scale=rstd[:, a:a + 1]).then_inc(S("y_rows_act"), 1)

    @block.vector
    def _(dve):
        chain = [0]

        def link(ins):
            chain[0] += 1
            ins.then_inc(S("dve_chain"), 1)
            dve.wait_ge(S("dve_chain"), chain[0])

        def columns_norm(k, d0=0, d1=DC):
            l, w = k // 3, k % 3
            gain = vec[:, l, V_N1 + DC * w + d0:V_N1 + DC * w + d1]
            for v in range(2):
                b0, b1 = 3 * DC * w + d0, 3 * DC * w + d1
                a0, a1 = b0 + DC, b1 + DC
                link(dve.tensor_tensor(colB[:, k, v, d0:d1], modcol[:, l, v, b0:b1], vec[:, l, b0:b1], ALU.add))
                link(dve.tensor_tensor(colA[:, k, v, d0:d1], modcol[:, l, v, a0:a1], vec[:, l, a0:a1], ALU.add))
                link(dve.scalar_tensor_tensor(out=colA[:, k, v, d0:d1], in0=colA[:, k, v, d0:d1], scalar=1.0, in1=gain,
                                              op0=ALU.add, op1=ALU.mult))
            if k:
                shift = colB[:, k].rearrange("p v d -> p d v")
                link(dve.tensor_copy(shift_split[:, :, 0:2], shift))
                dve.tensor_tensor(shift_split[:, :, 2:4], shift, shift_split[:, :, 0:2].bitcast(F32), ALU.subtract)\
                   .then_inc(S("shift_ready"), 1)

        def columns_gate(k):
            l, w = k // 3, k % 3
            for v in range(2):
                o = 3 * DC * w + 2 * DC
                link(dve.tensor_tensor(colG[:, k, v, :], modcol[:, l, v, o:o + DC], vec[:, l, o:o + DC], ALU.add))
                if w != 1:
                    link(dve.tensor_scalar(colG[:, k, v, :], colG[:, k, v, :], 0.5, None, ALU.mult))

        def add_squares(Q, par, n):
            dve.wait_ge(S("sq_ready"), Q + 1)
            wait(dve, S("ssq_added"), Q)
            dve.tensor_tensor(ssq[:, 0:n], ssq[:, 0:n], sq[:, par, 0:n], ALU.add).then_inc(S("ssq_added"), 1)

        def first_split(k, m, i=0):
            dve.wait_ge(S("first_hi_done"), DC * (k - 1) + m + 1 + i * 2)
            for v in range(norm_tokens(k) // SEQ):
                xs, hs, ls = (a[:, bass.ds(m + i * 2, 1), SEQ * v:SEQ * v + SEQ].rearrange("p a n -> p (a n)") for a in (x, u_hi, u_lo))
                last = dve.scalar_tensor_tensor(out=ls, in0=xs, scalar=colA[:, k, v, bass.ds(m + i * 2, 1)], in1=hs.bitcast(F32),
                                                op0=ALU.mult, op1=ALU.subtract)
            last.then_inc(S("first_u_ready"), 1)

        def rstd_of(k):
            n = norm_tokens(k)
            dve.wait_ge(S("root_ready"), k + 1)
            link(dve.reciprocal(rstd[:, 0:n], root[:, 0:n]))

        def norm(k):
            n = norm_tokens(k)
            if k:
                rstd_of(k)

            def scale(d):
                if d >= 3:
                    dve.wait_ge(S("u_ready"), DC * k + d - 2)
                for v in range(n // SEQ):
                    cols = slice(SEQ * v, SEQ * v + SEQ)
                    last = dve.scalar_tensor_tensor(out=tmp[:, d % 3, cols], in0=x[:, d, cols], scalar=colA[:, k, v, d:d + 1],
                                                    in1=rstd[:, cols], op0=ALU.mult, op1=ALU.mult)
                last.then_inc(S("t_ready"), 1)

            scale(0)
            for d in range(DC):
                q = DC * k + d
                if k == 0 and d == DC // 2 - 1:
                    start_columns(N_START - 1, N_START)
                    columns_norm(0, DC // 2, DC)
                if d + 1 < DC:
                    scale(d + 1)
                dve.wait_ge(S("u_hi_done"), q + 1)
                for v in range(n // SEQ):
                    cols = slice(SEQ * v, SEQ * v + SEQ)
                    last = dve.scalar_tensor_tensor(out=u_lo[:, d, cols], in0=tmp[:, d % 3, cols], scalar=colB[:, k, v, d:d + 1],
                                                    in1=u_hi[:, d, cols].bitcast(F32), op0=ALU.add, op1=ALU.subtract)
                last.then_inc(S("u_ready"), 1)
            if k:
                dve.wait_ge(S("shift_summed"), k)
                sums = bank[:, 6:8, 0:4].rearrange("p u (a v) -> p u a v", a=2)
                link(dve.tensor_copy(shift_sum[:], sums[:, :, 0, :]))
                link(dve.tensor_tensor(shift_sum[:], shift_sum[:], sums[:, :, 1, :], ALU.add))

        def mod_products(G, first=False):
            acc = (sums_start if first else sums_bg)[0]
            for k in range(DC):
                if first:
                    dve.wait_ge(first_loaded[0], 16)
                    w = mod_first[:, 0, k, :]
                else:
                    if k % MK == 0:
                        dve.wait_ge(mod_loaded[k // MK], G * 16)
                    w = mod_w[:, k // MK, k % MK, :]
                for v in range(2):
                    if k == 0:
                        ins = dve.tensor_scalar(acc[:, v, :], w, sil[:, v, k:k + 1], None, ALU.mult)
                    else:
                        dve.wait_ge(S("mod_mac"), G * (2 * DC) + 2 * k + v - 1)
                        ins = dve.scalar_tensor_tensor(out=acc[:, v, :], in0=w, scalar=sil[:, v, k:k + 1], in1=acc[:, v, :],
                                                       op0=ALU.mult, op1=ALU.add)
                    ins.then_inc(S("mod_mac"), 1)

        def mod_split(G, first=False):
            acc, acc_hi, acc_lo, _ = sums_start if first else sums_bg
            dve.wait_ge(S("mod_mac"), G * (2 * DC) + 2 * DC)
            dve.tensor_copy(acc_hi[:], acc[:]).then_inc(S("acc_hi_done"), 1)
            dve.wait_ge(S("acc_hi_done"), G + 1)
            dve.tensor_tensor(acc_lo[:], acc[:], acc_hi[:].bitcast(F32), ALU.subtract).then_inc(S("acc_ready"), 1)

        def mod_extract(G, layer, group, first=False):
            mtmp = (sums_start if first else sums_bg)[3]
            dve.wait_ge(S("red_ready"), G + 1)
            dve.tensor_tensor(mtmp[:], bank[:, 6:8, :].rearrange("p v (a b) -> p (v a) b", a=MGC),
                              ident[:].unsqueeze(1).to_broadcast([P, 2 * MGC, P]), ALU.mult).then_inc(S("mod_masked"), 1)
            dve.wait_ge(S("mod_masked"), G + 1)
            dve.tensor_reduce(modcol[:, layer, :, bass.ds(group * MGC, MGC)], mtmp[:].rearrange("p (v a) b -> p v a b", v=2),
                              AX_X, ALU.add).then_inc(S("mod_kept"), 1)

        def mod_plan(l, f, G):
            layer, first = BG[l, f]
            return layer, first + G - BG_BASE[l, f]

        def update(done, b, m, k, n):
            dve.wait_ge(S("w_used"), done)
            for v in range(n // SEQ):
                cols = slice(SEQ * v, SEQ * v + SEQ)
                xs = x[:, bass.ds(m, 1), cols].rearrange("p a n -> p (a n)")
                last = dve.scalar_tensor_tensor(out=xs, in0=bank[:, b, cols], scalar=colG[:, k, v, bass.ds(m, 1)],
                                                in1=xs, op0=ALU.mult, op1=ALU.add)
            last.then_inc(S("x_done"), 1)

        def ffn(l, f):
            k = norm_of(l, f)
            n = norm_tokens(k)
            nxt = k + 1
            for half in (0, 1):
                s0 = ffn_step(l, f, half)
                mods = bodies_of_mods(l, f, "in", half)

                def hidden(s, c):
                    b = (s0 + c) % 2
                    dve.wait_ge(S("silu_ready"), s0 + s + 1)
                    dve.tensor_tensor(hf[:, b, 0:n], bank[:, 2 * b, 0:n], sg[:, b, 0:n], ALU.mult).then_inc(S("h_prod"), 1)
                    split_hidden(s, b)

                def split_hidden(s, b):
                    dve.wait_ge(S("h_prod"), s0 + s + 1)
                    hs = h_hi[:, bass.ds(s, 1), 0:n].rearrange("p a n -> p (a n)")
                    dve.tensor_copy(hs, hf[:, b, 0:n]).then_inc(S("h_hi_done"), 1)
                    dve.wait_ge(S("h_hi_done"), s0 + s + 1)
                    dve.tensor_tensor(h_lo[:, bass.ds(s, 1), 0:n].rearrange("p a n -> p (a n)"), hf[:, b, 0:n],
                                      hs.bitcast(F32), ALU.subtract).then_inc(S("h_ready"), 1)

                def first_hidden():
                    b = s0 % 2
                    dve.wait_ge(S("w_used"), finished(phases[l, f, "in", 0], 1, 0))
                    dve.tensor_tensor(sg[:, b, 0:n], bank[:, 2 * b + 1, 0:n], rstd[:, 0:n], ALU.mult).then_inc(S("gate_scaled"), 1)
                    link(dve.tensor_tensor(hf[:, b, 0:n], bank[:, 2 * b, 0:n], rstd[:, 0:n], ALU.mult))
                    dve.wait_ge(S("silu_ready"), s0 + 1)
                    for v in range(n // SEQ):
                        cols = slice(SEQ * v, SEQ * v + SEQ)
                        last = dve.scalar_tensor_tensor(out=hf[:, b, cols], in0=hf[:, b, cols], scalar=shift_sum[:, 0, v:v + 1],
                                                        in1=sg[:, b, cols], op0=ALU.add, op1=ALU.mult)
                    last.then_inc(S("h_prod"), 1)
                    split_hidden(0, b)

                def body(i):
                    start = half == 0 and isinstance(i, int) and i == 0
                    with_mods = mods and not (start and k)
                    G = mods[0] + i - (1 if half == 0 and k else 0) if with_mods else None
                    if with_mods:
                        mod_products(G)
                    if start and k:
                        first_hidden()
                    else:
                        hidden(0 + i * 2, 0)
                    if with_mods:
                        mod_split(G)
                    hidden(1 + i * 2, 1)
                    if with_mods:
                        mod_extract(G, *mod_plan(l, f, G))
                turns(dve, FH // 2, body, peel=half == 0)
                hidden(FH - 1, FH - 1)
                if half == 0:
                    dve.wait_ge(S("mod_kept"), BG_BASE[l, f] + BG_PARTS[l, f].get(("in", 0), 0) if (l, f) in BG else mods_done(l, f))
                    columns_gate(k)
                else:
                    if k < 5:
                        dve.wait_ge(S("mod_kept"), mods_done(l, f))
                        columns_norm(nxt)
                    link(dve.memset(ssq[:], 0.0))
                m0 = out_step(l, f, half)
                mods = bodies_of_mods(l, f, "out", half)

                def body(i):
                    G = mods[0] + i if mods else None
                    if mods:
                        mod_products(G)
                        mod_split(G)
                    for c in range(2):
                        update(finished(phases[l, f, "out", half], 1, c, i, 2), 4 + c, c + i * 2, k, n)
                        if half == 1:
                            add_squares(DC * nxt + c + i * 2, c, norm_tokens(nxt))
                            if nxt < 6:
                                first_split(nxt, c, i)
                            else:
                                m = c + i * 2
                                dve.wait_ge(S("x_done"), m0 + m + 1)
                                dve.tensor_scalar(y_cols(bass.ds(m, 1)), x[:, bass.ds(m, 1), 0:SEQ].rearrange("p a n -> p (a n)"),
                                                  vec[:, 0, bass.ds(V_FIN + m, 1)], None, ALU.mult).then_inc(S("y_ready_t"), 1)
                    if mods:
                        mod_extract(G, *mod_plan(l, f, G))
                turns(dve, DC // 2 - 1, body)
                body(DC // 2 - 1)

        dve.wait_ge(S("ones_set"), 3)
        dve.tensor_copy(ones_r[:], ones_f[:]).then_inc(S("ones_r_set"), 1)
        link(dve.memset(ssq[:], 0.0))
        dve.wait_ge(S("vec_t"), 1)
        dve.tensor_copy(vec[:], bank[:, 6, 0:DEPTH * V_ROWS].rearrange("p (l r) -> p l r", l=DEPTH)).then_inc(S("vec_ready"), 1)
        dve.wait_ge(S("vec_ready"), 1)
        link(dve.tensor_scalar(gq[:], vec[:, :, V_QN], HD ** -0.5, None, ALU.mult))
        for d in range(DC):
            dve.wait_ge(S("x_turned"), d + 1)
            dve.tensor_copy(x[:, d, :], bank[:, 4 + d % 3, :]).then_inc(S("x_done"), 1)
            if d:
                add_squares(d - 1, (d - 1) % 2, TOK)
        add_squares(DC - 1, (DC - 1) % 2, TOK)

        def start_columns(g0, g1):
            dve.wait_ge(S("modt_ready"), 1 if g1 < N_START else 2)
            link(dve.tensor_copy(modcol[:, 0, :, MGC * g0:MGC * g1],
                                 bank[:, 5, 2 * MGC * g0:2 * MGC * g1].rearrange("p (a v) -> p v a", v=2)))
        mod_products(0, first=True)
        mod_split(0, first=True)
        rstd_of(0)
        mod_extract(0, 0, 0, first=True)
        start_columns(1, N_START - 1)
        dve.wait_ge(S("mod_kept"), 1)
        columns_norm(0, 0, DC // 2)
        norm(0)
        for l in range(DEPTH):
            ffn(l, 1)
            k = norm_of(l, 0)
            norm(k)
            nh = len(HEAD)
            for idx in range(10):
                if idx < 5:
                    n = head_tokens(l, HEAD[idx][0])
                    dve.wait_ge(S("w_used"), finished(phases[l, "head"], idx, 0))
                if idx < 2:
                    link(dve.tensor_tensor(qk[:, idx, 0:n], bank[:, idx, 0:n], rstd[:, 0:n], ALU.mult))
                    for v in range(n // SEQ):
                        cols = slice(SEQ * v, SEQ * v + SEQ)
                        last = dve.tensor_scalar(qk[:, idx, cols], qk[:, idx, cols], shift_sum[:, idx, v:v + 1], None, ALU.add)
                    last.then_inc(S("qk_raw"), 1)
                elif idx < 5:
                    dve.tensor_copy(qk[:, idx, 0:n], bank[:, idx % 4, 0:n]).then_inc(S("qk_raw"), 1)
                if 3 <= idx < 8:
                    c = idx - 3
                    n = head_tokens(l, HEAD[c][0])
                    gain = vec[:, l, V_KN:V_KN + 1] if c == 0 else gq[:, l:l + 1]
                    dve.wait_ge(S("qk_root"), 5 * l + c + 1)
                    link(dve.reciprocal(rstd[:, 0:n], root[:, 0:n]))
                    dve.scalar_tensor_tensor(out=qk[:, c, 0:n], in0=qk[:, c, 0:n], scalar=gain, in1=rstd[:, 0:n],
                                             op0=ALU.mult, op1=ALU.mult).then_inc(S("qk_normed"), 1)
                if idx >= 5:
                    c = idx - 5
                    dve.wait_ge(S("rope_loaded"), 16 * (l + 1))
                    dve.wait_ge(S("qk_swapped"), 5 * l + c + 1)
                    link(dve.tensor_tensor(ssq[:, 0:SEQ], bank[:, 5, 0:SEQ], rope_cs[:, 1, :], ALU.mult))
                    link(dve.tensor_tensor(ssq[:, SEQ:TOK], qk[:, c, 0:SEQ], rope_cs[:, 0, :], ALU.mult))
                    dve.tensor_tensor(qk[:, c, 0:SEQ], ssq[:, SEQ:TOK], ssq[:, 0:SEQ], ALU.add).then_inc(S("qk_ready"), 1)
            for j in range(4):
                dve.wait_ge(S("flipped"), 4 * l + j + 1)
                dve.tensor_tensor(bias[:, j // 2, 2 * (j % 2):2 * (j % 2) + 2, :].rearrange("p h (i k) -> p (h i) k", k=GRID_W),
                                  bank[:, 6 + j % 2, :].rearrange("p (i k) -> p i k", k=GRID_W),
                                  band[:].unsqueeze(1).to_broadcast([P, 2 * ROWS, GRID_W]), ALU.add).then_inc(S("bias_ready"), 1)
            tiles = TT if l == DEPTH - 1 else 2 * TT
            for c in range(2):
                for b in range(tiles // 2):
                    dve.wait_ge(S("z_ready"), z0[l] + c * (tiles // 2) + b + 1)
                    dve.tensor_copy(Zs[:, c, 2 * b:2 * b + 2, :], bank[:, 6 + b, :].rearrange("p (a z) -> p a z", a=2))\
                       .then_inc(S("z_copied"), 1)
            n = late_tokens(l)

            def to_cat(src, c):
                link(dve.tensor_copy(cat_hi[:, c, 0:n], src))
                dve.tensor_tensor(cat_lo[:, c, 0:n], src, cat_hi[:, c, 0:n].bitcast(F32), ALU.subtract).then_inc(S("cat_ready"), 1)

            js = jobs(l)
            per = 2 if l == DEPTH - 1 else 4

            def maximum(q):
                kind, c, up, s = js[q]
                J = job0[l] + q
                keys = TOK if s == 0 else CTX
                dve.wait_ge(S("s_ready"), J + 1)
                sc = bank[:, 2 * (J % 2):2 * (J % 2) + 2, 0:keys]
                if kind == "n" and s == 0:
                    link(dve.tensor_tensor(sc[:, :, 0:SEQ], sc[:, :, 0:SEQ], bias[:, :, 2 * c + up, :], ALU.add))
                link(dve.tensor_reduce(smax[:, J % 2, :], sc, AX_X, ALU.max))
                dve.tensor_scalar(smax[:, J % 2, :], smax[:, J % 2, :], -1.0, None, ALU.mult).then_inc(S("max_ready"), 1)

            maximum(0)
            for c in range(2):
                dve.wait_ge(S("four_ready"), 2 * l + c + 1)
                to_cat(bank[:, 6 + c, 0:n], c)

            def normalise(q):
                kind, c, up, s = js[q]
                J = job0[l] + q
                keys = TOK if s == 0 else CTX
                dve.wait_ge(S("exp_done"), J + 1)
                link(dve.reciprocal(rrec[:, J % 2, :], rsum[:, J % 2, :]))
                for b in range(TT):
                    last = dve.tensor_scalar(probs[:, J % 2, b, 0:keys], probs[:, J % 2, b, 0:keys], rrec[:, J % 2, b:b + 1],
                                             None, ALU.mult)
                last.then_inc(S("p_ready"), 1)

            def copy_pt(q):
                kind, c, up, s = js[q]
                J = job0[l] + q
                dve.wait_ge(S("pt_ready"), J + 1)
                src = bank[:, 4, :].rearrange("p (k t) -> p k t", k=2)
                dst = pT[:, J % 2, 0:2, :] if s == 0 else pT[:, J % 2, 0:1, :]
                dve.tensor_copy(dst, src if s == 0 else src[:, 0:1, :]).then_inc(S("pt_dve"), 1)

            def finish(q):
                if (q + 1) % per == 0:
                    chunk = q // per
                    dve.wait_ge(S("o_ready"), job0[l] + q + 1)
                    to_cat(bank[:, 6 + chunk % 2, 0:n], 2 + chunk)

            N = len(js)
            for q in range(N + 4):
                if 1 <= q < N:
                    maximum(q)
                if 1 <= q <= N:
                    normalise(q - 1)
                if 2 <= q <= N + 1:
                    copy_pt(q - 2)
                if q >= 4:
                    finish(q - 4)
            key = (l, "gate")
            MG0 = DC * l

            def body(i):
                dve.wait_ge(S("sig_ready"), 3 * MG0 + 3 + i * 3)
                dve.wait_ge(S("w_used"), finished(phases[key], 3, 0, i, 1))
                for j in range(3):
                    last = dve.tensor_tensor(tmp[:, j, 0:n], bank[:, 3 + j, 0:n], sig[:, j, 0:n], ALU.mult)
                last.then_inc(S("prod_done"), 1)
                dve.wait_ge(S("prod_done"), MG0 + 1 + i)
                dve.tensor_tensor(tmp[:, 3, 0:n], tmp[:, 0, 0:n], tmp[:, 1, 0:n], ALU.add).then_inc(S("sum_step"), 1)
                dve.wait_ge(S("sum_step"), 2 * MG0 + 1 + i * 2)
                dve.tensor_tensor(tmp[:, 3, 0:n], tmp[:, 3, 0:n], tmp[:, 2, 0:n], ALU.add).then_inc(S("sum_step"), 1)
                dve.wait_ge(S("sum_step"), 2 * MG0 + 2 + i * 2)
                ms = mg_hi[:, bass.ds(i, 1), 0:n].rearrange("p a n -> p (a n)")
                dve.tensor_copy(ms, tmp[:, 3, 0:n]).then_inc(S("mg_hi_done"), 1)
                dve.wait_ge(S("mg_hi_done"), MG0 + 1 + i)
                dve.tensor_tensor(mg_lo[:, bass.ds(i, 1), 0:n].rearrange("p a n -> p (a n)"), tmp[:, 3, 0:n],
                                  ms.bitcast(F32), ALU.subtract).then_inc(S("mg_ready"), 1)
            turns(dve, DC, body)
            dve.wait_ge(S("mod_kept"), mods_done(l, 1))
            columns_gate(k)
            columns_norm(k + 1)
            link(dve.memset(ssq[:], 0.0))
            for m in range(DC):
                update(finished(phases[l, "wo"], m % 2, m // 2), 2 + m % 2, m, k, late_tokens(l))
                add_squares(DC * (k + 1) + m, m % 2, norm_tokens(k + 1))
                first_split(k + 1, m)
            norm(k + 1)
            ffn(l, 2)
            if l + 1 < DEPTH:
                norm(k + 2)
        dve.wait_ge(S("root_ready"), 3 * DEPTH + 1)
        dve.reciprocal(rstd[:, 0:TT], root[:, 0:TT]).then_inc(S("row_rstd"), 1)
        dve.wait_ge(S("row_rstd"), 1)
        for a in range(TT):
            dve.wait_ge(S("yt_last"), a + 1)
            dve.tensor_scalar(y_rows[:, a, 512:D], bank[:, 2 * a + 1, :], rstd[:, a:a + 1], None, ALU.mult).then_inc(S("y_rows_dve"), 1)

    @block.tensor
    def _(pe):
        def products(ph, j, c, i, per, dst, hi_, lo_, k0, n, start, stop, k_wait=None):
            slot, g, _ = ph.at(j, c, i, per)
            pe.wait_ge(S("w_lo_ready"), g + 1)
            nk = ph.kd[j]
            for kk in range(nk):
                if k_wait:
                    k_wait(k0 + kk)
                last = three(dst, slot, kk, hi_, lo_, k0 + kk, n, start and kk == 0, stop and kk == nk - 1)
            last.then_inc(S("w_used"), 1)

        def three(dst, slot, kk, hi_, lo_, ka, n, start, stop):
            pe.matmul(dst, w_hi[:, slot, kk, :], hi_[:, ka, 0:n], start=start, stop=False)
            pe.matmul(dst, w_hi[:, slot, kk, :], lo_[:, ka, 0:n], start=False, stop=False)
            return pe.matmul(dst, w_lo[:, slot, kk, :], hi_[:, ka, 0:n], start=False, stop=stop)

        def pair(ph, units, dsts, n, k, first=True):
            early = first and k > 0
            slots = []
            for (j, c) in units:
                slot, g, _ = ph.at(j, c)
                pe.wait_ge(S("w_lo_ready"), g + 1)
                slots.append(slot)
            if early:
                pe.wait_ge(S("shift_ready"), k)
            for kk in range(DC):
                if early:
                    pe.wait_ge(S("first_u_ready"), DC * (k - 1) + kk + 1)
                else:
                    pe.wait_ge(S("u_ready"), DC * k + kk + 1)
                for u, (s, d, nn) in enumerate(zip(slots, dsts, n)):
                    if early:
                        shift = bank[:, 6 + u, 0:4]
                        pe.matmul(shift, w_hi[:, s, kk, :], shift_split[:, kk, :], start=kk == 0, stop=False)
                        summed = pe.matmul(shift, w_lo[:, s, kk, :], shift_split[:, kk, :], start=False, stop=kk == DC - 1)
                    last = three(d, s, kk, u_hi, u_lo, kk, nn, kk == 0, kk == DC - 1)
                    if kk == DC - 1:
                        last.then_inc(S("w_used"), 1)
                if early and kk < DC - 1:
                    last.then_inc(S("first_used"), 1)
                if early and kk == DC - 1:
                    summed.then_inc(S("shift_summed"), 1)
                if early and kk == 1:
                    mean_square(k)
                if first and k == 0 and kk == 1:
                    turn_mod(N_START - 1, N_START)

        def mean_square(k):
            n = norm_tokens(k)
            pe.wait_ge(S("ssq_added"), DC * (k + 1))
            pe.matmul(bank[:, 4, 0:n], ones_mean[:], ssq[:, 0:n], start=True, stop=True).then_inc(S("ms_ready"), 1)

        def mod_reduce(G, first=False):
            _, acc_hi, acc_lo, _ = sums_start if first else sums_bg
            pe.wait_ge(S("acc_ready"), G + 1)
            wait(pe, S("mod_kept"), G)
            for v in range(2):
                pe.matmul(bank[:, 6 + v, :], ones_r[:], acc_hi[:, v, :], start=True, stop=False)
                last = pe.matmul(bank[:, 6 + v, :], ones_r[:], acc_lo[:, v, :], start=False, stop=True)
            last.then_inc(S("red_ready"), 1)

        def ffn(l, f):
            k = norm_of(l, f)
            n = norm_tokens(k)
            for half in (0, 1):
                ph = phases[l, f, "in", half]
                s0 = ffn_step(l, f, half)
                mods = bodies_of_mods(l, f, "in", half)

                def hidden(s, c, i):
                    b = (s0 + c) % 2
                    wait(pe, S("h_prod"), s0 + s - 1)
                    if isinstance(s, int) and s < 2 and half == 0:
                        pair(ph, [(0, s), (1, s)], [bank[:, 2 * b, 0:n], bank[:, 2 * b + 1, 0:n]], [n, n], k, s == 0)
                        return
                    for j in range(2):
                        products(ph, j, c, i, 2, bank[:, 2 * b + j, 0:n], u_hi, u_lo, 0, n, True, True)

                def body(i):
                    for c in range(2):
                        hidden(c + i * 2, c, i)
                    if mods and not (half == 0 and k and isinstance(i, int)):
                        mod_reduce(mods[0] + i - (1 if half == 0 and k else 0))
                turns(pe, FH // 2, body, peel=half == 0)
                hidden(FH - 1, FH - 1, 0)
                ph = phases[l, f, "out", half]
                m0 = out_step(l, f, half)
                mods = bodies_of_mods(l, f, "out", half)

                def body(i):
                    for c in range(2):
                        pe.wait_ge(S("x_done"), m0 - 1 + c + i * 2)
                        for j in range(2):
                            def hidden_wait(kc):
                                if kc == 0:
                                    pe.wait_ge(S("h_ready"), s0 + FH - 2)
                                elif kc >= FH - 2:
                                    pe.wait_ge(S("h_ready"), s0 + kc + 1)
                            products(ph, j, c, i, 2, bank[:, 4 + c, 0:n], h_hi, h_lo, j * FFN_OUT[0], n, j == 0, j == 1,
                                     hidden_wait if c == 0 else None)
                    if mods:
                        mod_reduce(mods[0] + i)
                turns(pe, DC // 2 - 1, body)
                body(DC // 2 - 1)

        pe.wait_ge(ident_loaded, 16)
        pe.wait_ge(vec_loaded, 16)
        for l in range(DEPTH):
            last = pe.transpose(bank[:, 6, V_ROWS * l:V_ROWS * (l + 1)], vec_rows[:, l, :], ident[0:V_ROWS, 0:V_ROWS])
        last.then_inc(S("vec_t"), 1)
        for s in range(2):
            pe.wait_ge(rows_loaded[s], 16)

        def turn_x(d):
            wait(pe, S("x_done"), d - 2)
            for a in range(2 * TT):
                last = pe.transpose(bank[:, 4 + d % 3, P * a:P * a + P], tok_rows[:, a, P * d:P * d + P], ident[:])
            last.then_inc(S("x_turned"), 1)

        def mod_group(g, k0=0, k1=DC):
            pe.wait_ge(first_loaded[g], 16)
            for kk in range(k0, k1):
                last = pe.matmul(bank[0:2, g, :], sil[:, :, kk], mod_first[:, g, kk, :], start=kk == 0, stop=kk == DC - 1)
            if k1 == DC:
                last.then_inc(S("rows_mm"), 1)

        def turn_mod(g0, g1):
            pe.wait_ge(S("mod_rows_ready"), g1 - 1)
            for g in range(g0, g1):
                for a in range(MGC):
                    o = 2 * (MGC * g + a)
                    last = pe.transpose(bank[:, 5, o:o + 2], mod_rows[:, g, P * a:P * a + P], ident[0:2, 0:2])
            last.then_inc(S("modt_ready"), 1)

        pe.wait_ge(S("vec_ready"), 1)
        pe.wait_ge(S("ones_set"), 3)
        pe.wait_ge(S("ones_r_set"), 1)
        for d in range(DC):
            turn_x(d)
        pe.wait_ge(S("sil_ready"), 1)
        mod_group(1)
        mean_square(0)
        mod_group(2)
        mod_reduce(0, first=True)
        mod_group(3, 0, 2)
        turn_mod(1, 3)
        mod_group(3, 2, DC)
        for l in range(DEPTH):
            ffn(l, 1)
            k = norm_of(l, 0)
            pe.wait_ge(S("mod_kept"), mods_done(l, 1))
            ph = phases[l, "head"]
            nh = len(HEAD)

            pe.wait_ge(const_loaded, 16 * 4)

            def statistics(c):
                n = head_tokens(l, HEAD[c][0])
                pe.wait_ge(S("qk_sq"), 5 * l + c + 1)
                wait(pe, S("qk_root"), 5 * l + c)
                pe.matmul(bank[:, 4, 0:n], head_mean[:], head_sq(c, n), start=True, stop=True).then_inc(S("qk_ms"), 1)

            def swap(c):
                pe.wait_ge(S("qk_normed"), 5 * l + c + 1)
                wait(pe, S("qk_ready"), 5 * l + c)
                pe.matmul(bank[:, 5, 0:SEQ], rope_swap[:], qk[:, c, 0:SEQ], start=True, stop=True).then_inc(S("qk_swapped"), 1)

            for idx in range(nh):
                n = head_tokens(l, HEAD[idx][0])
                if idx in (0, 2):
                    n1 = head_tokens(l, HEAD[idx + 1][0])
                    pair(ph, [(idx, 0), (idx + 1, 0)], [bank[:, idx, 0:n], bank[:, idx + 1, 0:n1]], [n, n1], k, idx == 0)
                elif idx >= 4:
                    if idx - 4 < 5:
                        pe.wait_ge(S("qk_raw"), 5 * l + idx - 3)
                    else:
                        pe.wait_ge(S("head_copied"), 9 * l + idx - 8)
                    products(ph, idx, 0, 0, 0, bank[:, idx % 4, 0:n], u_hi, u_lo, 0, n, True, True)
                if 3 <= idx <= 7:
                    statistics(idx - 3)
                if 5 <= idx <= 9:
                    swap(idx - 5)
            for c in range(3):
                if c < 2:
                    pe.wait_ge(S("qk_ready"), 5 * l + 5)
                    pe.wait_ge(S("head_copied"), 9 * l + (1, 6, 7)[c])
                else:
                    pe.wait_ge(S("head_copied"), 9 * l + 7)
                    pe.wait_ge(S("vn_ready"), 3 * l + 1)
                for a in range(4):
                    last = pe.transpose(bank[:, 4 + c % 2, P * a:P * a + P], vT[:, c, P * a:P * a + P], ident[:])
                last.then_inc(S("vt_ready"), 1)
            pe.wait_ge(S("bias_loaded"), 16 * ROWS * NA_HEADS * (l + 1))
            for j in range(4):
                if j >= 2:
                    pe.wait_ge(S("bias_ready"), 4 * l + j - 1)
                pe.matmul(bank[:, 6 + j % 2, :], flip[:], bias[:, j // 2, 2 * (j % 2):2 * (j % 2) + 2, :],
                          start=True, stop=True).then_inc(S("flipped"), 1)
            pe.wait_ge(S("bias_ready"), 4 * l + 4)
            js = jobs(l)
            per = 2 if l == DEPTH - 1 else 4

            def scores(q):
                kind, c, up, s = js[q]
                J = job0[l] + q
                rows = slice(HD * up, HD * up + HD)
                keys = slice(0, TOK) if s == 0 else slice(SEQ, TOK)
                nk = TOK if s == 0 else CTX
                if kind == "g":
                    qs, ks = qk[rows, 1 + c, :], qk[rows, 0, keys]
                else:
                    qs, ks = nqk[rows, 2 + c, :], nqk[rows, c, keys]
                wait(pe, S("exp_done"), J - 1)
                for b in range(TT):
                    o = SEQ * s + P * b
                    last = pe.matmul(bank[:, 2 * (J % 2) + b, 0:nk], qs[:, o:o + P], ks, start=True, stop=True)
                last.then_inc(S("s_ready"), 1)

            pe.wait_ge(S("dft_loaded"), 32 * (l + 1))
            pe.wait_ge(S("head_copied"), 9 * l + 9)
            tiles = TT if l == DEPTH - 1 else 2 * TT
            for c in range(2):
                for b in range(tiles // 2):
                    if c == 1:
                        pe.wait_ge(S("z_copied"), z0[l] + b + 1)
                    for a in range(2):
                        o = (2 * b + a) * P
                        last = pe.matmul(bank[:, 6 + b, 2 * P * a:2 * P * a + 2 * P], fT[:, c, o:o + P], dft_chan[:],
                                         start=True, stop=True)
                    last.then_inc(S("z_ready"), 1)
                scores(c)
            pe.wait_ge(S("z_copied"), z0[l] + tiles)
            for c in range(2):
                for s in range(tiles // TT):
                    for a in range(TT):
                        for part in range(2):
                            last = pe.matmul(bank[:, 6 + c, SEQ * s:SEQ * s + SEQ], Zs[:, c, TT * s + a, P * part:P * part + P],
                                             dft_tok[:, part, a, :], start=a == 0 and part == 0, stop=a == TT - 1 and part == 1)
                last.then_inc(S("four_ready"), 1)
            def transposes(q):
                kind, c, up, s = js[q]
                J = job0[l] + q
                pe.wait_ge(S("p_ready"), J + 1)
                wait(pe, S("pt_act"), J)
                wait(pe, S("pt_dve"), J)
                for kt in range(4 if s == 0 else 2):
                    for b in range(TT):
                        dst = bank[:, 4 + kt // 2, SEQ * (kt % 2) + P * b:SEQ * (kt % 2) + P * b + P] if s == 0 \
                            else bank[:, 4 + kt, P * b:P * b + P]
                        last = pe.transpose(dst, probs[:, J % 2, b, P * kt:P * kt + P], ident[:])
                last.then_inc(S("pt_ready"), 1)

            def values(q):
                kind, c, up, s = js[q]
                J = job0[l] + q
                chunk = q // per
                if q % per == 0 and chunk >= 2:
                    pe.wait_ge(S("cat_ready"), DC * l + 2 + chunk - 1)
                pe.wait_ge(S("pt_act"), J + 1)
                pe.wait_ge(S("pt_dve"), J + 1)
                v0 = HD * up if kind == "g" else P + P * c + HD * up
                dst = bank[HD * up:HD * up + HD, 6 + chunk % 2, SEQ * s:SEQ * s + SEQ]
                tiles_ = 4 if s == 0 else 2
                for kt in range(tiles_):
                    key_tile = kt if s == 0 else 2 + kt
                    last = pe.matmul(dst, Vn[:, key_tile, v0:v0 + HD], pT[:, J % 2, kt, :], start=kt == 0, stop=kt == tiles_ - 1)
                last.then_inc(S("o_ready"), 1)

            pe.wait_ge(S("head_copied"), 9 * l + 9)
            pe.wait_ge(S("vn_ready"), 3 * l + 3)
            pe.wait_ge(S("cat_ready"), DC * l + 2)
            N = len(js)
            for q in range(N + 3):
                if 2 <= q < N:
                    scores(q)
                if 2 <= q <= N + 1:
                    transposes(q - 2)
                if q >= 3:
                    values(q - 3)
            ph = phases[l, "gate"]
            n = late_tokens(l)
            pe.wait_ge(S("exp_done"), job0[l] + N)
            pe.wait_ge(S("pt_dve"), job0[l] + N)
            pe.wait_ge(S("pt_act"), job0[l] + N)
            MG0 = DC * l

            def body(i):
                for j in range(3):
                    wait(pe, S("sig_ready"), 3 * MG0 + j - 2 + i * 3)
                    products(ph, j, 0, i, 1, bank[:, j, 0:n], u_hi, u_lo, 0, n, True, True)
                wait(pe, S("prod_done"), MG0 + i)
                if isinstance(i, int):
                    pe.wait_ge(S("cat_ready"), DC * (l + 1))
                slot, g, _ = ph.at(3, 0, i, 1)
                pe.wait_ge(S("w_lo_ready"), g + 1)
                for b, (k0, k1) in enumerate(((0, 2), (2, 6), (6, 8))):
                    for kk in range(k0, k1):
                        last = three(bank[:, 3 + b, 0:n], slot, kk, cat_hi, cat_lo, kk, n, kk == k0, kk == k1 - 1)
                last.then_inc(S("w_used"), 1)
            turns(pe, DC, body, peel=True)
            ph = phases[l, "wo"]
            m0 = out_step(l, 0)
            pe.wait_ge(S("sig_ready"), 3 * (MG0 + DC))

            def body(i):
                for c in range(2):
                    for j in range(2):
                        if c == 0 and j == 1:
                            pe.wait_ge(S("prod_done"), MG0 + DC)
                        pe.wait_ge(S("x_done"), m0 - 1 + 2 * c + j + i * 4)

                        def merged(kc):
                            if c == 0 and j == 0:
                                pe.wait_ge(S("mg_ready"), MG0 + kc + 1)
                        products(ph, j, c, i, 2, bank[:, 2 + j, 0:n], mg_hi, mg_lo, 0, n, True, True, merged)
            turns(pe, 2, body)
            ffn(l, 2)
            if l + 1 < DEPTH:
                pe.wait_ge(S("mod_kept"), mods_done(l, 2))
        for d in range(DC):
            pe.wait_ge(S("y_ready_t"), d + 1)
            for a in range(TT):
                q = 2 * a + d // 4
                last = pe.transpose(bank[:, q, P * (d % 4):P * (d % 4) + P], y_cols(slice(d, d + 1))[:, P * a:P * a + P], ident[:])
                if d % 4 == 3 and d // 4 == 0:
                    last.then_inc(S("yt_first"), 1)
                if d == DC - 1:
                    last.then_inc(S("yt_last"), 1)
        pe.wait_ge(S("ssq_added"), DC * (3 * DEPTH + 1))
        for a in range(TT):
            last = pe.matmul(bank[:, 4, a:a + 1], ssq[:, P * a:P * a + P], ones_mean[:, 0:1], start=True, stop=True)
        last.then_inc(S("row_ms"), 1)
    ctx.close()


IN_NAMES = ["x", "c", "ctx", "c_ctx", "mod_w", "mod_b", "norm_ffn1", "ffn1_w_in", "ffn1_w_out", "norm_mix", "w_in", "q_norm",
            "k_norm", "na_rpb", "w_fourier", "w_gqa_out", "w_na_out", "w_o", "norm_ffn2", "ffn2_w_in", "ffn2_w_out", "final_norm"]


def constants():
    f32 = np.float32
    c = {"c_ident": np.eye(P, dtype=f32)}
    c["c_head_mean"] = np.kron(np.eye(2), np.full((HD, HD), 1.0 / HD)).astype(f32)
    swap = np.zeros((P, P), f32)
    for i in range(0, P, 2):
        swap[i + 1, i] = -1.0
        swap[i, i + 1] = 1.0
    c["c_rope_swap"] = swap
    c["c_flip"] = np.kron(np.eye(2), np.eye(GRID_W)[::-1]).astype(f32)
    tok = np.arange(SEQ)
    freqs = f32(10000.0) ** (-np.arange(HD // 4, dtype=f32) / f32(HD // 4))
    ang = np.concatenate([(tok // GRID_W).astype(f32)[:, None] * freqs, (tok % GRID_W).astype(f32)[:, None] * freqs], axis=1)
    pair = (np.arange(P) % HD) // 2
    c["c_rope"] = np.stack([np.cos(ang.astype(np.float64)).T[pair], np.sin(ang.astype(np.float64)).T[pair]], axis=1).astype(f32)
    ch = np.arange(FG)
    a = 2 * np.pi * (np.outer(ch, ch) % FG) / FG
    c["c_dft_chan"] = np.concatenate([np.kron(np.eye(2), np.cos(a)), np.kron(np.eye(2), np.sin(a))], axis=1).astype(f32)
    b = 2 * np.pi * (np.outer(tok, tok) % SEQ) / SEQ
    norm = 1.0 / np.sqrt(SEQ * FG)
    both = np.stack([np.cos(b) * norm, -np.sin(b) * norm])
    c["c_dft_tok"] = np.ascontiguousarray(both.reshape(2, TT, P, SEQ).transpose(2, 0, 1, 3)).astype(f32)
    col = np.arange(GRID_W)
    cs = np.clip(col - WIN_W // 2, 0, GRID_W - WIN_W)
    inside = (col[None, :] >= cs[:, None]) & (col[None, :] < cs[:, None] + WIN_W)
    c["c_band"] = np.where(np.tile(inside, (2, 1)), 0.0, -1e30).astype(f32)
    return c


def kernel(**inputs):
    import concourse.bacc as _bacc
    from concourse.bass_utils import run_bass_kernel_spmd as _run

    nc = _bacc.Bacc("TRN2", target_bir_lowering=False, num_devices=1)
    a = {n: np.ascontiguousarray(inputs[n]) for n in IN_NAMES}
    feed = {n: a[n] for n in ("mod_w", "ffn1_w_in", "ffn1_w_out", "w_in", "na_rpb", "w_fourier", "w_gqa_out", "w_na_out", "w_o",
                              "ffn2_w_in", "ffn2_w_out")}
    feed["x"], feed["ctx"] = a["x"][0], a["ctx"][0]
    packs = []
    for l in range(DEPTH):
        rows = [a["mod_b"][l], a["norm_ffn1"][l], a["norm_mix"][l], a["norm_ffn2"][l], a["final_norm"], a["c"][0], a["c_ctx"],
                a["q_norm"][l], a["q_norm"][l], a["k_norm"][l], a["k_norm"][l]]
        packs.append(np.concatenate([r.reshape(-1) for r in rows]).reshape(V_ROWS, P))
    feed["vec_rows"] = np.ascontiguousarray(np.stack(packs, axis=1))
    feed.update(constants())
    arrays, t = {}, {}
    for name, v in feed.items():
        arrays[f"in_{name}"] = v
        t[name] = nc.dram_tensor(f"in_{name}", v.shape, mybir.dt.from_np(v.dtype), kind="ExternalInput").ap()
    out = nc.dram_tensor("out_y", (SEQ, D), F32, kind="ExternalOutput").ap()
    build(nc, t, out)
    r = _run(nc, [arrays], core_ids=[0])
    return r.results[0]["out_y"].reshape(1, SEQ, D)
```
